# Optimizing a Trainium2 kernel written in Bass

```python
import math
import jax, jax.numpy as jnp
from jax import lax
import numpy as np

D_MODEL = 2048
BATCH = 1
SEQ = 256
DEPTH = 2
DEC_BATCH = 8
DEC_SEQ = 1
PAST_LEN = 2048
PAGE_SIZE = 128

HEAD_DIM = 128
ROPE_DIM = HEAD_DIM // 4
ROPE_THETA = 500000.0
NORM_EPS = 1e-6
Q_BLOCK = 128
PLE_DIM = 256
ATTN_SCALE = HEAD_DIM ** -0.5
TINY = 1e-30
A_HEADS = D_MODEL // (2 * HEAD_DIM)
A_PATTERNS = ((128, 1), (512, 4), (2048, 16))
A_GROUPS = len(A_PATTERNS)
A_WIN_MAX = max(w for w, _ in A_PATTERNS)
A_WIDTH = A_HEADS * HEAD_DIM
B_CHUNK = 128
B_WIDTH = D_MODEL - A_WIDTH
B_GROUPS = 8
B_GROUP_DIM = B_WIDTH // B_GROUPS
C_HEADS = D_MODEL // HEAD_DIM
C_KV_HEADS = 4
C_GQA = C_HEADS // C_KV_HEADS
C_WIDTH = C_HEADS * HEAD_DIM
C_KV_WIDTH = C_KV_HEADS * HEAD_DIM
CMP_LEN = 32
CMP_STRIDE = 16
SEL_BLOCK = 64
SEL_TOP = 16
C_WIN = 512
FORCE_BONUS = 1000.0
AB_SIZES = (A_GROUPS * A_WIDTH, A_WIDTH, A_WIDTH, A_WIDTH, B_WIDTH, B_WIDTH, B_WIDTH)
C_SIZES = (C_WIDTH,) + (C_KV_WIDTH,) * 6 + (3 * C_HEADS, C_WIDTH)

kernel_name = 'hybrid_dilated_gmlp_nsa_step'

def rms_norm(x, g):
    xf = x.astype(jnp.float32)
    y = xf * lax.rsqrt(jnp.mean(xf * xf, axis=-1, keepdims=True) + NORM_EPS)
    return (y * g.astype(jnp.float32)).astype(x.dtype)

def layer_norm(x, g):
    xf = x.astype(jnp.float32)
    xc = xf - jnp.mean(xf, axis=-1, keepdims=True)
    y = xc * lax.rsqrt(jnp.mean(xc * xc, axis=-1, keepdims=True) + NORM_EPS)
    return (y * g.astype(jnp.float32)).astype(x.dtype)

def split_points(sizes):
    pts, acc = [], 0
    for s in sizes[:-1]:
        acc += s
        pts.append(acc)
    return pts

def query_block(S):
    return Q_BLOCK if S % Q_BLOCK == 0 else S

def to_blocks(a, qb):
    B, S = a.shape[0], a.shape[1]
    return jnp.moveaxis(a.reshape((B, S // qb, qb) + a.shape[2:]), 1, 0)

def from_blocks(a):
    a = jnp.moveaxis(a, 0, 1)
    return a.reshape((a.shape[0], a.shape[1] * a.shape[2]) + a.shape[3:])

def rope_partial(x, pos):
    half = ROPE_DIM // 2
    inv = jnp.exp(-math.log(ROPE_THETA) * jnp.arange(half, dtype=jnp.float32) / half)
    ang = pos.astype(jnp.float32)[:, None] * inv[None, :]
    bshape = (1, pos.shape[0]) + (1,) * (x.ndim - 3) + (half,)
    cos = jnp.cos(ang).reshape(bshape)
    sin = jnp.sin(ang).reshape(bshape)
    xr = x[..., :ROPE_DIM].astype(jnp.float32)
    x1, x2 = xr[..., :half], xr[..., half:]
    rot = jnp.concatenate([x1 * cos - x2 * sin, x2 * cos + x1 * sin], axis=-1).astype(x.dtype)
    return jnp.concatenate([rot, x[..., ROPE_DIM:]], axis=-1)

def dilated_attention(q, k_all, v_all, q_off):
    S = q.shape[1]
    qb = query_block(S)

    def one_block(args):
        q_blk, blk = args
        rows = q_off + blk * qb + jnp.arange(qb)
        maxes, dens, nums = [], [], []
        for g, (window, dil) in enumerate(A_PATTERNS):
            idx = rows[:, None] - dil * jnp.arange(window // dil + 1)[None, :]
            valid = idx >= 0
            idx = jnp.maximum(idx, 0)
            k_g = k_all[:, idx]
            v_g = v_all[:, idx]
            s = jnp.einsum('bqhd,bqmhd->bqhm', q_blk[:, :, g], k_g).astype(jnp.float32) * ATTN_SCALE
            s = jnp.where(valid[None, :, None, :], s, -jnp.inf)
            m = jnp.max(s, axis=-1)
            e = jnp.exp(s - m[..., None])
            maxes.append(m)
            dens.append(jnp.sum(e, axis=-1))
            nums.append(jnp.einsum('bqhm,bqmhd->bqhd', e, v_g.astype(jnp.float32)))
        m_all = jnp.stack(maxes)
        w = jnp.exp(m_all - jnp.max(m_all, axis=0))
        num = jnp.sum(w[..., None] * jnp.stack(nums), axis=0)
        den = jnp.sum(w * jnp.stack(dens), axis=0)
        return (num / den[..., None]).astype(q.dtype)

    out = lax.map(one_block, (to_blocks(q, qb), jnp.arange(S // qb)))
    return from_blocks(out)

def band_attention(q, k_all, v_all, q_off, window):
    S = q.shape[1]
    qb = query_block(S)
    pad = ((0, 0), (window, 0), (0, 0), (0, 0))
    k_pad = jnp.pad(k_all, pad)
    v_pad = jnp.pad(v_all, pad)
    span = window + qb

    def one_block(args):
        q_blk, blk = args
        q0 = q_off + blk * qb
        k_b = lax.dynamic_slice_in_dim(k_pad, q0, span, axis=1)
        v_b = lax.dynamic_slice_in_dim(v_pad, q0, span, axis=1)
        krow = q0 - window + jnp.arange(span)
        qrow = q0 + jnp.arange(qb)
        valid = (krow[None, :] >= 0) & (krow[None, :] <= qrow[:, None]) & (krow[None, :] >= qrow[:, None] - window)
        s = jnp.einsum('bqhgd,bkhd->bqhgk', q_blk, k_b).astype(jnp.float32) * ATTN_SCALE
        s = jnp.where(valid[None, :, None, None, :], s, -jnp.inf)
        p = jax.nn.softmax(s, axis=-1)
        return jnp.einsum('bqhgk,bkhd->bqhgd', p, v_b.astype(jnp.float32))

    return from_blocks(lax.map(one_block, (to_blocks(q, qb), jnp.arange(S // qb))))

def compress(rows, w):
    B, L = rows.shape[0], rows.shape[1]
    n = L // CMP_STRIDE
    seg = rows[:, :n * CMP_STRIDE].reshape(B, n, CMP_STRIDE, C_KV_HEADS, HEAD_DIM)
    first = jnp.einsum('bnrhd,rh->bnhd', seg, w[:CMP_STRIDE])
    second = jnp.einsum('bnrhd,rh->bnhd', seg, w[CMP_STRIDE:])
    return first[:, :-1] + second[:, 1:]

def block_view(rows):
    B, L, H, D = rows.shape
    Lp = -(-L // SEL_BLOCK) * SEL_BLOCK
    rows = jnp.pad(rows, ((0, 0), (0, Lp - L), (0, 0), (0, 0)))
    return rows.reshape(B, Lp // SEL_BLOCK, SEL_BLOCK, H, D).transpose(0, 3, 1, 2, 4)

def make_fetch(k_new, v_new, n_past_blocks, pool, page_table, li):
    kb_new, vb_new = block_view(k_new), block_view(v_new)
    nb_new = kb_new.shape[2]
    bi = jnp.arange(k_new.shape[0])[:, None, None, None]
    hi = jnp.arange(C_KV_HEADS)[None, None, :, None]

    def fetch(idx):
        j_new = jnp.clip(idx - n_past_blocks, 0, nb_new - 1)
        k_n, v_n = kb_new[bi, hi, j_new], vb_new[bi, hi, j_new]
        if pool is None:
            return k_n, v_n
        bpp = pool.shape[3] // SEL_BLOCK
        j_past = jnp.clip(idx, 0, n_past_blocks - 1)
        phys = page_table[bi, j_past // bpp][..., None]
        off = (j_past % bpp)[..., None] * SEL_BLOCK + jnp.arange(SEL_BLOCK)
        h5 = hi[..., None]
        k_p = pool[phys, li, 0, off, h5]
        v_p = pool[phys, li, 1, off, h5]
        is_past = (idx < n_past_blocks)[..., None, None]
        return jnp.where(is_past, k_p, k_n), jnp.where(is_past, v_p, v_n)

    return fetch

def compressed_and_selected(q, q_rot, pos, k_cmp, v_cmp, total_len, fetch):
    S = q.shape[1]
    qb = query_block(S)
    n_cmp = k_cmp.shape[1]
    n_sel = -(-total_len // SEL_BLOCK)
    top = min(SEL_TOP, n_sel)
    blk_last = jnp.arange(n_cmp) * CMP_STRIDE + CMP_LEN - 1
    ci = jnp.arange(n_cmp)[:, None]
    sj = jnp.arange(n_sel)[None, :]
    shared = jnp.minimum(ci * CMP_STRIDE + CMP_LEN, (sj + 1) * SEL_BLOCK) - jnp.maximum(ci * CMP_STRIDE, sj * SEL_BLOCK)
    cmp_to_sel = jnp.maximum(shared, 0).astype(jnp.float32) / CMP_LEN
    sel_ids = jnp.arange(n_sel)[None, :]

    def one_block(args):
        q_blk, qr_blk, p_blk = args
        vis = blk_last[None, :] <= p_blk[:, None]
        s = jnp.einsum('bqhgd,bnhd->bqhgn', q_blk, k_cmp).astype(jnp.float32) * ATTN_SCALE
        s = jnp.where(vis[None, :, None, None, :], s, -jnp.inf)
        m = jnp.max(s, axis=-1, keepdims=True)
        m = jnp.where(jnp.isfinite(m), m, 0.0)
        e = jnp.exp(s - m)
        prob = e / jnp.maximum(jnp.sum(e, axis=-1, keepdims=True), TINY)
        o_cmp = jnp.einsum('bqhgn,bnhd->bqhgd', prob, v_cmp.astype(jnp.float32))
        imp = jnp.einsum('bqhgn,nj->bqhj', prob, cmp_to_sel)
        cur = (p_blk // SEL_BLOCK)[:, None]
        forced = (sel_ids == 0) | (sel_ids == cur) | (sel_ids == cur - 1)
        score = jnp.where(forced[:, None, :], imp + FORCE_BONUS, imp)
        score = jnp.where((sel_ids <= cur)[:, None, :], score, -jnp.inf)
        val, idx = lax.top_k(score, top)
        ok = jnp.isfinite(val)
        k_b, v_b = fetch(idx)
        kpos = idx[..., None] * SEL_BLOCK + jnp.arange(SEL_BLOCK)
        valid = ok[..., None] & (kpos <= p_blk[None, :, None, None, None])
        s2 = jnp.einsum('bqhgd,bqhkrd->bqhgkr', qr_blk, k_b).astype(jnp.float32) * ATTN_SCALE
        s2 = jnp.where(valid[:, :, :, None], s2, -jnp.inf)
        sh = s2.shape
        p2 = jax.nn.softmax(s2.reshape(sh[:4] + (-1,)), axis=-1).reshape(sh)
        o_sel = jnp.einsum('bqhgkr,bqhkrd->bqhgd', p2, v_b.astype(jnp.float32))
        return o_cmp, o_sel

    o_cmp, o_sel = lax.map(one_block, (to_blocks(q, qb), to_blocks(q_rot, qb), pos.reshape(S // qb, qb)))
    return from_blocks(o_cmp), from_blocks(o_sel)

def chunk_spatial_mix(vn, ws, bs):
    B, S, _ = vn.shape
    Sp = -(-S // B_CHUNK) * B_CHUNK
    vp = jnp.pad(vn, ((0, 0), (0, Sp - S), (0, 0))).reshape(B, Sp // B_CHUNK, B_CHUNK, B_GROUPS, B_GROUP_DIM)
    w = ws * jnp.tril(jnp.ones((B_CHUNK, B_CHUNK), ws.dtype))
    mixed = jnp.einsum('gts,bnsgc->bntgc', w, vp) + jnp.transpose(bs)[None, None, :, :, None]
    return mixed.reshape(B, Sp, B_WIDTH)[:, :S]

def ab_mixer(h, li, pos, a_past, prm):
    B, S, _ = h.shape
    xn = rms_norm(h, prm['ln_ab'][li])
    q, k, v, z_a, u_b, v_b, z_b = jnp.split(xn @ prm['w_in_ab'][li], split_points(AB_SIZES), axis=-1)
    q = rope_partial(rms_norm(q.reshape(B, S, A_GROUPS, A_HEADS, HEAD_DIM), prm['qn_a'][li]), pos)
    k = rope_partial(rms_norm(k.reshape(B, S, A_HEADS, HEAD_DIM), prm['kn_a'][li]), pos)
    v = v.reshape(B, S, A_HEADS, HEAD_DIM)
    if a_past is None:
        k_all, v_all, q_off = k, v, 0
        keep = min(A_WIN_MAX, S)
        kv_rows = jnp.stack([k[:, S - keep:], v[:, S - keep:]], axis=1)
    else:
        k_all = jnp.concatenate([a_past[:, 0], k], axis=1)
        v_all = jnp.concatenate([a_past[:, 1], v], axis=1)
        q_off = a_past.shape[2]
        kv_rows = jnp.stack([k, v], axis=1)
    o_a = dilated_attention(q, k_all, v_all, q_off).reshape(B, S, A_WIDTH)
    v_n = layer_norm(v_b, prm['ln_sgu'][li])
    o_b = u_b * chunk_spatial_mix(v_n, prm['ws_b'][li], prm['bs_b'][li])
    y = jnp.concatenate([o_a * jax.nn.silu(z_a), o_b * jax.nn.silu(z_b)], axis=-1) @ prm['w_out_ab'][li]
    chunk_start = ((S - 1) // B_CHUNK) * B_CHUNK
    return y, kv_rows, v_n[:, chunk_start:]

def nsa_mixer(h, li, pos, past, prm):
    B, S, _ = h.shape
    xn = rms_norm(h, prm['ln_c'][li])
    q, kc, vc, ks, vs, kw, vw, g, z = jnp.split(xn @ prm['w_in_c'][li], split_points(C_SIZES), axis=-1)
    kv_shape = (B, S, C_KV_HEADS, HEAD_DIM)
    q = rms_norm(q.reshape(B, S, C_KV_HEADS, C_GQA, HEAD_DIM), prm['qn_c'][li])
    q_rot = rope_partial(q, pos)
    kc, vc, vs, vw = kc.reshape(kv_shape), vc.reshape(kv_shape), vs.reshape(kv_shape), vw.reshape(kv_shape)
    ks = rope_partial(rms_norm(ks.reshape(kv_shape), prm['kn_c'][li, 1]), pos)
    kw = rope_partial(rms_norm(kw.reshape(kv_shape), prm['kn_c'][li, 2]), pos)
    if past is None:
        kc_all, vc_all, n_past = kc, vc, 0
        fetch = make_fetch(ks, vs, 0, None, None, li)
        kw_all, vw_all, w_off = kw, vw, 0
        keep = min(C_WIN, S)
        win_rows = jnp.stack([kw[:, S - keep:], vw[:, S - keep:]], axis=1)
    else:
        pages = past['cmp'][past['page_table'], li]
        n_past = pages.shape[1] * pages.shape[3]
        kc_all = jnp.concatenate([pages[:, :, 0].reshape(B, n_past, C_KV_HEADS, HEAD_DIM), kc], axis=1)
        vc_all = jnp.concatenate([pages[:, :, 1].reshape(B, n_past, C_KV_HEADS, HEAD_DIM), vc], axis=1)
        fetch = make_fetch(ks, vs, n_past // SEL_BLOCK, past['sel'], past['page_table'], li)
        wbuf = past['win'][:, li]
        kw_all = jnp.concatenate([wbuf[:, 0], kw], axis=1)
        vw_all = jnp.concatenate([wbuf[:, 1], vw], axis=1)
        w_off = wbuf.shape[2]
        win_rows = jnp.stack([kw, vw], axis=1)
    k_cmp = rms_norm(compress(kc_all, prm['cw_k'][li]), prm['kn_c'][li, 0])
    v_cmp = compress(vc_all, prm['cw_v'][li])
    o_cmp, o_sel = compressed_and_selected(q, q_rot, pos, k_cmp, v_cmp, n_past + S, fetch)
    o_win = band_attention(q_rot, kw_all, vw_all, w_off, C_WIN)
    gate = jax.nn.sigmoid(g.astype(jnp.float32)).reshape(B, S, 3, C_KV_HEADS, C_GQA, 1)
    o = gate[:, :, 0] * o_cmp + gate[:, :, 1] * o_sel + gate[:, :, 2] * o_win
    y = (o.reshape(B, S, C_WIDTH).astype(h.dtype) * jax.nn.silu(z)) @ prm['w_out_c'][li]
    return y, jnp.stack([kc, vc], axis=1), jnp.stack([ks, vs], axis=1), win_rows

def run_trunk(x, p, start, past, prm):
    B, S, _ = x.shape
    pos = start + jnp.arange(S, dtype=jnp.int32)
    h = x
    a_rows, b_rows, cmp_rows, sel_rows, win_rows = [], [], [], [], []
    for i in range(DEPTH):
        li = i // 2
        if i % 2 == 0:
            a_past = None if past is None else past['a'][:, li]
            mix, kv_a, v_b = ab_mixer(h, li, pos, a_past, prm)
            a_rows.append(kv_a)
            b_rows.append(v_b)
        else:
            mix, kv_c, kv_s, kv_w = nsa_mixer(h, li, pos, past, prm)
            cmp_rows.append(kv_c)
            sel_rows.append(kv_s)
            win_rows.append(kv_w)
        h = h + mix
        h = h + jax.nn.sigmoid(h @ prm['w_ple_gate'][i]) * (p[i] @ prm['w_ple'][i])
    return (h, jnp.stack(a_rows, axis=1), jnp.stack(b_rows, axis=1), jnp.stack(cmp_rows, axis=1),
            jnp.stack(sel_rows, axis=1), jnp.stack(win_rows, axis=1))

def setup_inputs(seed: int = 0) -> dict:
    key = jax.random.key(seed)
    keys = iter(jax.random.split(key, 48))

    def normal(shape, scale=1.0):
        return scale * jax.random.normal(next(keys), shape, jnp.float32)

    def gain(shape, noise=0.05):
        return 1.0 + normal(shape, noise)

    n_ab, n_c = (DEPTH + 1) // 2, DEPTH // 2
    n_pages = PAST_LEN // PAGE_SIZE
    n_used = DEC_BATCH * n_pages
    n_phys = n_used + max(1, n_used // 4)
    win_a, win_c = min(A_WIN_MAX, PAST_LEN), min(C_WIN, PAST_LEN)
    page_table = jax.random.permutation(next(keys), n_phys)[:n_used].reshape(DEC_BATCH, n_pages).astype(jnp.int32)
    return {
        'x_prompt': normal((BATCH, SEQ, D_MODEL)),
        'x_sample': normal((DEC_BATCH, DEC_SEQ, D_MODEL)),
        'cache_a_kv': normal((DEC_BATCH, n_ab, 2, win_a, A_HEADS, HEAD_DIM)),
        'cache_c_cmp_kv': normal((n_phys, n_c, 2, PAGE_SIZE, C_KV_HEADS, HEAD_DIM)),
        'cache_c_sel_kv': normal((n_phys, n_c, 2, PAGE_SIZE, C_KV_HEADS, HEAD_DIM)),
        'cache_c_win_kv': normal((DEC_BATCH, n_c, 2, win_c, C_KV_HEADS, HEAD_DIM)),
        'page_table': page_table,
        'p_prompt': normal((DEPTH, BATCH, SEQ, PLE_DIM)),
        'p_sample': normal((DEPTH, DEC_BATCH, DEC_SEQ, PLE_DIM)),
        'ln_ab': gain((n_ab, D_MODEL)),
        'w_in_ab': normal((n_ab, D_MODEL, sum(AB_SIZES)), D_MODEL ** -0.5),
        'qn_a': gain((n_ab, HEAD_DIM)),
        'kn_a': gain((n_ab, HEAD_DIM)),
        'ln_sgu': gain((n_ab, B_WIDTH)),
        'ws_b': normal((n_ab, B_GROUPS, B_CHUNK, B_CHUNK), 0.5 * B_CHUNK ** -0.5),
        'bs_b': gain((n_ab, B_GROUPS, B_CHUNK), 0.1),
        'w_out_ab': normal((n_ab, D_MODEL, D_MODEL), 0.5 * D_MODEL ** -0.5),
        'ln_c': gain((n_c, D_MODEL)),
        'w_in_c': normal((n_c, D_MODEL, sum(C_SIZES)), D_MODEL ** -0.5),
        'qn_c': gain((n_c, HEAD_DIM)),
        'kn_c': gain((n_c, 3, HEAD_DIM)),
        'cw_k': gain((n_c, CMP_LEN, C_KV_HEADS), 0.2) / CMP_LEN,
        'cw_v': gain((n_c, CMP_LEN, C_KV_HEADS), 0.2) / CMP_LEN,
        'w_out_c': normal((n_c, C_WIDTH, D_MODEL), 0.5 * C_WIDTH ** -0.5),
        'w_ple': normal((DEPTH, PLE_DIM, D_MODEL), 0.5 * PLE_DIM ** -0.5),
        'w_ple_gate': normal((DEPTH, D_MODEL, D_MODEL), D_MODEL ** -0.5),
    }

def reference(x_prompt, x_sample, cache_a_kv, cache_c_cmp_kv, cache_c_sel_kv, cache_c_win_kv, page_table,
              p_prompt, p_sample, ln_ab, w_in_ab, qn_a, kn_a, ln_sgu, ws_b, bs_b, w_out_ab,
              ln_c, w_in_c, qn_c, kn_c, cw_k, cw_v, w_out_c, w_ple, w_ple_gate):
    prm = dict(ln_ab=ln_ab, w_in_ab=w_in_ab, qn_a=qn_a, kn_a=kn_a, ln_sgu=ln_sgu, ws_b=ws_b, bs_b=bs_b,
               w_out_ab=w_out_ab, ln_c=ln_c, w_in_c=w_in_c, qn_c=qn_c, kn_c=kn_c, cw_k=cw_k, cw_v=cw_v,
               w_out_c=w_out_c, w_ple=w_ple, w_ple_gate=w_ple_gate)
    y_prompt, a_p, b_p, cmp_p, sel_p, win_p = run_trunk(x_prompt, p_prompt, 0, None, prm)
    past = dict(a=cache_a_kv, cmp=cache_c_cmp_kv, sel=cache_c_sel_kv, win=cache_c_win_kv, page_table=page_table)
    past_len = page_table.shape[1] * cache_c_cmp_kv.shape[3]
    y_sample, a_s, b_s, cmp_s, sel_s, win_s = run_trunk(x_sample, p_sample, past_len, past, prm)
    return (y_prompt, y_sample, a_p, a_s, b_p, b_s, cmp_p, cmp_s, sel_p, sel_s, win_p, win_s)


_drawn_inputs = setup_inputs


def setup_inputs(seed=0):
    import zlib

    import numpy as np

    out = dict(_drawn_inputs(seed))
    spreads = {}
    factors = {'cache_a_kv': 3.067,
     'cache_c_cmp_kv': 7.188,
     'cache_c_sel_kv': 6.248,
     'cache_c_win_kv': 5.378,
     'qn_a': 8.0,
     'bs_b': 2.843,
     'qn_c': 8.0,
     'cw_k': 8.0,
     'cw_v': 8.0}
    for name, (base, spread) in spreads.items():
        noise = np.random.default_rng([zlib.crc32(name.encode()), seed]).standard_normal(out[name].shape)
        drawn = base * np.exp(spread * noise) if base else spread * noise
        out[name] = __import__('jax').numpy.asarray(drawn.astype(out[name].dtype))
    for name, factor in factors.items():
        out[name] = (out[name] * factor).astype(out[name].dtype)
    return out
```

```python
from contextlib import ExitStack

import numpy as np

import concourse.bass as bass
from concourse import mybir

ALU = mybir.AluOpType
ACT = mybir.ActivationFunctionType
F32 = mybir.dt.float32
I32 = mybir.dt.int32
AX = mybir.AxisListType.X

P = 128
D = 2048
KC = D // P
S = 256
B = 8
T = S + B
PAST = 2048
NPG = PAST // P
AH = 8
PATTERNS = ((128, 1), (512, 4), (2048, 16))
AG = len(PATTERNS)
CH = 4
GQ = 4
HQ = CH * GQ
CKV = CH * P
CMP, SEG = 32, 16
NCMP = PAST // SEG - 1
NCP = S // SEG - 1
SB_ = 64
NSEL = PAST // SB_
NPICK = NSEL - 2
TOP = 16 - 3
WIN = 512
WT = WIN // P
PLE = 256
EPS = 1e-6
SCALE = float(P) ** -0.5
NEG = -1e30
TINY = 1e-30
HALF = 16
CB = 256
HB = KC // 2
NW = 4
NP = 4

C_ID = 0
C_GRP = C_ID + P
C_TRIL = C_GRP + P
C_COS = C_TRIL + P
C_SIN = C_COS + T
C_VIS = C_SIN + T
C_SEE = C_VIS + 32
C_C2S = C_SEE + 32
C_ROW = C_C2S + NPICK
C_END = C_ROW + CH
M_A = AG * 3 * P
M_CAUSAL = 3 * P
M_C = M_CAUSAL + NPICK * NPICK


def shape_constants():
    c = np.zeros((P, C_END), np.float32)
    i = np.arange(P)
    c[:, C_ID:C_ID + P] = np.eye(P)
    c[:, C_GRP:C_GRP + P] = (i[:, None] // GQ) == (i[None, :] // GQ)
    c[:, C_TRIL:C_TRIL + P] = i[:, None] <= i[None, :]
    pos = np.concatenate([np.arange(S), np.full(B, PAST)]).astype(np.float32)
    inv = np.exp((-np.log(np.float32(500000.0)) * np.arange(HALF, dtype=np.float32) / np.float32(HALF)).astype(np.float32)).astype(np.float32)
    ang = (pos[None, :] * inv[:, None]).astype(np.float32)
    cos, sin = np.cos(ang.astype(np.float64)), np.sin(ang.astype(np.float64))
    c[0:HALF, C_COS:C_COS + T] = cos
    c[HALF:2 * HALF, C_COS:C_COS + T] = cos
    c[0:HALF, C_SIN:C_SIN + T] = -sin
    c[HALF:2 * HALF, C_SIN:C_SIN + T] = sin
    for qt in range(2):
        see = (np.arange(16)[None, :] * SEG + CMP - 1 <= (qt * P + i)[:, None]) & (np.arange(16)[None, :] < NCP)
        c[:, C_VIS + 16 * qt:C_VIS + 16 * qt + 16] = np.where(see, 0.0, NEG)
        c[:, C_SEE + 16 * qt:C_SEE + 16 * qt + 16] = see
    n = np.arange(NCMP)[:, None]
    j = np.arange(1, NPICK + 1)[None, :]
    shared = np.minimum(n * SEG + CMP, (j + 1) * SB_) - np.maximum(n * SEG, j * SB_)
    c[:NCMP, C_C2S:C_ROW] = np.maximum(shared, 0) / CMP
    c[:, C_ROW:C_END] = (i[:, None] // 32) == np.arange(CH)[None, :]
    a = np.full((P, M_A), NEG, np.float32)
    m = np.zeros((P, M_C), np.float32)
    for qt in range(2):
        nk = P * (qt + 1)
        q, k = (qt * P + i)[:, None], np.arange(nk)[None, :]
        off = AG * P * qt
        for g, (window, dil) in enumerate(PATTERNS):
            ok = (k <= q) & (q - k <= window) & ((q - k) % dil == 0)
            a[:, off + g * nk:off + (g + 1) * nk] = np.where(ok, 0.0, NEG)
        m[:, P * qt:P * qt + nk] = np.where(k <= q, 0.0, NEG)
    e = np.arange(NPICK)
    m[:, M_CAUSAL:] = (e[None, None, :] < e[None, :, None]).reshape(1, -1)
    return c, a, m


def hybrid_trunk(nc, A):
    with ExitStack() as ctx:
        def sb(name, shape, dt=F32):
            return ctx.enter_context(nc.sbuf_tensor(name, shape, dt))

        def bank(name):
            return ctx.enter_context(nc.psum_tensor(name, [P, 512], F32))

        made = {}

        def sem(name):
            if name not in made:
                made[name] = ctx.enter_context(nc.semaphore(name))
            return made[name]

        PE_STEPS = ("pc_made", "gT_made", "gate_made", "kcpT_made", "scmp_made", "psum_made", "imp_made", "ptexp_made", "vn_made")
        DVE_STEPS = ("kcp_ready", "kcpT_set", "pc_centred", "pc_p", "qz_c", "kc_ready", "scmp_p", "pexp_ready", "sw_p", "vnew_set")

        def step(name):
            return sem("pe_steps" if name in PE_STEPS else "dve_steps")

        def done(name):
            steps = PE_STEPS if name in PE_STEPS else DVE_STEPS
            return step(name), steps.index(name) + 1

        const = sb("const", [P, C_END])
        mask = sb("mask", [P, M_C])
        ones = sb("ones", [P, P])
        zrow = sb("zrow", [1, 512])
        r0 = sb("r0", [P, KC, T])
        r1 = sb("r1", [P, KC, T])
        wring = sb("wring", [P, NW, HB, CB])
        proj = sb("proj", [P, 64, T])
        kcmp = sb("kcmp", [P, B, 4, P])
        vcmp = sb("vcmp", [P, B, 4, P])
        cring = sb("cring", [P, NP, 2 * CKV])
        scr = sb("scr", [P, 8, T])
        pT = sb("pT", [P, 2, T])
        small = sb("small", [P, 384])
        wide = sb("wide", [P, 2, 64, CH])
        ptab = sb("ptab", [1, B * NPG], I32)
        PJ = [bank(f"PJ{i}") for i in range(4)]
        XB = [bank(f"XB{i}") for i in range(4)]
        ident = const[:, C_ID:C_ID + P]
        cos, sin = const[0:32, C_COS:C_COS + T], const[0:32, C_SIN:C_SIN + T]

        at = [0]

        def cols(n):
            a = at[0]
            at[0] += n
            assert at[0] <= 384
            return small[:, a:a + n]
        NG = 2 * KC + 8 + 6
        gains = cols(NG)
        g_ab, g_c, g_sgu = gains[:, 0:KC], gains[:, KC:2 * KC], gains[:, 2 * KC:2 * KC + 8]
        g_qa, g_ka, g_qc = (gains[:, 2 * KC + 8 + n:2 * KC + 9 + n] for n in range(3))
        g_kc = gains[:, 2 * KC + 11:NG]
        eps = cols(1)
        nmx, den = cols(8), cols(8)
        rden, pnew = cols(8), cols(8)
        w00, b00 = cols(8), cols(8)
        lnt = sb("lnt", [P, 2, T])
        pnewT, lnr = lnt[:, 0, :], lnt[:, 1, :]
        vs_a = cols(AH * B)

        Z = proj[:, 40:64, :].rearrange("p a t -> p (a t)")
        x_nat = Z[:, 0:3 * D].rearrange("p (a n) -> p a n", a=3)
        p_nat = proj[:, 36:39, :].rearrange("p a t -> p (a t)")[:, 0:3 * PLE].rearrange("p (a n) -> p a n", a=3)

        w_ab = A["w_in_ab"][0].rearrange("(k p) n -> p k n", p=P)
        cmp_pool = A["cache_c_cmp_kv"].rearrange("n l v r h d -> n r (l v) (h d)")
        n_phys = A["cache_c_cmp_kv"].shape[0]

        AB1, AB2, OUT0, GATE0 = 0, 20, 36, 44
        CQ, CZ, OUT1, GATE1 = 52, 72, 80, 88
        CMP_A, AK, AV, CMP_B = 0, 80, 104, 128

        k_nat = Z[:, 0:2048].rearrange("p (t n) -> p t n", t=2)
        s_nat = Z[0:B, 2048:4096].rearrange("p (v n) -> p v n", v=2)
        S_sb = Z[:, 4096:5632].rearrange("p (u n) -> p u n", u=2)
        PT = Z[:, 5632:6144].rearrange("p (u n) -> p u n", u=2)
        qz = Z[:, 0:1536].rearrange("p (g b h m) -> p g b h m", g=AG, b=B, h=AH)
        KT = Z[:, 1536:3584].rearrange("p (u n) -> p u n", u=2)
        Sd = Z[:, 3584:4368].rearrange("p (u n) -> p u n", u=2)
        PTd = Z[:, 4368:5136].rearrange("p (g u r) -> p g u r", g=AG, u=2)
        Od = Z[:, 5136:5648].rearrange("p (u n) -> p u n", u=2)
        prod = Z[:, 1536:2304].rearrange("p (g u r) -> p g u r", g=AG, u=2)
        diag = Z[:, 2304:2560].rearrange("p (u r) -> p u r", u=2)

        xc = proj[:, 56:64, :]
        sq8 = proj[:, 8:16, :]
        vn_nat = sq8.rearrange("p a t -> p (a t)")[:, 0:2048].rearrange("p (t n) -> p t n", t=2)
        vn_s = proj[0:B, 16:20, :].rearrange("p a t -> p (a t)")[:, 0:1024]
        ws_nat = proj[:, 20:24, :].rearrange("p a t -> p (a t)")[:, 0:1024].rearrange("p (g s) -> p g s", g=8)
        wsT = proj[:, 24:28, :].rearrange("p a t -> p (a t)")[:, 0:1024].rearrange("p (g s) -> p g s", g=8)
        bs = proj[0:1, 28:32, :].rearrange("p a t -> p (a t)")[:, 0:1024]
        wple = proj[:, 16:32, :].rearrange("p a t -> p (a t)")[:, 0:4096].rearrange("p (k n) -> p k n", k=2)

        F = proj[:, 56:64, :].rearrange("p a t -> p (a t)")
        SC = scr[:, :, :].rearrange("p a t -> p (a t)")
        Q = proj[:, 0:16, :].rearrange("p a t -> p (a t)")
        KV = proj[:, 16:24, :].rearrange("p a t -> p (a t)")
        kst = F[:, 0:2048].rearrange("p (a t n) -> p a t n", a=2, t=2)
        c_nat = cring[0:B, 0:3, :].rearrange("p a (v n) -> p (a v) n", v=2)
        r40 = proj[:, 56:64, :]
        wg = cring[:, 3, 0:16 * 48].rearrange("p (k n) -> p k n", k=16)
        gT = lnt[0:48, 0, :]
        gate_p = lnt[:, 1, 0:96].rearrange("p (t j h) -> p t j h", t=2, j=3)
        gate_8 = lnt[0:B, 1, 96:144]
        gate_s = lnt[:, 1, 144:147]
        kcp = SC[:, 0:128]
        kcpT = SC[:, 128:256]
        vcp = SC[0:32, 256:768].rearrange("p (h d) -> p h d", h=CH)
        junk = SC[:, 1800:1928]
        Pc = SC[:, 768:1280].rearrange("p (u n) -> p u n", n=16)
        PcT = SC[0:16, 1280:1536].rearrange("p (u n) -> p u n", u=2)
        S_c = F[:, 0:1024].rearrange("p (u n) -> p u n", u=2)
        PT_c = F[:, 1024:2048].rearrange("p (u n) -> p u n", u=2)
        qzu = SC[:, 0:1024].rearrange("p (b h m) -> p b h m", b=B, h=CH)
        qzr = Q[:, 0:1024].rearrange("p (b h m) -> p b h m", b=B, h=CH)
        S_sel = KV[:, 0:2048]
        KTc = F[:, 0:2048].rearrange("p (h n) -> p h n", h=CH)
        PT_sel = SC[:, 0:2048].rearrange("p (g r) -> p g r", g=NPG)
        S_win = Q[:, 1024:1536]
        S_cmp = Q[:, 1536:1664]
        P_sum = Q[:, 1664:1792]
        imp = Q[:, 1792:1792 + NPICK]
        rank = Q[:, 1824:1824 + NPICK]
        sneg = Q[:, 1856:1888]
        gt = Q[:, 1888:2788].rearrange("p (j i) -> p j i", j=NPICK)
        eq = Q[:, 2788:3688].rearrange("p (j i) -> p j i", j=NPICK)
        P_exp = Q[:, 1888:2400].rearrange("p (a h i) -> p a h i", a=4, h=CH)
        PT_exp = Q[:, 2400:2912].rearrange("p (a r) -> p a r", a=4)
        PT_win = Q[:, 2912:3424].rearrange("p (a r) -> p a r", a=4)
        vnew = Q[:, 3424:3552]
        diag_c = Q[:, 3688:3944].rearrange("p (u r) -> p u r", u=2)
        O_c = KV[:, 0:256].rearrange("p (u d) -> p u d", u=2)
        s_new = cols(2)
        p_new = cols(2)
        mx_c, den_c, rd_c = cols(3), cols(3), cols(3)
        cmx = cols(32)
        kss, krt = cols(32), cols(32)
        y_nat = proj[:, 32:48, :].rearrange("p a t -> p (a t)")[:, 0:4096].rearrange("p (t n) -> p t n", t=2)
        y_s = proj[0:B, 48:56, :].rearrange("p a t -> p (a t)")[:, 0:2048]
        hring = cring[:, :, :].rearrange("p a (s n) -> p (a s) n", s=2)

        def tileT(c):
            return slice(c * P, (c + 1) * P)

        block = ctx.enter_context(nc.Block())

        @block.sync
        def _(sp):
            sp.dma_start(const[:, :], A["const"]).then_inc(sem("consts_in"), 16)
            sp.dma_start(mask[:, 0:M_A], A["mask_a"]).then_inc(sem("mask_a_in"), 16)
            r = 0
            for src in (A["ln_ab"][0], A["ln_c"][0], A["ln_sgu"][0], A["qn_a"][0], A["kn_a"][0], A["qn_c"][0],
                        A["kn_c"].rearrange("l k d -> (l k d)")):
                n = src.shape[0] // P
                sp.dma_start(scr[r:r + n, 7, 0:P], src.rearrange("(c p) -> c p", p=P)).then_inc(sem("gains_in"), 16)
                r += n
            for t in range(2):
                sp.dma_start(x_nat[:, t, :], A["x_prompt"][0, tileT(t), :]).then_inc(sem("x_in"), 16)
                sp.dma_start(p_nat[:, t, :], A["p_prompt"][0, 0, tileT(t), :]).then_inc(sem("x_in"), 16)
            sp.dma_start(x_nat[0:B, 2, :], A["x_sample"].rearrange("b s d -> b (s d)")).then_inc(sem("x_in"), 16)
            sp.dma_start(p_nat[0:B, 2, :], A["p_sample"][0].rearrange("b s d -> b (s d)")).then_inc(sem("x_in"), 16)
            sp.dma_start(ptab[:, :], A["page_table"].rearrange("(o b) n -> o (b n)", o=1)).then_inc(sem("ptab_in"), 16)
            sp.wait_ge(sem("wide_zero"), 1)
            for v, w in enumerate((A["cw_k"], A["cw_v"])):
                for n in range(8):
                    for half in range(2):
                        sp.dma_start(wide[SEG * n:SEG * (n + 1), v, 32 + n - half, :], w[0, SEG * half:SEG * (half + 1), :])\
                          .then_inc(sem("wide_in"), 16)
            sp.wait_ge(sem("ptab_in"), 16)

            def weights(n, w, i, bl):
                for hf in range(2):
                    q = 2 * (bl % 2) + hf
                    if hf == 0:
                        sp.wait_ge(sem("w_used"), n + 1)
                    else:
                        sp.wait_ge(sem("proj_made"), n * 2 + 2)
                    sp.dma_start(wring[:, q], w[:, hf * HB:(hf + 1) * HB, bass.ds((i * 4 + bl) * CB, CB)])\
                      .then_inc(sem(f"w_in{q}"), 16)

            def pages(i, n0, bl, pool):
                for n in range(4):
                    pg = 4 * bl + n
                    sp.wait_ge(sem("c_used"), i * 16 + (4 * bl + n + 1 + (16 * n0 if n0 == 0 else CMP_B)))
                    page = sp.value_load(ptab[0:1, bass.ds(i * NPG + (n0 * NPG + pg), 1)], min_val=0, max_val=n_phys - 1)
                    sp.dma_start(cring[:, n, :].rearrange("p (v c) -> p v c", v=2), pool[bass.ds(page, 1)])\
                      .then_inc(sem(f"c_in{n}"), 16)

            with sp.Fori(0, 5) as i:
                for bl in range(4):
                    weights(i * 4 + bl, w_ab, i, bl)
                    pages(i, 0, bl, cmp_pool)

            for kv, base in ((0, AK), (1, AV)):
                for b in range(B):
                    for g, (window, dil) in enumerate(PATTERNS):
                        n = base + AG * b + g
                        rows = slice(PAST - window, PAST, dil)
                        if n == AK + NP:
                            sp.wait_ge(sem("nat_taken"), 32)
                            for t in range(2):
                                sp.dma_start(A["new_a_kv_prompt"][0, 0, 0, tileT(t)].rearrange("p h d -> p (h d)"), k_nat[:, t, :])\
                                  .then_inc(sem("a_out"), 16)
                                sp.dma_start(A["new_a_kv_prompt"][0, 0, 1, tileT(t)], proj[:, 32:40, tileT(t)]).then_inc(sem("a_out"), 16)
                            sp.dma_start(A["new_a_kv_sample"].rearrange("b l v s h d -> (b l) v (s h d)"), s_nat).then_inc(sem("a_out"), 16)
                        sp.wait_ge(sem("c_used"), n + 1)
                        sp.dma_start(cring[:, n % NP, :], A["cache_a_kv"][b, 0, kv, rows].rearrange("r h d -> r (h d)"))\
                          .then_inc(sem(f"c_in{n % NP}"), 16)

            with sp.Fori(0, 3) as i:
                for bl in range(4):
                    weights(i * 4 + (AB2 + bl), w_ab, i + 5, bl)
                    pages(i, 5, bl, cmp_pool)
            for bl in range(4):
                weights(AB2 + 12 + bl, w_ab, 8, bl)
            sp.wait_ge(sem("oTd"), B)
            sp.dma_start(ws_nat, A["ws_b"][0].rearrange("g t s -> t g s")).then_inc(sem("ws_in"), 16)
            sp.dma_start(bs, A["bs_b"].rearrange("l g t -> l (g t)")).then_inc(sem("ws_in"), 16)

            w_o = A["w_out_ab"][0].rearrange("(k p) n -> p k n", p=P)
            with sp.Fori(0, 2) as i:
                for bl in range(4):
                    weights(i * 4 + (OUT0 + bl), w_o, i, bl)
            sp.wait_ge(sem("vn_taken"), 16)
            sp.dma_start(A["state_b_v_prompt"].rearrange("b l c n -> (b l c) n"), vn_nat[:, 1, :]).then_inc(sem("b_out"), 16)
            sp.dma_start(A["state_b_v_sample"].rearrange("b l s n -> b (l s n)"), vn_s).then_inc(sem("b_out"), 16)
            sp.wait_ge(sem("mixed"), 8)
            sp.wait_ge(sem("b_out"), 32)
            sp.dma_start(wple, A["w_ple"][0].rearrange("(k p) n -> p k n", p=P)).then_inc(sem("wple_in"), 16)
            w_g = A["w_ple_gate"][0].rearrange("(k p) n -> p k n", p=P)
            with sp.Fori(0, 2) as i:
                for bl in range(4):
                    weights(i * 4 + (GATE0 + bl), w_g, i, bl)
            sp.dma_start(mask[:, :], A["mask_c"]).then_inc(sem("mask_c_in"), 16)
            for t in range(2):
                sp.dma_start(p_nat[:, t, :], A["p_prompt"][1, 0, tileT(t), :]).then_inc(sem("p_in"), 16)
            sp.dma_start(p_nat[0:B, 2, :], A["p_sample"][1].rearrange("b s d -> b (s d)")).then_inc(sem("p_in"), 16)
            w_c = A["w_in_c"][0].rearrange("(k p) n -> p k n", p=P)
            with sp.Fori(0, 5) as i:
                for bl in range(4):
                    weights(i * 4 + (CQ + bl), w_c, i, bl)
            sp.wait_ge(sem("c_used"), NP + CMP_B + 48)
            sp.dma_start(wg, w_c[:, :, 40 * P:40 * P + 48]).then_inc(sem("wg_in"), 16)
            sp.wait_ge(sem("cnat_taken"), 48)
            k2 = {0: ("cmp", 16), 1: ("cmp", 20), 2: ("sel", None), 3: ("sel", 28), 4: ("win", None), 5: ("win", 36)}
            for n, (name, slot) in k2.items():
                for t in range(2):
                    src = proj[:, slot:slot + 4, tileT(t)] if slot is not None else kst[:, n // 4, t, :]
                    dst = A[f"new_c_{name}_kv_prompt"][0, 0, n % 2, tileT(t)]
                    sp.dma_start(dst if slot is not None else dst.rearrange("p h d -> p (h d)"), src).then_inc(sem("c_out"), 16)
                sp.dma_start(A[f"new_c_{name}_kv_sample"][:, 0, n % 2, 0].rearrange("b h d -> b (h d)"), c_nat[:, n, :])\
                  .then_inc(sem("c_out"), 16)
            sp.wait_ge(sem("gate_taken"), 3)
            with nc.allow_non_contiguous_dma(reason="384 gate values change partitions"):
                for j in range(3):
                    for h in range(CH):
                        sp.dma_start(gate_s[32 * h:32 * h + 32, j:j + 1],
                                     gate_8[:, j * HQ + GQ * h:j * HQ + GQ * h + GQ]).then_inc(sem("gate_s_in"), 16)
            sp.wait_ge(sem("c_out"), 16 * 18)
            sel_pool = A["cache_c_sel_kv"].rearrange("n l v r h d -> n r (l v) (h d)")

            def page_of(b_pg):
                return sp.value_load(ptab[0:1, bass.ds(b_pg, 1)], min_val=0, max_val=n_phys - 1)

            def page_set(first, kv, n):
                for q in range(4):
                    page = page_of(first + q)
                    sp.dma_start(hring[:, 4 * (n % 2) + q, :].rearrange("p (o c) -> p o c", o=1),
                                 sel_pool[bass.ds(page, 1), :, kv, :].rearrange("o r c -> r o c")).then_inc(sem(f"set_in{n % 2}"), 16)

            win = A["cache_c_win_kv"].rearrange("b l v (w p) h d -> b w p (l v) (h d)", p=P)

            def win_set(b, kv, n):
                for q in range(WT):
                    sp.dma_start(hring[:, 4 * (n % 2) + q, :].rearrange("p (o c) -> p o c", o=1),
                                 win[bass.ds(b, 1), q, :, kv, :].rearrange("o p c -> p o c")).then_inc(sem(f"set_in{n % 2}"), 16)

            with sp.Fori(0, 4) as i:
                for b in range(B):
                    sp.wait_ge(sem("kt_T"), i * 32 + (4 * b + 4))
                    page_set(i * 4 + b * NPG, 0, b)
            for b in range(B):
                sp.wait_ge(sem("kt_T"), 128 + 4 * b + 4)
                win_set(b, 0, b)
            sp.wait_ge(sem("kt_T"), 8 + 160)
            with sp.Fori(0, 4) as i:
                for n in range(10):
                    b2, k = n // 5, n % 5
                    sp.wait_ge(sem("set_used"), i * 10 + (n + 1))
                    if k < 4:
                        page_set(i * 2 * NPG + (b2 * NPG + 4 * k), 1, n)
                    else:
                        win_set(i * 2 + b2, 1, n)

            w_z = w_c[:, :, 40 * P + 48:40 * P + 48 + D]
            with sp.Fori(0, 2) as i:
                for bl in range(4):
                    weights(i * 4 + (CZ + bl), w_z, i, bl)
            w_o1 = A["w_out_c"][0].rearrange("(k p) n -> p k n", p=P)
            with sp.Fori(0, 2) as i:
                for bl in range(4):
                    weights(i * 4 + (OUT1 + bl), w_o1, i, bl)
            sp.wait_ge(sem("cat1"), 2)
            sp.dma_start(wple, A["w_ple"][1].rearrange("(k p) n -> p k n", p=P)).then_inc(sem("wple_in"), 16)
            w_g1 = A["w_ple_gate"][1].rearrange("(k p) n -> p k n", p=P)
            with sp.Fori(0, 2) as i:
                for bl in range(4):
                    weights(i * 4 + (GATE1 + bl), w_g1, i, bl)
            for q in range(4):
                sp.wait_ge(sem("y_taken"), 8 * (q + 1))
                a = slice(q * 512, (q + 1) * 512)
                for t in range(2):
                    sp.dma_start(A["y_prompt"][0, tileT(t), a], y_nat[:, t, a]).then_inc(sem("y_out"), 16)
                sp.dma_start(A["y_sample"][:, 0, a], y_s[:, a]).then_inc(sem("y_out"), 16)
            sp.wait_ge(sem("a_out"), 16 * 5)
            sp.wait_ge(sem("b_out"), 32)
            sp.wait_ge(sem("c_out"), 16 * 18)
            sp.wait_ge(sem("y_out"), 16 * 12)

        @block.gpsimd
        def _(pool):
            nc.gpsimd.memset(wide[:, :, :, :], 0.0).then_inc(sem("wide_zero"), 1)
            nc.gpsimd.memset(ones[:, :], 1.0).then_inc(sem("ones_set"), 1)
            nc.gpsimd.memset(zrow[:, :], 0.0).then_inc(sem("ones_set"), 1)
            nc.gpsimd.memset(eps, EPS).then_inc(sem("ones_set"), 1)

        @block.scalar
        def _(act):
            for f, n in (("w_used", 2), ("proj_made", 4), ("c_used", NP), ("proj_free", 4), ("cmp_free", 1),
                         ("kt_T", 8), ("kt_used", 4), ("S_taken", 1), ("set_used", 2), ("OT_taken", 2)):
                act.sem_inc(sem(f), n)
            act.wait_ge(sem("xT_made"), 1)
            nc.scalar.copy(gains, XB[3][:, 0:NG]).then_inc(sem("gains_set"), 1)
            for c in range(KC + 2):
                act.wait_ge(sem("xT_made"), c + 2)
                dst = r0[:, c, :] if c < KC else pT[:, c - KC, :]
                nc.scalar.copy(dst, XB[c % 4][:, 0:T]).then_inc(sem("xT_taken"), 1)
            act.wait_ge(sem("ones_set"), 3)

            def rms(layer, h, sq):
                for c in range(KC):
                    if layer == 0:
                        act.wait_ge(sem("xT_taken"), c + 1)
                    nc.scalar.activation(sq[:, c, :], h[:, c, :], ACT.Square).then_inc(sem(f"rms_sq{layer}"), 1)
                act.wait_ge(sem(f"rms_sum{layer}"), 1)
                nc.scalar.activation(scr[:, 0, :], XB[0][:, 0:T], ACT.Sqrt, bias=eps, scale=1.0 / D)\
                  .then_inc(sem(f"rms_root{layer}"), 1)

            rms(0, r0, r1)
            with act.Fori(0, 5) as i:
                for j in range(8):
                    act.wait_ge(sem("proj_made"), i * 8 + (4 + j + 1))
                    nc.scalar.copy(proj[:, bass.ds(i * 8 + j, 1), :], PJ[j % 4][:, 0:T]).then_inc(sem("proj_free"), 1)

            for grp in range(4):
                if grp == 0:
                    act.wait_ge(sem("proj_free"), 4 + 40)
                else:
                    act.wait_ge(sem("qn_sum"), 8 * grp)
                    act.wait_ge(sem("qn_done"), grp)
                nc.scalar.activation(scr[:, :, :], proj[:, 8 * grp:8 * grp + 8, :], ACT.Square).then_inc(sem("qn_sq"), 1)
                for j in range(8):
                    act.wait_ge(sem("qn_sum"), 8 * grp + j + 1)
                    nc.scalar.activation(Z[:, j * T:(j + 1) * T], XB[j % 4][:, 0:T], ACT.Sqrt, bias=eps, scale=1.0 / P)\
                      .then_inc(sem("qn_root"), 1)
            act.wait_ge(sem("qn_done"), 4)
            for t in range(16):
                act.wait_ge(sem("nat_made"), t + 1)
                src = XB[t % 4]
                dst = k_nat[:, :, tileT(t)] if t < 8 else proj[:, 24 + t, 0:S].rearrange("p (t n) -> p t n", t=2)
                nc.scalar.copy(dst, src[:, 0:S].rearrange("p (t n) -> p t n", t=2)).then_inc(sem("nat_taken"), 1)
                nc.scalar.copy(s_nat[:, t // 8, tileT(t % 8)], src[0:B, S:S + P]).then_inc(sem("nat_taken"), 1)

            def pa_exp(u):
                nk = AG * P * (u % 2 + 1)
                act.wait_ge(sem("pa_max"), u + 1)
                nc.scalar.activation(S_sb[:, u % 2, 0:nk], S_sb[:, u % 2, 0:nk], ACT.Exp, bias=nmx[:, u % 2:u % 2 + 1],
                                     accum_out=den[:, u % 2:u % 2 + 1]).then_inc(sem("pa_exp"), 1)

            def pa_out(u):
                qt = u % 2
                act.wait_ge(sem("pa_pT"), u + 1)
                nc.scalar.copy(PT[:, u % 2, 0:P * (qt + 1)], XB[3][:, 0:P * (qt + 1)]).then_inc(sem("pa_pT_taken"), 1)
                act.wait_ge(sem("pa_o"), u + 1)
                nc.scalar.copy(scr[:, u // 2, tileT(qt)], XB[3][:, 384:512]).then_inc(sem("pa_o_taken"), 1)

            pa_exp(0)
            for u in range(16):
                if u < 15:
                    pa_exp(u + 1)
                pa_out(u)

            act.wait_ge(sem("a_out"), 16 * 5)
            for n in range(B * AG):
                act.wait_ge(sem("dk_T"), n + 1)
                if n >= 2:
                    act.wait_ge(sem("c_used"), AK + NP + n - 1)
                nc.scalar.copy(KT[:, n % 2, 0:512], XB[2][:, :]).then_inc(sem("dk_T_taken"), 1)
            for u in range(2):
                act.wait_ge(sem("d_max"), 1)
                nc.scalar.activation(Sd[:, u, 0:387], Sd[:, u, 0:387], ACT.Exp, bias=nmx[:, u:u + 1],
                                     accum_out=den[:, u:u + 1]).then_inc(sem("d_exp"), 1)
            act.wait_ge(sem("d_pT"), 1)
            nc.scalar.copy(PTd[:, 0:2, :, :], XB[2][:, :].rearrange("p (g u r) -> p g u r", g=2, u=2)).then_inc(sem("d_pT_taken"), 1)
            nc.scalar.copy(PTd[:, 2, :, :], XB[3][:, 0:256].rearrange("p (u r) -> p u r", u=2)).then_inc(sem("d_pT_taken"), 1)
            for b in range(B):
                act.wait_ge(sem("c_used"), AV + NP + 3 * b + 3)
                nc.scalar.copy(Od[:, b % 2, :], XB[b % 2][:, 0:256]).then_inc(sem("dO_taken"), 1)

            act.wait_ge(sem("oTd"), B)
            with act.Fori(0, 3) as i:
                for j in range(8):
                    act.wait_ge(sem("proj_made"), i * 8 + (44 + j + 1))
                    nc.scalar.copy(proj[:, bass.ds(i * 8 + (40 + j), 1), :], PJ[j % 4][:, 0:T]).then_inc(sem("proj_free"), 1)
            for j in range(8):
                act.wait_ge(sem("proj_made"), 68 + j + 1)
                nc.scalar.copy(proj[:, j, :], PJ[j % 4][:, 0:T]).then_inc(sem("proj_free"), 1)
            act.wait_ge(sem("ln_centred"), 1)
            nc.scalar.activation(sq8, xc, ACT.Square).then_inc(sem("ln_sq"), 1)
            act.wait_ge(sem("ln_sum"), 2)
            nc.scalar.activation(pnewT, XB[1][:, 0:T], ACT.Sqrt, bias=eps, scale=1.0 / 1024).then_inc(sem("ln_root"), 1)
            act.wait_ge(sem("proj_free"), 4 + 72)
            nc.scalar.activation(proj[:, 40:48, :], proj[:, 40:48, :], ACT.Silu).then_inc(sem("silu"), 1)
            nc.scalar.activation(proj[:, 0:8, :], proj[:, 0:8, :], ACT.Silu).then_inc(sem("silu"), 1)
            for g in range(8):
                act.wait_ge(sem("vn_T"), g + 1)
                src = XB[g % 2]
                nc.scalar.copy(vn_nat[:, :, tileT(g)], src[:, 0:S].rearrange("p (t n) -> p t n", t=2)).then_inc(sem("vn_taken"), 1)
                nc.scalar.copy(vn_s[:, tileT(g)], src[0:B, S:S + P]).then_inc(sem("vn_taken"), 1)

            def ple(layer, free):
                act.wait_ge(sem(free[0]), free[1])
                for c in range(KC):
                    act.wait_ge(sem(f"ple_made{layer}"), c + 1)
                    nc.scalar.copy(proj[:, c, :], XB[c % 4][:, 0:T]).then_inc(sem(f"ple_taken{layer}"), 1)

            def gate(layer, done):
                with act.Fori(0, 2) as i:
                    for j in range(8):
                        act.wait_ge(sem("proj_made"), i * 8 + (4 + done + j + 1))
                        act.wait_ge(sem(f"h_new{layer}"), i * 8 + (j + 1))
                        nc.scalar.activation(scr[:, j % 4, :], PJ[j % 4][:, 0:T], ACT.Sigmoid).then_inc(sem("proj_free"), 1)
            ple(0, ("cat0", 4))
            gate(0, 88)

            for k in range(2):
                act.wait_ge(sem("pT_made"), k + 1)
                nc.scalar.copy(pT[:, k, :], XB[1 + k][:, 0:T]).then_inc(sem("pT_taken"), 1)
            act.wait_ge(sem("h_new0"), 4 + KC)
            rms(1, r1, r0)
            act.wait_ge(sem("xn_ready1"), KC)
            with act.Fori(0, 5) as i:
                for j in range(8):
                    act.wait_ge(sem("proj_made"), i * 8 + (4 + 104 + j + 1))
                    nc.scalar.copy(proj[:, bass.ds(i * 8 + j, 1), :], PJ[j % 4][:, 0:T]).then_inc(sem("proj_free"), 1)

            n = 0
            for grp, (first, size) in enumerate(((0, 8), (8, 8), (24, 4), (32, 4))):
                if grp == 0:
                    act.wait_ge(sem("proj_free"), 4 + 144)
                else:
                    act.wait_ge(sem("cn_done"), grp)
                nc.scalar.activation(scr[:, 0:size, :], proj[:, first:first + size, :], ACT.Square).then_inc(sem("cn_sq"), 1)
                for j in range(size):
                    n += 1
                    act.wait_ge(sem("cn_sum"), n)
                    nc.scalar.activation(r40[:, j, :], XB[j % 4][:, 0:T], ACT.Sqrt, bias=eps, scale=1.0 / P)\
                      .then_inc(sem("cn_root"), 1)
            act.wait_ge(sem("cn_done"), 4)
            for t in range(24):
                act.wait_ge(sem("cnat_made"), t + 1)
                src, v = XB[t % 4], t // 4
                dst = kst[:, v // 4, :, tileT(t % 4)] if v in (2, 4) else proj[:, 16 + t, 0:S].rearrange("p (t n) -> p t n", t=2)
                nc.scalar.copy(dst, src[:, 0:S].rearrange("p (t n) -> p t n", t=2)).then_inc(sem("cnat_taken"), 1)
                nc.scalar.copy(c_nat[:, v, tileT(t % 4)], src[0:B, S:S + P]).then_inc(sem("cnat_taken"), 1)
            act.wait_ge(*done("pc_made"))
            nc.scalar.copy(kcp, XB[0][:, 0:P]).then_inc(sem("act_chain"), 1)
            nc.scalar.copy(vcp, XB[1][0:32, :].rearrange("p (h d) -> p h d", h=CH)).then_inc(sem("vcp_set"), 1)
            act.wait_ge(sem("act_chain"), 1)
            nc.scalar.activation(junk, kcp, ACT.Square, accum_out=kss[:, 0:1]).then_inc(sem("act_chain"), 1)
            act.wait_ge(sem("act_chain"), 2)
            nc.scalar.activation(krt[:, 0:1], kss[:, 0:1], ACT.Sqrt, bias=eps, scale=1.0 / P).then_inc(sem("pc_root"), 1)
            act.wait_ge(*done("gT_made"))
            nc.scalar.activation(gT, XB[2][0:48, 0:T], ACT.Sigmoid).then_inc(sem("gT_set"), 1)
            act.wait_ge(*done("gate_made"))
            for t in range(2):
                nc.scalar.copy(gate_p[:, t].rearrange("p j h -> p (j h)"), XB[3][:, 64 * t:64 * t + 48]).then_inc(sem("gate_taken"), 1)
            nc.scalar.copy(gate_8, XB[3][0:B, 128:176]).then_inc(sem("gate_taken"), 1)
            act.wait_ge(*done("pc_centred"))
            nc.scalar.activation(Pc, Pc, ACT.Exp).then_inc(sem("pc_exp"), 1)
            act.wait_ge(*done("pc_p"))
            act.wait_ge(sem("c_out"), 16 * 18)

            def pc_exps(u):
                qt, nk = u % 2, P * (u % 2 + 1)
                act.wait_ge(sem("cu_max"), u + 1)
                for br in range(2):
                    a = slice(br * nk, (br + 1) * nk)
                    nc.scalar.activation(S_c[:, qt, a], S_c[:, qt, a], ACT.Exp, bias=nmx[:, 2 * qt + br:2 * qt + br + 1],
                                         accum_out=den[:, 2 * qt + br:2 * qt + br + 1]).then_inc(sem("cu_exp"), 1)

            def pc_out(u):
                qt, nk = u % 2, P * (u % 2 + 1)
                act.wait_ge(sem("cu_pT"), u + 1)
                nc.scalar.copy(PT_c[:, qt, 0:2 * nk], XB[2][:, 0:2 * nk]).then_inc(sem("cu_pT_taken"), 1)
                nc.scalar.copy(PcT[:, qt, :], XB[3][0:16, 0:P]).then_inc(sem("cu_pT_taken"), 1)
                act.wait_ge(sem("cu_o"), u + 1)
                nc.scalar.copy(proj[:, 40 + u // 2, tileT(qt)], XB[3][:, P:2 * P]).then_inc(sem("cu_o_taken"), 1)

            pc_exps(0)
            for u in range(32):
                if u < 31:
                    pc_exps(u + 1)
                pc_out(u)

            for b in range(B):
                for a in range(4):
                    n = 4 * b + a
                    if n >= 2:
                        act.wait_ge(sem("ks_sum"), n - 1)
                    nc.scalar.activation(SC[:, 1800 + P * (n % 2):1800 + P * (n % 2 + 1)], kcmp[:, b, a, :], ACT.Square,
                                         accum_out=kss[:, n:n + 1]).then_inc(sem("ks_sum"), 1)
            act.wait_ge(sem("ks_sum"), 32)
            nc.scalar.activation(krt, kss, ACT.Sqrt, bias=eps, scale=1.0 / P).then_inc(sem("ks_root"), 1)
            for b in range(B):
                act.wait_ge(sem("kcT_made"), b + 1)
                nc.scalar.activation(kcmp[:, b].rearrange("p a r -> p (a r)"), XB[b % 4][:, :], ACT.Copy, scale=g_kc[:, 0:1])\
                  .then_inc(sem("kcT_taken"), 1)
            act.wait_ge(sem("sc_max"), 1)
            nc.scalar.activation(S_cmp[:, 0:NCMP], S_cmp[:, 0:NCMP], ACT.Exp, bias=mx_c[:, 0:1], accum_out=den_c[:, 0:1])\
              .then_inc(sem("sc_exp"), 1)
            act.wait_ge(*done("psum_made"))
            nc.scalar.copy(P_sum, XB[0][:, 128:256]).then_inc(sem("psum_taken"), 1)

            def k_even(c, base):
                for m in range(0, 32, 2):
                    act.wait_ge(sem("kt_T"), c * 32 + (8 + base + m + 1))
                    act.wait_ge(sem("kt_used"), c * 32 + (base + m + 1))
                    nc.scalar.copy(KTc[:, m % 4, :], XB[1 + m % 2][:, :]).then_inc(sem("kt_even"), 1)
            act.wait_ge(*done("ptexp_made"))
            nc.scalar.copy(PT_exp.rearrange("p a r -> p (a r)"), XB[3][:, :]).then_inc(sem("ptexp_taken"), 1)
            with act.Fori(0, 4) as i:
                k_even(i, 0)
            k_even(0, 128)
            for br, (s_br, n) in enumerate(((S_sel, 2048), (S_win, 512))):
                act.wait_ge(sem("sw_max"), br + 1)
                nc.scalar.activation(s_br, s_br, ACT.Exp, bias=mx_c[:, 1 + br:2 + br], accum_out=den_c[:, 1 + br:2 + br]).then_inc(sem("sw_exp"), 1)
                nc.scalar.activation(p_new[:, br:br + 1], s_new[:, br:br + 1], ACT.Exp, bias=mx_c[:, 1 + br:2 + br]).then_inc(sem("sw_exp"), 1)
            for q in range(5):
                act.wait_ge(sem("sw_pT"), q + 1)
                dst = PT_sel[:, 4 * q:4 * q + 4, :] if q < 4 else PT_win
                nc.scalar.copy(dst.rearrange("p a r -> p (a r)"), XB[q % 4][:, :]).then_inc(sem("sw_pT_taken"), 1)
            with act.Fori(0, 4) as i:
                for b2 in range(2):
                    act.wait_ge(sem("set_used"), i * 10 + (2 + 5 * b2 + 5))
                    nc.scalar.copy(O_c[:, b2, :], XB[b2][:, 0:P]).then_inc(sem("O_taken"), 1)

            with act.Fori(0, 2) as i:
                for j in range(8):
                    act.wait_ge(sem("proj_made"), i * 8 + (4 + 144 + j + 1))
                    nc.scalar.activation(proj[:, bass.ds(i * 8 + j, 1), :], PJ[j % 4][:, 0:T], ACT.Silu).then_inc(sem("proj_free"), 1)
            ple(1, ("cat1", 2))
            gate(1, 176)
            for c in range(KC):
                act.wait_ge(sem("y_made"), c + 1)
                nc.scalar.copy(y_nat[:, :, tileT(c)], XB[c % 4][:, 0:S].rearrange("p (t n) -> p t n", t=2)).then_inc(sem("y_taken"), 1)
                nc.scalar.copy(y_s[:, tileT(c)], XB[c % 4][0:B, S:S + P]).then_inc(sem("y_taken"), 1)

        @block.vector
        def _(dve):
            chain = [0]

            def link(ins):
                chain[0] += 1
                ins.then_inc(sem("dve_chain"), 1)
                dve.wait_ge(sem("dve_chain"), chain[0])

            def normalise(layer, h, xn, g):
                dve.wait_ge(sem(f"rms_root{layer}"), 1)
                link(nc.vector.reciprocal(scr[:, 1, :], scr[:, 0, :]))
                for c in range(KC):
                    nc.vector.scalar_tensor_tensor(xn[:, c, :], h[:, c, :], g[:, c:c + 1], scr[:, 1, :],
                                                   ALU.mult, ALU.mult).then_inc(sem(f"xn_ready{layer}"), 1)

            def compressed(rounds, first, c0):
                with dve.Fori(0, rounds) as i:
                    dve.wait_ge(sem("c_used"), i * 16 + (c0 + NP + 16))
                    nc.vector.tensor_copy(kcmp[:, bass.ds(i + first, 1)].rearrange("p o a d -> p (o a) d"),
                                          XB[0][:, :].rearrange("p (a d) -> p a d", a=4)).then_inc(sem("cmp_half"), 1)
                    nc.vector.tensor_copy(vcmp[:, bass.ds(i + first, 1)].rearrange("p o a d -> p (o a) d"),
                                          XB[1][:, :].rearrange("p (a d) -> p a d", a=4)).then_inc(sem("cmp_free"), 1)

            def rope(dst, src, tmp, swp, heads):
                cosb = cos.rearrange("p (o t) -> p o t", o=1).broadcast_to([32, heads, T])
                sinb = sin.rearrange("p (o t) -> p o t", o=1).broadcast_to([32, heads, T])
                link(nc.vector.stream_shuffle(swp, src, [(m + HALF) % 32 for m in range(32)]))
                link(nc.vector.tensor_tensor(swp, swp, sinb, ALU.mult))
                link(nc.vector.tensor_tensor(tmp, src, cosb, ALU.mult))
                link(nc.vector.tensor_tensor(dst, tmp, swp, ALU.add))

            dve.wait_ge(sem("gains_set"), 1)
            normalise(0, r0, r1, g_ab)
            compressed(5, 0, CMP_A)

            for grp in range(4):
                dve.wait_ge(sem("qn_root"), 8 * grp + 8)
                r8 = Z[:, 0:8 * T]
                x8 = proj[:, 8 * grp:8 * grp + 8, :].rearrange("p a t -> p (a t)")
                link(nc.vector.reciprocal(r8, r8))
                link(nc.vector.scalar_tensor_tensor(x8, x8, g_qa if grp < 3 else g_ka, r8, ALU.mult, ALU.mult))
                x32 = proj[0:32, 8 * grp:8 * grp + 8, :]
                rope(x32, x32, Z[0:32, 8 * T:16 * T].rearrange("p (a t) -> p a t", a=8),
                     Z[0:32, 16 * T:24 * T].rearrange("p (a t) -> p a t", a=8), 8)
                dve.sem_inc(sem("qn_done"), 1)

            def pa_scores(u):
                qt, nk = u % 2, P * (u % 2 + 1)
                dve.wait_ge(sem("pa_s"), u + 1)
                if u >= 2:
                    dve.wait_ge(sem("pa_pT"), u - 1)
                m = mask[:, AG * P * qt:AG * P * qt + AG * nk]
                if qt == 0:
                    link(nc.vector.scalar_tensor_tensor(S_sb[:, 0, 0:384], XB[0][:, 0:384], SCALE, m, ALU.mult, ALU.add))
                else:
                    link(nc.vector.scalar_tensor_tensor(S_sb[:, 1, 0:512], XB[1][:, :], SCALE, m[:, 0:512], ALU.mult, ALU.add))
                    link(nc.vector.scalar_tensor_tensor(S_sb[:, 1, 512:768], XB[2][:, 0:256], SCALE, m[:, 512:768], ALU.mult, ALU.add))
                nc.vector.tensor_reduce(nmx[:, qt:qt + 1], S_sb[:, qt, 0:AG * nk], AX, ALU.max, negate=True).then_inc(sem("pa_max"), 1)

            def pa_probs(u):
                qt, nk = u % 2, P * (u % 2 + 1)
                dve.wait_ge(sem("pa_exp"), u + 1)
                s0, s1, s2 = (S_sb[:, qt, g * nk:(g + 1) * nk] for g in range(AG))
                link(nc.vector.reciprocal(rden[:, qt:qt + 1], den[:, qt:qt + 1]))
                link(nc.vector.tensor_tensor(s0, s0, s1, ALU.add))
                link(nc.vector.tensor_tensor(s0, s0, s2, ALU.add))
                nc.vector.tensor_scalar(s0, s0, rden[:, qt:qt + 1], None, ALU.mult).then_inc(sem("pa_p"), 1)

            dve.wait_ge(sem("mask_a_in"), 16)
            pa_scores(0)
            for u in range(16):
                if u < 15:
                    pa_scores(u + 1)
                pa_probs(u)

            dve.wait_ge(sem("a_out"), 16 * 5)
            link(nc.vector.memset(Z[:, 0:1536], 0.0))
            for g in range(AG):
                for b in range(B):
                    ins = nc.vector.tensor_copy(qz[:, g, b, :, b], proj[:, 8 * g:8 * g + 8, S + b])
            link(ins)
            dve.sem_inc(sem("qz_set"), 1)
            for n in range(B * AG):
                dve.wait_ge(sem("dk_T"), n + 1)
                if n >= 2:
                    dve.wait_ge(sem("c_used"), AK + NP + n - 1)
                nc.vector.tensor_copy(KT[:, n % 2, 512:1024], XB[3][:, :]).then_inc(sem("dk_T_taken2"), 1)
            dve.wait_ge(sem("c_used"), AK + NP + B * AG)
            dve.wait_ge(sem("dk_T_taken"), B * AG)
            link(nc.vector.memset(Z[:, 1536:2560], 0.0))
            for g in range(AG):
                for u in range(2):
                    ins = nc.vector.tensor_tensor(prod[:, g, u, :].rearrange("p (j b) -> p j b", j=4)[:, :, 0:B],
                                                  proj[:, 8 * g + 4 * u:8 * g + 4 * u + 4, S:T],
                                                  proj[:, 24 + 4 * u:28 + 4 * u, S:T], ALU.mult)
            ins.then_inc(sem("d_prod"), 1)
            dve.wait_ge(sem("d_s"), 1)
            for u in range(2):
                link(nc.vector.tensor_scalar(Sd[:, u, 0:387], XB[u][:, 0:387], SCALE, None, ALU.mult))
            nc.vector.tensor_reduce(nmx[:, 0:2], Sd[:, :, 0:387], AX, ALU.max, negate=True).then_inc(sem("d_max"), 1)
            dve.wait_ge(sem("d_exp"), 2)
            link(nc.vector.reciprocal(rden[:, 0:2], den[:, 0:2]))
            for u in range(2):
                link(nc.vector.tensor_scalar(Sd[:, u, 0:387], Sd[:, u, 0:387], rden[:, u:u + 1], None, ALU.mult))
            link(nc.vector.tensor_reduce(pnew[:, 0:2], Sd[:, :, 384:387], AX, ALU.add))
            for u in range(2):
                link(nc.vector.tensor_scalar(diag[:, u, :], ident, pnew[:, u:u + 1], None, ALU.mult))
            dve.sem_inc(sem("d_p"), 1)
            dve.wait_ge(sem("d_new"), 1)
            link(nc.vector.tensor_tensor(vs_a.rearrange("p (u j b) -> p u j b", u=2, j=4),
                                         XB[1][:, 0:256].rearrange("p (u j b) -> p u j b", u=2, j=4)[:, :, :, 0:B],
                                         proj[:, 32:40, S:T].rearrange("p (u j) b -> p u j b", u=2), ALU.mult))
            dve.sem_inc(sem("d_new_taken"), 1)
            vs4 = vs_a.rearrange("p (u j b) -> p u j b", u=2, j=4)
            scr4 = scr[:, :, :].rearrange("p (u j) t -> p u j t", u=2)
            for b in range(B):
                dve.wait_ge(sem("dO_T"), b + 1)
                src = XB[2 + b % 2][:, 0:256].rearrange("p (u j b) -> p u j b", u=2, j=4)[:, :, :, b]
                nc.vector.tensor_tensor(scr4[:, :, :, S + b], src, vs4[:, :, :, b], ALU.add).then_inc(sem("oTd"), 1)

            compressed(3, 5, CMP_B)

            dve.wait_ge(sem("ln_sum"), 1)
            link(nc.vector.tensor_scalar(pnewT, XB[0][:, 0:T], 1.0 / 1024, None, ALU.mult))
            link(nc.vector.tensor_tensor(xc, xc, pnewT.rearrange("p (o t) -> p o t", o=1).broadcast_to([P, 8, T]), ALU.subtract))
            dve.sem_inc(sem("ln_centred"), 1)
            dve.wait_ge(sem("ln_root"), 1)
            link(nc.vector.reciprocal(lnr, pnewT))
            for g in range(8):
                ins = nc.vector.scalar_tensor_tensor(xc[:, g, :], xc[:, g, :], g_sgu[:, g:g + 1], lnr, ALU.mult, ALU.mult)
            link(ins)
            dve.sem_inc(sem("vn_ready"), 1)
            for n in range(2):
                dve.wait_ge(sem("ws_T"), n + 1)
                nc.vector.tensor_tensor(wsT[:, 4 * n:4 * n + 4, :], XB[2 + n][:, :].rearrange("p (g s) -> p g s", g=4),
                                        const[:, C_TRIL:C_TRIL + P].rearrange("p (o s) -> p o s", o=1).broadcast_to([P, 4, P]),
                                        ALU.mult).then_inc(sem("wsT_set"), 1)
            dve.wait_ge(sem("w00_made"), 1)
            link(nc.vector.tensor_copy(w00, XB[2][:, 0:8]))
            link(nc.vector.tensor_copy(b00, XB[2][:, 8:16]))
            dve.sem_inc(sem("w00_taken"), 1)
            for g in range(8):
                link(nc.vector.tensor_scalar(rden, xc[:, g, S:T], w00[:, g:g + 1], b00[:, g:g + 1], ALU.mult, ALU.add))
                link(nc.vector.tensor_tensor(proj[:, 48 + g, S:T], proj[:, 48 + g, S:T], rden, ALU.mult))
                dve.wait_ge(sem("mix_made"), g + 1)
                nc.vector.tensor_tensor(proj[:, 48 + g, 0:S], proj[:, 48 + g, 0:S], XB[g % 4][:, 0:S], ALU.mult)\
                  .then_inc(sem("mixed"), 1)
            dve.wait_ge(sem("silu"), 2)
            dve.wait_ge(sem("mixed"), 8)
            for n in range(2):
                a = slice(4 * n, 4 * n + 4)
                nc.vector.tensor_tensor(r1[:, 4 * n:4 * n + 4, :], scr[:, a, :], proj[:, 40 + 4 * n:44 + 4 * n, :], ALU.mult).then_inc(sem("cat0"), 1)
                nc.vector.tensor_tensor(r1[:, 8 + 4 * n:12 + 4 * n, :], proj[:, 48 + 4 * n:52 + 4 * n, :], proj[:, a, :], ALU.mult).then_inc(sem("cat0"), 1)

            def add_mix(h, done):
                with dve.Fori(0, 2) as i:
                    for j in range(8):
                        dve.wait_ge(sem("proj_made"), i * 8 + (4 + done + j + 1))
                        hj = h[:, bass.ds(i * 8 + j, 1), :]
                        nc.vector.tensor_tensor(hj, hj, PJ[j % 4][:, 0:T].rearrange("p (o t) -> p o t", o=1), ALU.add)\
                          .then_inc(sem("proj_free"), 1)

            def gated(layer, h, out, done):
                dve.sem_inc(sem(f"h_new{layer}"), 4)
                dve.wait_ge(sem(f"ple_taken{layer}"), KC)
                with dve.Fori(0, 2) as i:
                    for j in range(8):
                        dve.wait_ge(sem("proj_free"), i * 8 + (4 + done + j + 1))
                        sg = scr[:, j % 4, :].rearrange("p (o t) -> p o t", o=1)
                        tm = scr[:, 4 + j % 4, :].rearrange("p (o t) -> p o t", o=1)
                        nc.vector.tensor_tensor(tm, sg, proj[:, bass.ds(i * 8 + j, 1), :], ALU.mult).then_inc(sem(f"gp{layer}"), 1)
                        dve.wait_ge(sem(f"gp{layer}"), i * 8 + (j + 1))
                        nc.vector.tensor_tensor(out[:, bass.ds(i * 8 + j, 1), :], tm, h[:, bass.ds(i * 8 + j, 1), :], ALU.add)\
                          .then_inc(sem(f"h_new{layer}"), 1)
            add_mix(r0, 72)
            gated(0, r0, r1, 88)

            normalise(1, r1, r0, g_c)
            n = 0
            for grp, (first, size, g) in enumerate(((0, 8, g_qc), (8, 8, g_qc), (24, 4, g_kc[:, 1:2]), (32, 4, g_kc[:, 2:3]))):
                n += size
                dve.wait_ge(sem("cn_root"), n)
                r = F[:, 0:size * T]
                x = proj[:, first:first + size, :].rearrange("p a t -> p (a t)")
                link(nc.vector.reciprocal(r, r))
                link(nc.vector.scalar_tensor_tensor(x, x, g, r, ALU.mult, ALU.mult))
                src = proj[0:32, first:first + size, :]
                if grp < 2:
                    link(nc.vector.tensor_copy(proj[:, 40 + first:48 + first, :].rearrange("p a t -> p (a t)"), x))
                    dst = tmp = proj[0:32, 40 + first:48 + first, :]
                else:
                    dst, tmp = src, SC[0:32, 4 * T:8 * T].rearrange("p (a t) -> p a t", a=4)
                rope(dst, src, tmp, SC[0:32, 0:size * T].rearrange("p (a t) -> p a t", a=size), size)
                dve.sem_inc(sem("cn_done"), 1)

            def over(x, dims):
                return x.broadcast_to(dims)

            dve.wait_ge(sem("pc_root"), 1)
            link(nc.vector.reciprocal(krt[:, 0:1], krt[:, 0:1]))
            nc.vector.tensor_scalar(kcp, kcp, krt[:, 0:1], None, ALU.mult).then_inc(step("kcp_ready"), 1)
            dve.wait_ge(*done("kcpT_made"))
            nc.vector.tensor_scalar(kcpT, XB[1][:, 0:P], g_kc[:, 0:1], None, ALU.mult).then_inc(step("kcpT_set"), 1)
            for n in range(8):
                dve.wait_ge(sem("pcs_made"), n + 1)
                h = n % 4
                nc.vector.tensor_scalar(Pc[:, 4 * n:4 * n + 4, :],
                                        XB[n % 4][:, :].rearrange("p (g m) -> p g m", g=GQ)[:, :, 32 * h:32 * h + 16],
                                        SCALE, None, ALU.mult).then_inc(sem("pcs_taken"), 1)
            dve.wait_ge(sem("pcs_taken"), 8)
            Pq = Pc.rearrange("p (q h) n -> p q h n", q=2)
            vis = const[:, C_VIS:C_VIS + 32].rearrange("p (q o n) -> p q o n", q=2, o=1)
            see = const[:, C_SEE:C_SEE + 32].rearrange("p (q o n) -> p q o n", q=2, o=1)
            pmx = cmx[:, 0:32]
            link(nc.vector.tensor_tensor(Pq, Pq, over(vis, [P, 2, HQ, 16]), ALU.add))
            link(nc.vector.tensor_reduce(pmx, Pc, AX, ALU.max))
            pm3 = pmx.rearrange("p (u o) -> p u o", o=1)
            link(nc.vector.tensor_tensor(Pc, Pc, over(pm3, [P, 32, 16]), ALU.subtract))
            dve.sem_inc(step("pc_centred"), 1)
            dve.wait_ge(sem("pc_exp"), 1)
            link(nc.vector.tensor_tensor(Pq, Pq, over(see, [P, 2, HQ, 16]), ALU.mult))
            link(nc.vector.tensor_reduce(pmx, Pc, AX, ALU.add))
            link(nc.vector.tensor_scalar(pmx, pmx, TINY, None, ALU.max))
            link(nc.vector.reciprocal(pmx, pmx))
            dve.wait_ge(sem("gate_taken"), 3)
            link(nc.vector.tensor_tensor(pmx.rearrange("p (q h) -> p q h", q=2), pmx.rearrange("p (q h) -> p q h", q=2),
                                         gate_p[:, :, 0, :], ALU.mult))
            link(nc.vector.tensor_tensor(Pc, Pc, over(pm3, [P, 32, 16]), ALU.mult))
            dve.sem_inc(step("pc_p"), 1)
            dve.wait_ge(sem("c_out"), 16 * 18)
            dve.wait_ge(sem("mask_c_in"), 16)

            def cu_scores(u):
                qt, nk = u % 2, P * (u % 2 + 1)
                dve.wait_ge(sem("cu_s"), u + 1)
                if u >= 2:
                    dve.wait_ge(sem("cu_pT"), u - 1)
                m = mask[:, P * qt:P * qt + nk].rearrange("p (o n) -> p o n", o=1)
                s2 = S_c[:, qt, 0:2 * nk].rearrange("p (b n) -> p b n", b=2)
                link(nc.vector.scalar_tensor_tensor(s2, XB[qt][:, 0:2 * nk].rearrange("p (b n) -> p b n", b=2), SCALE,
                                                    over(m, [P, 2, nk]), ALU.mult, ALU.add))
                nc.vector.tensor_reduce(nmx[:, 2 * qt:2 * qt + 2], s2, AX, ALU.max, negate=True).then_inc(sem("cu_max"), 1)

            def cu_probs(u):
                hq, qt, nk = u // 2, u % 2, P * (u % 2 + 1)
                dve.wait_ge(sem("cu_exp"), 2 * u + 2)
                rd = rden[:, 2 * qt:2 * qt + 2]
                link(nc.vector.reciprocal(rd, den[:, 2 * qt:2 * qt + 2]))
                link(nc.vector.tensor_tensor(rd, rd, gate_p[:, qt, 1:3, hq], ALU.mult))
                s2 = S_c[:, qt, 0:2 * nk].rearrange("p (b n) -> p b n", b=2)
                nc.vector.tensor_tensor(s2, s2, over(rd.rearrange("p (b o) -> p b o", o=1), [P, 2, nk]), ALU.mult).then_inc(sem("cu_p"), 1)

            cu_scores(0)
            for u in range(32):
                if u < 31:
                    cu_scores(u + 1)
                cu_probs(u)

            dve.wait_ge(sem("cu_o_taken"), 32)
            link(nc.vector.memset(SC[:, 0:1024], 0.0))
            for b in range(B):
                ins = nc.vector.tensor_copy(qzu[:, b, :, 4 * b:4 * b + 4], proj[:, 0:16, S + b].rearrange("p (h g) -> p h g", h=CH))
            link(ins)
            link(nc.vector.memset(Q[:, 0:1024], 0.0))
            for b in range(B):
                ins = nc.vector.tensor_copy(qzr[:, b, :, 4 * b:4 * b + 4], proj[:, 40:56, S + b].rearrange("p (h g) -> p h g", h=CH))
            for br, slot in enumerate((24, 32)):
                for g in range(GQ):
                    q4 = proj[:, 40:56, S:T].rearrange("p (h g) b -> p g h b", h=CH)[:, g]
                    ins = nc.vector.tensor_tensor(diag_c[:, br, :].rearrange("p (h b g) -> p g h b", h=CH, b=B)[:, g], q4,
                                                  proj[:, slot:slot + 4, S:T], ALU.mult)
            link(ins)
            dve.sem_inc(step("qz_c"), 1)
            dve.wait_ge(sem("ks_root"), 1)
            link(nc.vector.reciprocal(krt, krt))
            k32 = kcmp[:, :, :, :].rearrange("p b a d -> p (b a) d")
            link(nc.vector.tensor_tensor(k32, k32, over(krt.rearrange("p (n o) -> p n o", o=1), [P, 32, P]), ALU.mult))
            dve.sem_inc(step("kc_ready"), 1)
            dve.wait_ge(*done("scmp_made"))
            link(nc.vector.tensor_scalar(S_cmp, XB[0][:, 0:P], SCALE, None, ALU.mult))
            link(nc.vector.tensor_scalar(s_new, XB[1][:, 0:2], SCALE, None, ALU.mult))
            nc.vector.tensor_reduce(mx_c[:, 0:1], S_cmp[:, 0:NCMP], AX, ALU.max, negate=True).then_inc(sem("sc_max"), 1)
            dve.wait_ge(sem("sc_exp"), 1)
            link(nc.vector.memset(S_cmp[:, NCMP:P], 0.0))
            link(nc.vector.tensor_scalar(rd_c[:, 0:1], den_c[:, 0:1], TINY, None, ALU.max))
            link(nc.vector.reciprocal(rd_c[:, 0:1], rd_c[:, 0:1]))
            link(nc.vector.tensor_scalar(S_cmp, S_cmp, rd_c[:, 0:1], None, ALU.mult))
            dve.sem_inc(step("scmp_p"), 1)
            dve.wait_ge(*done("imp_made"))
            link(nc.vector.tensor_copy(imp, XB[1][:, 0:NPICK]))
            imp_i = over(imp.rearrange("p (o i) -> p o i", o=1), [P, NPICK, NPICK])
            imp_j = over(imp.rearrange("p (j o) -> p j o", o=1), [P, NPICK, NPICK])
            link(nc.vector.tensor_tensor(gt, imp_i, imp_j, ALU.is_gt))
            link(nc.vector.tensor_tensor(eq, imp_i, imp_j, ALU.is_equal))
            link(nc.vector.tensor_tensor(eq, eq, mask[:, M_CAUSAL:].rearrange("p (j i) -> p j i", j=NPICK), ALU.mult))
            link(nc.vector.tensor_tensor(gt, gt, eq, ALU.add))
            link(nc.vector.tensor_reduce(rank, gt, AX, ALU.add))
            link(nc.vector.memset(sneg, 0.0))
            link(nc.vector.tensor_scalar(sneg[:, 1:1 + NPICK], rank, float(TOP), NEG, ALU.is_ge, ALU.mult))
            dve.wait_ge(sem("gate_s_in"), 16 * 12)
            link(nc.vector.tensor_scalar(S_cmp, S_cmp, gate_s[:, 0:1], None, ALU.mult))
            for h in range(CH):
                own = const[:, C_ROW + h:C_ROW + h + 1]
                ins = nc.vector.tensor_scalar(P_exp[:, :, h, :], S_cmp.rearrange("p (a i) -> p a i", a=4), own, None, ALU.mult)
            link(ins)
            dve.sem_inc(step("pexp_ready"), 1)

            def k_odd(c, base):
                for m in range(1, 32, 2):
                    dve.wait_ge(sem("kt_T"), c * 32 + (8 + base + m + 1))
                    dve.wait_ge(sem("kt_used"), c * 32 + (base + m + 1))
                    nc.vector.tensor_copy(KTc[:, m % 4, :], XB[1 + m % 2][:, :]).then_inc(sem("kt_odd"), 1)

            with dve.Fori(0, 4) as i:
                k_odd(i, 0)
                dve.wait_ge(sem("kt_used"), i * 32 + (4 + 32))
                nc.vector.tensor_tensor(S_sel.rearrange("p (c j n) -> p c j n", c=4, j=8)[:, bass.ds(i, 1)].rearrange("p o j n -> p (o j) n"),
                                        XB[0][:, :].rearrange("p (j n) -> p j n", j=8),
                                        over(sneg.rearrange("p (c j o) -> p c j o", c=4, o=1)[:, bass.ds(i, 1)].rearrange("p c j o -> p (c j) o"), [P, 8, SB_]),
                                        ALU.add).then_inc(sem("S_taken"), 1)
            k_odd(0, 128)
            dve.wait_ge(sem("kt_used"), 4 + 160)
            link(nc.vector.tensor_copy(S_win, XB[0][:, :]))
            for br, s_br in enumerate((S_sel, S_win)):
                if br == 0:
                    dve.wait_ge(sem("S_taken"), 5)
                link(nc.vector.tensor_scalar(s_br, s_br, SCALE, None, ALU.mult))
                link(nc.vector.tensor_reduce(mx_c[:, 1 + br:2 + br], s_br, AX, ALU.max))
                link(nc.vector.tensor_tensor(mx_c[:, 1 + br:2 + br], mx_c[:, 1 + br:2 + br], s_new[:, br:br + 1], ALU.max))
                link(nc.vector.tensor_scalar(mx_c[:, 1 + br:2 + br], mx_c[:, 1 + br:2 + br], -1.0, None, ALU.mult))
                dve.sem_inc(sem("sw_max"), 1)
            dve.wait_ge(sem("sw_exp"), 4)
            link(nc.vector.tensor_tensor(rd_c[:, 1:3], den_c[:, 1:3], p_new, ALU.add))
            link(nc.vector.reciprocal(rd_c[:, 1:3], rd_c[:, 1:3]))
            link(nc.vector.tensor_tensor(rd_c[:, 1:3], rd_c[:, 1:3], gate_s[:, 1:3], ALU.mult))
            link(nc.vector.tensor_tensor(p_new, p_new, rd_c[:, 1:3], ALU.mult))
            link(nc.vector.tensor_scalar(S_sel, S_sel, rd_c[:, 1:2], None, ALU.mult))
            link(nc.vector.tensor_scalar(S_win, S_win, rd_c[:, 2:3], None, ALU.mult))
            for br in range(2):
                link(nc.vector.tensor_scalar(diag_c[:, br, :], ident, p_new[:, br:br + 1], None, ALU.mult))
            dve.sem_inc(step("sw_p"), 1)
            dve.wait_ge(*done("vn_made"))
            for br, slot in enumerate((28, 36)):
                dst = vnew if br == 0 else diag_c[:, 0, :]
                for g in range(GQ):
                    ins = nc.vector.tensor_tensor(dst.rearrange("p (h b g) -> p g h b", h=CH, b=B)[:, g],
                                                  XB[2][:, tileT(br)].rearrange("p (h b g) -> p g h b", h=CH, b=B)[:, g],
                                                  proj[:, slot:slot + 4, S:T], ALU.mult)
                link(ins)
            link(nc.vector.tensor_tensor(vnew, vnew, diag_c[:, 0, :], ALU.add))
            dve.sem_inc(step("vnew_set"), 1)
            vn4 = vnew.rearrange("p (h b g) -> p b h g", h=CH, b=B)
            with dve.Fori(0, 4) as i:
                for b2 in range(2):
                    dve.wait_ge(sem("OT_made"), i * 2 + (b2 + 1))
                    src = XB[2 + b2][:, 0:P].rearrange("p (h b g) -> p b h g", h=CH, b=B)[:, bass.ds(i * 2 + b2, 1)].rearrange("p o h g -> p (o h) g")
                    new = vn4[:, bass.ds(i * 2 + b2, 1)].rearrange("p o h g -> p (o h) g")
                    dst = proj[:, 40:56, bass.ds(i * 2 + (b2 + S), 1)].rearrange("p (h g) o -> p h (g o)", h=CH)
                    nc.vector.tensor_tensor(dst, src, new, ALU.add).then_inc(sem("OT_taken"), 1)
            dve.wait_ge(sem("OT_taken"), 2 + B)
            dve.wait_ge(sem("proj_free"), 4 + 160)
            for n in range(2):
                a = slice(8 * n, 8 * n + 8)
                nc.vector.tensor_tensor(r0[:, a, :], proj[:, 40 + 8 * n:48 + 8 * n, :], proj[:, a, :], ALU.mult).then_inc(sem("cat1"), 1)
            add_mix(r1, 160)
            gated(1, r1, r0, 176)

        @block.tensor
        def _(pe):
            pe.wait_ge(sem("consts_in"), 16)
            pe.wait_ge(sem("gains_in"), 16 * 7)
            nc.tensor.transpose(XB[3][:, 0:NG], scr[0:NG, 7, 0:P], ident[0:NG, 0:NG]).then_inc(sem("xT_made"), 1)
            pe.wait_ge(sem("x_in"), 96)
            for c in range(KC + 2):
                src, k = (x_nat, c) if c < KC else (p_nat, c - KC)
                if c == 3:
                    pe.wait_ge(sem("gains_set"), 1)
                if c >= 4:
                    pe.wait_ge(sem("xT_taken"), c - 3)
                for t in range(3):
                    rows = P if t < 2 else B
                    ins = nc.tensor.transpose(XB[c % 4][:, t * P:t * P + rows], src[0:rows, t, tileT(k)], ident[0:rows, 0:rows])
                ins.then_inc(sem("xT_made"), 1)
            pe.wait_ge(sem("ones_set"), 2)
            pe.wait_ge(sem("xT_taken"), KC + 2)

            def rms(layer, sq):
                for c in range(KC):
                    pe.wait_ge(sem(f"rms_sq{layer}"), c + 1)
                    ins = nc.tensor.matmul(XB[0][:, 0:T], ones[:, :], sq[:, c, :], start=(c == 0), stop=(c == KC - 1))
                ins.then_inc(sem(f"rms_sum{layer}"), 1)

            rms(0, r1)

            def columns(x, bl, tiles, loads):
                for hf in range(2):
                    q = 2 * (bl % 2) + hf
                    pe.wait_ge(sem(f"w_in{q}"), loads * 16 + 16)
                    for c in range(2):
                        if hf == 0:
                            pe.wait_ge(sem("proj_free"), tiles + (c + 1))
                        for k in range(HB):
                            ins = nc.tensor.matmul(PJ[(2 * bl + c) % 4][:, 0:T], wring[:, q, k, tileT(c)],
                                                   x[:, hf * HB + k, :], start=(hf == 0 and k == 0),
                                                   stop=(hf == 1 and k == HB - 1))
                        if hf == 1:
                            ins.then_inc(sem("proj_made"), 1)
                    if hf == 0:
                        ins.then_inc(sem("w_used"), 1)

            def projection(x, first, rounds):
                with pe.Fori(0, rounds) as i:
                    for bl in range(4):
                        columns(x, bl, i * 8 + (2 * first + 2 * bl), i * 2 + (first // 2 + bl // 2))

            def compress(i, bl, free, loads):
                for n in range(4):
                    pg = 4 * bl + n
                    pe.wait_ge(sem(f"c_in{n}"), i * 64 + (16 * loads + 16 * (bl + 1)))
                    if pg == 0:
                        pe.wait_ge(sem("cmp_free"), i + free)
                    for v in range(2):
                        for lo, grp in ([(0, pg // 4 - 1)] if n == 0 and pg else []) + [(32 - 8 * (pg % 4), pg // 4)]:
                            for h in range(CH):
                                ins = nc.tensor.matmul(XB[v][32 * h:32 * h + 32, tileT(grp)], wide[:, v, lo:lo + 32, h],
                                                       cring[:, n, (v * CH + h) * P:(v * CH + h + 1) * P],
                                                       start=(pg == 0), stop=(pg == NPG - 1), skip_group_check=True)
                    ins.then_inc(sem("c_used"), 1)

            pe.wait_ge(sem("xn_ready0"), KC)
            pe.wait_ge(sem("wide_in"), 16 * 32)
            with pe.Fori(0, 5) as i:
                for bl in range(4):
                    columns(r1, bl, i * 8 + 2 * bl, i * 2 + bl // 2)
                    compress(i, bl, 1, 0)

            pe.wait_ge(sem("cmp_free"), 6)
            for grp in range(4):
                pe.wait_ge(sem("qn_sq"), grp + 1)
                for j in range(8):
                    if 8 * grp + j >= 4:
                        pe.wait_ge(sem("qn_root"), 8 * grp + j - 3)
                    nc.tensor.matmul(XB[j % 4][:, 0:T], ones[:, :], scr[:, j, :], start=True, stop=True)\
                      .then_inc(sem("qn_sum"), 1)
            pe.wait_ge(sem("qn_done"), 4)
            for t in range(16):
                if t >= 4:
                    pe.wait_ge(sem("nat_taken"), 2 * (t - 3))
                for c in range(3):
                    rows = P if c < 2 else B
                    ins = nc.tensor.transpose(XB[t % 4][0:rows, tileT(c)], proj[:, 24 + t, c * P:c * P + rows], ident)
                ins.then_inc(sem("nat_made"), 1)
            pe.wait_ge(sem("nat_taken"), 32)

            def pa_scores(u):
                h, qt = u // 2, u % 2
                if u >= 2:
                    pe.wait_ge(sem("pa_max"), u - 1)
                for g in range(AG):
                    nk = P * (qt + 1)
                    out = XB[0][:, g * P:(g + 1) * P] if qt == 0 else XB[1 + g // 2][:, (g % 2) * 256:(g % 2) * 256 + 256]
                    ins = nc.tensor.matmul(out, proj[:, 8 * g + h, tileT(qt)], proj[:, 24 + h, 0:nk], start=True, stop=True)
                ins.then_inc(sem("pa_s"), 1)

            pa_scores(0)
            for u in range(16):
                h, qt = u // 2, u % 2
                if u < 15:
                    pa_scores(u + 1)
                pe.wait_ge(sem("pa_p"), u + 1)
                if u >= 1:
                    pe.wait_ge(sem("pa_o_taken"), u)
                for k in range(qt + 1):
                    ins = nc.tensor.transpose(XB[3][:, tileT(k)], S_sb[:, qt, tileT(k)], ident)
                ins.then_inc(sem("pa_pT"), 1)
                pe.wait_ge(sem("pa_pT_taken"), u + 1)
                for k in range(qt + 1):
                    ins = nc.tensor.matmul(XB[3][:, 384:512], proj[:, 32 + h, tileT(k)], PT[:, qt, tileT(k)],
                                           start=(k == 0), stop=(k == qt))
                ins.then_inc(sem("pa_o"), 1)

            pe.wait_ge(sem("pa_o_taken"), 16)
            pe.wait_ge(sem("qz_set"), 1)
            for u in range(2):
                nc.tensor.matmul(XB[u][:, :], zrow[0:1, 0:P], zrow[0:1, :], start=True, stop=True)

            def dk_scores(n):
                b, g = n // AG, n % AG
                pe.wait_ge(sem("dk_T_taken"), n + 1)
                pe.wait_ge(sem("dk_T_taken2"), n + 1)
                for h in range(AH):
                    j = h % 4
                    ins = nc.tensor.matmul(XB[h // 4][32 * j:32 * j + B, tileT(g)], qz[:, g, b, h, :],
                                           KT[:, n % 2, tileT(h)], start=False, stop=True, skip_group_check=True)
                ins.then_inc(sem("c_used"), 1)

            for n in range(B * AG):
                pe.wait_ge(sem(f"c_in{n % NP}"), 16 * (20 + n // NP + 1))
                if n >= 1:
                    pe.wait_ge(sem("dk_T_taken"), n)
                    pe.wait_ge(sem("dk_T_taken2"), n)
                for h in range(AH):
                    ins = nc.tensor.transpose(XB[2 + h // 4][:, tileT(h % 4)], cring[:, n % NP, tileT(h)], ident)
                ins.then_inc(sem("dk_T"), 1)
                dk_scores(n)
            pe.wait_ge(sem("d_prod"), 1)
            for g in range(AG):
                for u in range(2):
                    ins = nc.tensor.matmul(XB[u][:, 384 + g:385 + g], prod[:, g, u, :], ones[:, 0:1],
                                           start=False, stop=True, skip_group_check=True)
            ins.then_inc(sem("d_s"), 1)
            pe.wait_ge(sem("d_p"), 1)
            for g in range(AG):
                for u in range(2):
                    ins = nc.tensor.transpose(XB[2 + g // 2][:, (g % 2) * 256 + u * P:(g % 2) * 256 + (u + 1) * P],
                                              Sd[:, u, tileT(g)], ident)
            ins.then_inc(sem("d_pT"), 1)
            for u in range(2):
                ins = nc.tensor.matmul(XB[1][:, tileT(u)], ones[:, :], diag[:, u, :], start=True, stop=True)
            ins.then_inc(sem("d_new"), 1)
            pe.wait_ge(sem("d_pT_taken"), 2)
            pe.wait_ge(sem("d_new_taken"), 1)

            def dO_T(b):
                pe.wait_ge(sem("dO_taken"), b + 1)
                if b >= 2:
                    pe.wait_ge(sem("oTd"), b - 1)
                for u in range(2):
                    ins = nc.tensor.transpose(XB[2 + b % 2][:, tileT(u)], Od[:, b % 2, tileT(u)], ident)
                ins.then_inc(sem("dO_T"), 1)

            for b in range(B):
                if b >= 2:
                    pe.wait_ge(sem("dO_taken"), b - 1)
                for g in range(AG):
                    n = AG * b + g
                    pe.wait_ge(sem(f"c_in{n % NP}"), 16 * (26 + n // NP + 1))
                    for h in range(AH):
                        u, j = h // 4, h % 4
                        ins = nc.tensor.matmul(XB[b % 2][32 * j:32 * j + 32, tileT(u)], PTd[:, g, u, 32 * j:32 * j + 32],
                                               cring[:, n % NP, tileT(h)], start=(g == 0 and u == 0), stop=(g == AG - 1),
                                               skip_group_check=True)
                    ins.then_inc(sem("c_used"), 1)
                if b >= 1:
                    dO_T(b - 1)
            dO_T(B - 1)

            pe.wait_ge(sem("dO_taken"), B)
            with pe.Fori(0, 3) as i:
                for bl in range(4):
                    columns(r1, bl, i * 8 + (40 + 2 * bl), i * 2 + (10 + bl // 2))
                    compress(i, bl, 6, 32)
            for bl in range(4):
                columns(r1, bl, 64 + 2 * bl, 16 + bl // 2)
            pe.wait_ge(sem("proj_free"), 4 + 64)
            pe.wait_ge(sem("cmp_free"), 9)
            for g in range(8):
                ins = nc.tensor.matmul(XB[0][:, 0:T], ones[:, :], xc[:, g, :], start=(g == 0), stop=(g == 7))
            ins.then_inc(sem("ln_sum"), 1)
            pe.wait_ge(sem("ws_in"), 32)
            for g in range(8):
                ins = nc.tensor.transpose(XB[2 + g // 4][:, tileT(g % 4)], ws_nat[:, g, :], ident)
                if g % 4 == 3:
                    ins.then_inc(sem("ws_T"), 1)
            pe.wait_ge(sem("ln_sq"), 1)
            for g in range(8):
                ins = nc.tensor.matmul(XB[1][:, 0:T], ones[:, :], sq8[:, g, :], start=(g == 0), stop=(g == 7))
            ins.then_inc(sem("ln_sum"), 1)
            pe.wait_ge(sem("wsT_set"), 2)
            nc.tensor.matmul(XB[2][:, 0:8], ones[0:1, :], wsT[0:1, :, 0], start=True, stop=True)
            nc.tensor.matmul(XB[2][:, 8:16], ones[0:1, :], bs.rearrange("p (g t) -> p g t", g=8)[:, :, 0],
                             start=True, stop=True).then_inc(sem("w00_made"), 1)
            pe.wait_ge(sem("vn_ready"), 1)
            for g in range(8):
                if g >= 2:
                    pe.wait_ge(sem("vn_taken"), 2 * (g - 1))
                for c in range(3):
                    rows = P if c < 2 else B
                    ins = nc.tensor.transpose(XB[g % 2][0:rows, tileT(c)], xc[:, g, c * P:c * P + rows], ident)
                ins.then_inc(sem("vn_T"), 1)
            pe.wait_ge(sem("vn_taken"), 16)
            pe.wait_ge(sem("w00_taken"), 1)
            for g in range(8):
                if g >= 4:
                    pe.wait_ge(sem("mixed"), g - 3)
                for c in range(2):
                    nc.tensor.matmul(XB[g % 4][:, tileT(c)], vn_nat[:, c, tileT(g)], wsT[:, g, :], start=True, stop=False)
                    ins = nc.tensor.matmul(XB[g % 4][:, tileT(c)], ones[0:1, :], bs[:, tileT(g)], start=False, stop=True)
                ins.then_inc(sem("mix_made"), 1)

            pe.wait_ge(sem("cat0"), 4)
            projection(r1, OUT0, 2)

            def ple(layer):
                pe.wait_ge(sem("wple_in"), 16 * (layer + 1))
                for c in range(KC):
                    if c >= 4:
                        pe.wait_ge(sem(f"ple_taken{layer}"), c - 3)
                    for k in range(2):
                        ins = nc.tensor.matmul(XB[c % 4][:, 0:T], wple[:, k, tileT(c)], pT[:, k, :], start=(k == 0), stop=(k == 1))
                    ins.then_inc(sem(f"ple_made{layer}"), 1)
            ple(0)
            pe.wait_ge(sem("proj_free"), 4 + 88)
            projection(r0, GATE0, 2)

            pe.wait_ge(sem("p_in"), 48)
            pe.wait_ge(sem("ple_taken0"), KC)
            for k in range(2):
                for c in range(3):
                    rows = P if c < 2 else B
                    ins = nc.tensor.transpose(XB[1 + k][:, c * P:c * P + rows], p_nat[0:rows, c, tileT(k)], ident[0:rows, 0:rows])
                ins.then_inc(sem("pT_made"), 1)
            rms(1, r0)
            pe.wait_ge(sem("pT_taken"), 2)
            pe.wait_ge(sem("xn_ready1"), KC)
            pe.wait_ge(sem("proj_free"), 4 + 104)
            projection(r0, CQ, 5)
            n = 0
            for grp, size in enumerate((8, 8, 4, 4)):
                pe.wait_ge(sem("cn_sq"), grp + 1)
                for j in range(size):
                    if n >= 4:
                        pe.wait_ge(sem("cn_root"), n - 3)
                    n += 1
                    nc.tensor.matmul(XB[j % 4][:, 0:T], ones[:, :], scr[:, j, :], start=True, stop=True).then_inc(sem("cn_sum"), 1)
            pe.wait_ge(sem("cn_done"), 4)
            for t in range(24):
                if t >= 4:
                    pe.wait_ge(sem("cnat_taken"), 2 * (t - 3))
                for c in range(3):
                    rows = P if c < 2 else B
                    ins = nc.tensor.transpose(XB[t % 4][0:rows, tileT(c)], proj[:, 16 + t, c * P:c * P + rows], ident)
                ins.then_inc(sem("cnat_made"), 1)
            pe.wait_ge(sem("cnat_taken"), 48)
            for pg in range(2):
                lo = 32 - 8 * pg
                for h in range(CH):
                    nc.tensor.matmul(XB[0][32 * h:32 * h + 32, 0:P], wide[:, 0, lo:lo + 32, h], proj[:, 16 + h, tileT(pg)],
                                     start=(pg == 0), stop=(pg == 1), skip_group_check=True)
                    ins = nc.tensor.matmul(XB[1][0:32, tileT(h)], wide[:, 1, lo:lo + 32, h], proj[:, 20 + h, tileT(pg)],
                                           start=(pg == 0 and h == 0), stop=(pg == 1), skip_group_check=True)
            ins.then_inc(step("pc_made"), 1)
            pe.wait_ge(sem("wg_in"), 16)
            for k in range(KC):
                ins = nc.tensor.matmul(XB[2][0:48, 0:T], wg[:, k, :], r0[:, k, :], start=(k == 0), stop=(k == KC - 1))
            ins.then_inc(step("gT_made"), 1)
            pe.wait_ge(sem("gT_set"), 1)
            for c in range(3):
                rows = P if c < 2 else B
                ins = nc.tensor.transpose(XB[3][0:rows, 64 * c:64 * c + 48], gT[:, c * P:c * P + rows], ident[0:48, 0:48])
            ins.then_inc(step("gate_made"), 1)
            pe.wait_ge(*done("kcp_ready"))
            pe.wait_ge(sem("vcp_set"), 1)
            nc.tensor.transpose(XB[1][:, 0:P], kcp, ident).then_inc(step("kcpT_made"), 1)
            pe.wait_ge(*done("kcpT_set"))
            pe.wait_ge(sem("gate_taken"), 3)
            for n in range(8):
                if n >= 4:
                    pe.wait_ge(sem("pcs_taken"), n - 3)
                for g in range(GQ):
                    ins = nc.tensor.matmul(XB[n % 4][:, tileT(g)], proj[:, 4 * (n % 4) + g, tileT(n // 4)], kcpT, start=True, stop=True)
                ins.then_inc(sem("pcs_made"), 1)
            pe.wait_ge(sem("pcs_taken"), 8)

            def cu_scores(u):
                hq, qt = u // 2, u % 2
                nk = P * (qt + 1)
                if u >= 2:
                    pe.wait_ge(sem("cu_max"), u - 1)
                for br, slot in enumerate((24, 32)):
                    ins = nc.tensor.matmul(XB[qt][:, br * nk:(br + 1) * nk], proj[:, 40 + hq, tileT(qt)],
                                           proj[:, slot + hq // GQ, 0:nk], start=True, stop=True)
                ins.then_inc(sem("cu_s"), 1)

            pe.wait_ge(*done("pc_p"))
            cu_scores(0)
            for u in range(32):
                hq, qt = u // 2, u % 2
                h, nk = hq // GQ, P * (qt + 1)
                if u < 31:
                    cu_scores(u + 1)
                pe.wait_ge(sem("cu_p"), u + 1)
                if u >= 1:
                    pe.wait_ge(sem("cu_o_taken"), u)
                nc.tensor.transpose(XB[3][0:16, 0:P], Pc[:, 16 * qt + hq, :], ident)
                for k in range(2 * (qt + 1)):
                    ins = nc.tensor.transpose(XB[2][:, tileT(k)], S_c[:, qt, tileT(k)], ident)
                ins.then_inc(sem("cu_pT"), 1)
                pe.wait_ge(sem("cu_pT_taken"), 2 * u + 2)
                nc.tensor.matmul(XB[3][:, P:2 * P], vcp[0:16, h, :], PcT[:, qt, :], start=True, stop=False)
                for k in range(2 * (qt + 1)):
                    br, kt = k // (qt + 1), k % (qt + 1)
                    ins = nc.tensor.matmul(XB[3][:, P:2 * P], proj[:, (28, 36)[br] + h, tileT(kt)], PT_c[:, qt, tileT(k)],
                                           start=False, stop=(k == 2 * qt + 1))
                ins.then_inc(sem("cu_o"), 1)

            pe.wait_ge(sem("cu_o_taken"), 32)
            pe.wait_ge(*done("kc_ready"))
            for b in range(B):
                if b >= 4:
                    pe.wait_ge(sem("kcT_taken"), b - 3)
                for a in range(4):
                    ins = nc.tensor.transpose(XB[b % 4][:, tileT(a)], kcmp[:, b, a, :], ident)
                ins.then_inc(sem("kcT_made"), 1)
            pe.wait_ge(sem("kcT_taken"), B)
            pe.wait_ge(*done("qz_c"))
            for b in range(B):
                for h in range(CH):
                    nc.tensor.matmul(XB[0][32 * h:32 * h + 32, 0:P].rearrange("p (a i) -> p a i", a=4), qzu[:, b, h, :],
                                     kcmp[:, b, :, 32 * h:32 * h + 32], start=(b == 0), stop=(b == B - 1), skip_group_check=True)
            for br in range(2):
                ins = nc.tensor.matmul(XB[1][:, br:br + 1], diag_c[:, br, :], ones[:, 0:1], start=True, stop=True)
            ins.then_inc(step("scmp_made"), 1)
            pe.wait_ge(*done("scmp_p"))
            nc.tensor.matmul(XB[0][:, 128:256], S_cmp, const[:, C_GRP:C_GRP + P], start=True, stop=True).then_inc(step("psum_made"), 1)
            pe.wait_ge(sem("psum_taken"), 1)
            nc.tensor.matmul(XB[1][:, 0:NPICK], P_sum[0:NCMP, :], const[0:NCMP, C_C2S:C_C2S + NPICK], start=True, stop=True)\
              .then_inc(step("imp_made"), 1)
            pe.wait_ge(*done("pexp_ready"))
            for a in range(4):
                ins = nc.tensor.transpose(XB[3][:, tileT(a)], P_exp[:, a].rearrange("p h i -> p (h i)"), ident)
            ins.then_inc(step("ptexp_made"), 1)

            def keys(c, base, n0):
                def scores(m):
                    b, h = m // CH, m % CH
                    pe.wait_ge(sem("kt_odd" if m % 2 else "kt_even"), c * 16 + (base // 2 + m // 2 + 1))
                    nc.tensor.matmul(XB[0][32 * h:32 * h + 32, :], qzr[:, b, h, :], KTc[:, h, :],
                                     start=(b == 0), stop=(b == B - 1), skip_group_check=True).then_inc(sem("kt_used"), 1)
                for m in range(32):
                    b, h = m // CH, m % CH
                    if h == 0:
                        pe.wait_ge(sem(f"set_in{b % 2}"), c * 256 + (n0 // 2 * 64 + 64 * (b // 2 + 1)))
                    if m >= 2:
                        pe.wait_ge(sem("kt_odd" if m % 2 else "kt_even"), c * 16 + (base // 2 + m // 2))
                    for q in range(4):
                        ins = nc.tensor.transpose(XB[1 + m % 2][:, tileT(q)], hring[:, 4 * (b % 2) + q, tileT(h)], ident)
                    ins.then_inc(sem("kt_T"), 1)
                    if m >= 1:
                        scores(m - 1)
                scores(31)

            pe.wait_ge(sem("ptexp_taken"), 1)
            with pe.Fori(0, 4) as i:
                pe.wait_ge(sem("S_taken"), i + 1)
                keys(i, 0, 0)
            pe.wait_ge(sem("S_taken"), 5)
            keys(0, 128, 32)
            pe.wait_ge(*done("sw_p"))
            for q in range(5):
                if q == 4:
                    pe.wait_ge(sem("sw_pT_taken"), 1)
                for a in range(4):
                    src = S_sel[:, tileT(4 * q + a)] if q < 4 else S_win[:, tileT(a)]
                    ins = nc.tensor.transpose(XB[q % 4][:, tileT(a)], src, ident)
                ins.then_inc(sem("sw_pT"), 1)
            pe.wait_ge(sem("sw_pT_taken"), 5)
            for br in range(2):
                ins = nc.tensor.matmul(XB[2][:, tileT(br)], ones[:, :], diag_c[:, br, :], start=True, stop=True)
            ins.then_inc(step("vn_made"), 1)
            pe.wait_ge(*done("vnew_set"))
            with pe.Fori(0, 4) as i:
                for b2 in range(2):
                    for a in range(4):
                        nc.tensor.matmul(XB[b2][:, 0:P], PT_exp[:, a, :], vcmp[:, bass.ds(i * 2 + b2, 1), a, :].rearrange("p o d -> p (o d)"),
                                         start=(a == 0), stop=False, skip_group_check=True)
                    for k in range(5):
                        n = 5 * b2 + k
                        pe.wait_ge(sem(f"set_in{n % 2}"), i * 320 + (20 * 64 + 64 * (n // 2 + 1)))
                        for q in range(4):
                            lhs = PT_sel[:, 4 * k + q, :] if k < 4 else PT_win[:, q, :]
                            for h in range(CH):
                                ins = nc.tensor.matmul(XB[b2][32 * h:32 * h + 32, 0:P], lhs[:, 32 * h:32 * h + 32],
                                                       hring[:, 4 * (n % 2) + q, tileT(h)], start=False,
                                                       stop=(k == 4 and q == 3), skip_group_check=True)
                        ins.then_inc(sem("set_used"), 1)
                    pe.wait_ge(sem("O_taken"), i * 2 + (b2 + 1))
                    pe.wait_ge(sem("OT_taken"), i * 2 + (b2 + 1))
                    nc.tensor.transpose(XB[2 + b2][:, 0:P], O_c[:, b2, :], ident).then_inc(sem("OT_made"), 1)

            pe.wait_ge(sem("OT_taken"), 2 + B)
            projection(r0, CZ, 2)
            pe.wait_ge(sem("cat1"), 2)
            projection(r0, OUT1, 2)
            ple(1)
            pe.wait_ge(sem("proj_free"), 4 + 176)
            projection(r1, GATE1, 2)
            for c in range(KC):
                if c >= 4:
                    pe.wait_ge(sem("y_taken"), 2 * (c - 3))
                if c == 0:
                    pe.wait_ge(sem("ple_taken1"), KC)
                pe.wait_ge(sem("h_new1"), 4 + c + 1)
                for a in range(3):
                    rows = P if a < 2 else B
                    ins = nc.tensor.transpose(XB[c % 4][0:rows, tileT(a)], r0[:, c, a * P:a * P + rows], ident)
                ins.then_inc(sem("y_made"), 1)


_OUTS = [("y_prompt", (1, S, D)), ("y_sample", (B, 1, D)),
         ("new_a_kv_prompt", (1, 1, 2, S, AH, P)), ("new_a_kv_sample", (B, 1, 2, 1, AH, P)),
         ("state_b_v_prompt", (1, 1, P, D // 2)), ("state_b_v_sample", (B, 1, 1, D // 2)),
         ("new_c_cmp_kv_prompt", (1, 1, 2, S, CH, P)), ("new_c_cmp_kv_sample", (B, 1, 2, 1, CH, P)),
         ("new_c_sel_kv_prompt", (1, 1, 2, S, CH, P)), ("new_c_sel_kv_sample", (B, 1, 2, 1, CH, P)),
         ("new_c_win_kv_prompt", (1, 1, 2, S, CH, P)), ("new_c_win_kv_sample", (B, 1, 2, 1, CH, P))]


def kernel(**inputs):
    import numpy as _np
    import concourse.bacc as _bacc
    from concourse import mybir as _mybir
    from concourse.bass_utils import run_bass_kernel_spmd as _run

    nc = _bacc.Bacc("TRN2", target_bir_lowering=False, num_devices=1)
    arrays, dram = {}, {}
    const, mask_a, mask_c = shape_constants()
    given = dict(inputs, const=const, mask_a=mask_a, mask_c=mask_c)
    for name, a in given.items():
        a = _np.ascontiguousarray(a)
        arrays[f"in_{name}_dram"] = a
        dram[name] = nc.dram_tensor(f"in_{name}_dram", a.shape, _mybir.dt.from_np(a.dtype), kind="ExternalInput").ap()
    for name, shape in _OUTS:
        dram[name] = nc.dram_tensor(f"out_{name}_dram", shape, _mybir.dt.float32, kind="ExternalOutput").ap()
    hybrid_trunk(nc, dram)
    r = _run(nc, [arrays], core_ids=[0])
    return tuple(r.results[0][f"out_{name}_dram"] for name, _ in _OUTS)
```

```python
from contextlib import ExitStack

import numpy as np

import concourse.bass as bass
from concourse import mybir

ALU = mybir.AluOpType
ACT = mybir.ActivationFunctionType
F32 = mybir.dt.float32
I32 = mybir.dt.int32
AX = mybir.AxisListType.X

P = 128
D = 2048
KC = D // P
S = 256
B = 8
T = S + B
PAST = 2048
NPG = PAST // P
AH = 8
PATTERNS = ((128, 1), (512, 4), (2048, 16))
AG = len(PATTERNS)
CH = 4
GQ = 4
HQ = CH * GQ
CKV = CH * P
CMP, SEG = 32, 16
NCMP = PAST // SEG - 1
NCP = S // SEG - 1
SB_ = 64
NSEL = PAST // SB_
NPICK = NSEL - 2
TOP = 16 - 3
WIN = 512
WT = WIN // P
PLE = 256
EPS = 1e-6
SCALE = float(P) ** -0.5
NEG = -1e30
TINY = 1e-30
HALF = 16
CB = 256
HB = KC // 2
NW = 4
NP = 4

C_ID = 0
C_GRP = C_ID + P
C_TRIL = C_GRP + P
C_COS = C_TRIL + P
C_SIN = C_COS + T
C_VIS = C_SIN + T
C_SEE = C_VIS + 32
C_C2S = C_SEE + 32
C_ROW = C_C2S + NPICK
C_END = C_ROW + CH
M_A = AG * 3 * P
M_CAUSAL = 3 * P
M_C = M_CAUSAL + NPICK * NPICK


def shape_constants():
    c = np.zeros((P, C_END), np.float32)
    i = np.arange(P)
    c[:, C_ID:C_ID + P] = np.eye(P)
    c[:, C_GRP:C_GRP + P] = (i[:, None] // GQ) == (i[None, :] // GQ)
    c[:, C_TRIL:C_TRIL + P] = i[:, None] <= i[None, :]
    pos = np.concatenate([np.arange(S), np.full(B, PAST)]).astype(np.float32)
    inv = np.exp((-np.log(np.float32(500000.0)) * np.arange(HALF, dtype=np.float32) / np.float32(HALF)).astype(np.float32)).astype(np.float32)
    ang = (pos[None, :] * inv[:, None]).astype(np.float32)
    cos, sin = np.cos(ang.astype(np.float64)), np.sin(ang.astype(np.float64))
    c[0:HALF, C_COS:C_COS + T] = cos
    c[HALF:2 * HALF, C_COS:C_COS + T] = cos
    c[0:HALF, C_SIN:C_SIN + T] = -sin
    c[HALF:2 * HALF, C_SIN:C_SIN + T] = sin
    for qt in range(2):
        see = (np.arange(16)[None, :] * SEG + CMP - 1 <= (qt * P + i)[:, None]) & (np.arange(16)[None, :] < NCP)
        c[:, C_VIS + 16 * qt:C_VIS + 16 * qt + 16] = np.where(see, 0.0, NEG)
        c[:, C_SEE + 16 * qt:C_SEE + 16 * qt + 16] = see
    n = np.arange(NCMP)[:, None]
    j = np.arange(1, NPICK + 1)[None, :]
    shared = np.minimum(n * SEG + CMP, (j + 1) * SB_) - np.maximum(n * SEG, j * SB_)
    c[:NCMP, C_C2S:C_ROW] = np.maximum(shared, 0) / CMP
    c[:, C_ROW:C_END] = (i[:, None] // 32) == np.arange(CH)[None, :]
    a = np.full((P, M_A), NEG, np.float32)
    m = np.zeros((P, M_C), np.float32)
    for qt in range(2):
        nk = P * (qt + 1)
        q, k = (qt * P + i)[:, None], np.arange(nk)[None, :]
        off = AG * P * qt
        for g, (window, dil) in enumerate(PATTERNS):
            ok = (k <= q) & (q - k <= window) & ((q - k) % dil == 0)
            a[:, off + g * nk:off + (g + 1) * nk] = np.where(ok, 0.0, NEG)
        m[:, P * qt:P * qt + nk] = np.where(k <= q, 0.0, NEG)
    e = np.arange(NPICK)
    m[:, M_CAUSAL:] = (e[None, None, :] < e[None, :, None]).reshape(1, -1)
    return c, a, m


def hybrid_trunk(nc, A):
    with ExitStack() as ctx:
        def sb(name, shape, dt=F32):
            return ctx.enter_context(nc.sbuf_tensor(name, shape, dt))

        def bank(name):
            return ctx.enter_context(nc.psum_tensor(name, [P, 512], F32))

        made = {}

        def sem(name):
            if name not in made:
                made[name] = ctx.enter_context(nc.semaphore(name))
            return made[name]

        PE_STEPS = ("pc_made", "gT_made", "gate_made", "kcpT_made", "scmp_made", "psum_made", "imp_made", "ptexp_made", "vn_made")
        DVE_STEPS = ("kc_ready", "kcp_ready", "kcpT_set", "pc_centred", "qz_c", "pc_p", "scmp_p", "pexp_ready", "sw_p", "vnew_set")

        def step(name):
            return sem("pe_steps" if name in PE_STEPS else "dve_steps")

        def done(name):
            steps = PE_STEPS if name in PE_STEPS else DVE_STEPS
            return step(name), steps.index(name) + 1

        const = sb("const", [P, C_END])
        mask = sb("mask", [P, M_C])
        ones = sb("ones", [P, P])
        zrow = sb("zrow", [1, 512])
        r0 = sb("r0", [P, KC, T])
        r1 = sb("r1", [P, KC, T])
        wring = sb("wring", [P, NW, HB, CB])
        proj = sb("proj", [P, 64, T])
        kcmp = sb("kcmp", [P, B, 4, P])
        vcmp = sb("vcmp", [P, B, 4, P])
        cring = sb("cring", [P, NP, 2 * CKV])
        scr = sb("scr", [P, 8, T])
        pT = sb("pT", [P, 2, T])
        small = sb("small", [P, 384])
        wide = sb("wide", [P, 2, 64, CH])
        ptab = sb("ptab", [1, B * NPG], I32)
        PJ = [bank(f"PJ{i}") for i in range(4)]
        XB = [bank(f"XB{i}") for i in range(4)]
        ident = const[:, C_ID:C_ID + P]
        cos, sin = const[0:32, C_COS:C_COS + T], const[0:32, C_SIN:C_SIN + T]

        at = [0]

        def cols(n):
            a = at[0]
            at[0] += n
            assert at[0] <= 384
            return small[:, a:a + n]
        NG = 2 * KC + 8 + 6
        gains = cols(NG)
        g_ab, g_c, g_sgu = gains[:, 0:KC], gains[:, KC:2 * KC], gains[:, 2 * KC:2 * KC + 8]
        g_qa, g_ka, g_qc = (gains[:, 2 * KC + 8 + n:2 * KC + 9 + n] for n in range(3))
        g_kc = gains[:, 2 * KC + 11:NG]
        eps = cols(1)
        nmx, den = cols(8), cols(8)
        rden, pnew = cols(8), cols(8)
        w00, b00 = cols(8), cols(8)
        lnt = sb("lnt", [P, 2, T])
        pnewT, lnr = lnt[:, 0, :], lnt[:, 1, :]
        vs_a = cols(AH * B)

        Z = proj[:, 40:64, :].rearrange("p a t -> p (a t)")
        x_nat = Z[:, 0:3 * D].rearrange("p (a n) -> p a n", a=3)
        p_nat = proj[:, 36:39, :].rearrange("p a t -> p (a t)")[:, 0:3 * PLE].rearrange("p (a n) -> p a n", a=3)

        w_ab = A["w_in_ab"][0].rearrange("(k p) n -> p k n", p=P)
        cmp_pool = A["cache_c_cmp_kv"].rearrange("n l v r h d -> n r (l v) (h d)")
        n_phys = A["cache_c_cmp_kv"].shape[0]

        AB1, AB2, OUT0, GATE0 = 0, 20, 36, 44
        CQ, CZ, OUT1, GATE1 = 52, 72, 80, 88
        CMP_A, AK, AV, CMP_B = 0, 80, 104, 128

        k_nat = proj[:, 48:56, :].rearrange("p a t -> p (a t)")[:, 0:2048].rearrange("p (t n) -> p t n", t=2)
        s_nat = proj[0:B, 56:64, :].rearrange("p a t -> p (a t)")[:, 0:2048].rearrange("p (v n) -> p v n", v=2)
        spare_k = kcmp[:, 5:8].rearrange("p b a r -> p (b a r)")
        spare_v = vcmp[:, 5:8].rearrange("p b a r -> p (b a r)")
        S_sb = spare_k.rearrange("p (u n) -> p u n", u=2)
        PT = spare_v[:, 0:512].rearrange("p (u n) -> p u n", u=2)
        qz = spare_k.rearrange("p (g b h m) -> p g b h m", g=AG, b=B, h=AH)
        prod = spare_v[:, 0:768].rearrange("p (g u r) -> p g u r", g=AG, u=2)
        diag = spare_v[:, 768:1024].rearrange("p (u r) -> p u r", u=2)
        W = proj[:, 8:32, :].rearrange("p a t -> p (a t)")
        KT = W[:, 0:2048].rearrange("p (u n) -> p u n", u=2)
        Sd = W[:, 2048:2832].rearrange("p (u n) -> p u n", u=2)
        PTd = W[:, 2832:3600].rearrange("p (g u r) -> p g u r", g=AG, u=2)
        Od = W[:, 3600:4112].rearrange("p (u n) -> p u n", u=2)

        SLOTS = 8
        PA_AT = 8
        DK_AT = PA_AT + 3 * 16 + 1
        DS_AT = DK_AT + AG * B + 1
        DP_AT = DS_AT + 4
        DV_AT = DP_AT + 2
        LN_AT = DV_AT + AG * B + 1
        VN_AT = LN_AT + 9

        xc = proj[:, 56:64, :]
        sq8 = proj[:, 8:16, :]
        vn_nat = sq8.rearrange("p a t -> p (a t)")[:, 0:2048].rearrange("p (t n) -> p t n", t=2)
        vn_s = proj[0:B, 16:20, :].rearrange("p a t -> p (a t)")[:, 0:1024]
        ws_nat = proj[:, 24:28, :].rearrange("p a t -> p (a t)")[:, 0:1024].rearrange("p (g s) -> p g s", g=8)
        wsT = proj[:, 20:24, :].rearrange("p a t -> p (a t)")[:, 0:1024].rearrange("p (g s) -> p g s", g=8)
        bs = proj[0:1, 28:32, :].rearrange("p a t -> p (a t)")[:, 0:1024]
        wple = proj[:, 16:32, :].rearrange("p a t -> p (a t)")[:, 0:4096].rearrange("p (k n) -> p k n", k=2)

        F = proj[:, 56:64, :].rearrange("p a t -> p (a t)")
        SC = scr[:, :, :].rearrange("p a t -> p (a t)")
        Q = proj[:, 0:16, :].rearrange("p a t -> p (a t)")
        KV = proj[:, 16:24, :].rearrange("p a t -> p (a t)")
        kst = F[:, 0:2048].rearrange("p (a t n) -> p a t n", a=2, t=2)
        c_nat = cring[0:B, 0:3, :].rearrange("p a (v n) -> p (a v) n", v=2)
        PAIRS = [2 * n for n in range(8)] + [24, 26, 32, 34]
        NAT = [v * CH + h for v in (0, 1, 3, 2, 5, 4) for h in range(CH)]
        wg = cring[:, 3, 0:16 * 48].rearrange("p (k n) -> p k n", k=16)
        gT = lnt[0:48, 0, :]
        gate_p = lnt[:, 1, 0:96].rearrange("p (t j h) -> p t j h", t=2, j=3)
        gate_8 = lnt[0:B, 1, 96:144]
        gate_s = lnt[:, 1, 144:147]
        kcp = SC[:, 0:128]
        kcpT = SC[:, 128:256]
        vcp = SC[0:32, 256:768].rearrange("p (h d) -> p h d", h=CH)
        Pc = SC[:, 768:1280].rearrange("p (u n) -> p u n", n=16)
        PcT = SC[0:16, 1280:1536].rearrange("p (u n) -> p u n", u=2)
        S_c = F[:, 0:1024].rearrange("p (u n) -> p u n", u=2)
        PT_c = F[:, 1024:2048].rearrange("p (u n) -> p u n", u=2)
        spare = wring[:, 2].rearrange("p k n -> p (k n)")
        qzu = spare[:, 0:1024].rearrange("p (b h m) -> p b h m", b=B, h=CH)
        qzr = Q[:, 0:1024].rearrange("p (b h m) -> p b h m", b=B, h=CH)
        S_sel = KV[:, 0:2048]
        KTc = wring[:, 3].rearrange("p k n -> p (k n)").rearrange("p (h n) -> p h n", h=CH)
        PT_sel = SC[:, 0:2048].rearrange("p (g r) -> p g r", g=NPG)
        S_win = Q[:, 1024:1536]
        S_cmp = Q[:, 1536:1664]
        P_sum = Q[:, 1664:1792]
        imp = Q[:, 1792:1792 + NPICK]
        rank = Q[:, 1824:1824 + NPICK]
        sneg = Q[:, 1856:1888]
        gt = Q[:, 1888:2788].rearrange("p (j i) -> p j i", j=NPICK)
        eq = Q[:, 2788:3688].rearrange("p (j i) -> p j i", j=NPICK)
        P_exp = Q[:, 1888:2400].rearrange("p (a h i) -> p a h i", a=4, h=CH)
        PT_exp = mask[:, M_CAUSAL:M_CAUSAL + 512].rearrange("p (a r) -> p a r", a=4)
        diag_c = Q[:, 3688:3944].rearrange("p (u r) -> p u r", u=2)
        O_c = KV[:, 0:256].rearrange("p (u d) -> p u d", u=2)
        PT_win = KV[:, 256:768].rearrange("p (a r) -> p a r", a=4)
        vnew = KV[:, 768:896]

        K_STEPS, K_FROM = 5 * 32, 3

        def k_steps(u):
            lo, hi = ((u + n - K_FROM) * K_STEPS // (32 - K_FROM) for n in range(2))
            return (range(lo, lo + 3), range(lo + 3, hi)) if u >= K_FROM else ((), ())

        s_new = cols(2)
        p_new = cols(2)
        mx_c, den_c, rd_c = cols(3), cols(3), cols(3)
        cmx = cols(32)
        kss, krt = cols(32), cols(32)
        y_nat = proj[:, 32:48, :].rearrange("p a t -> p (a t)")[:, 0:4096].rearrange("p (t n) -> p t n", t=2)
        y_s = proj[0:B, 48:56, :].rearrange("p a t -> p (a t)")[:, 0:2048]
        hring = cring[:, :, :].rearrange("p a (s n) -> p (a s) n", s=2)

        def tileT(c):
            return slice(c * P, (c + 1) * P)

        block = ctx.enter_context(nc.Block())

        @block.sync
        def _(sp):
            sp.dma_start(const[:, :], A["const"]).then_inc(sem("consts_in"), 16)
            r = 0
            for src in (A["ln_ab"][0], A["ln_c"][0], A["ln_sgu"][0], A["qn_a"][0], A["kn_a"][0], A["qn_c"][0],
                        A["kn_c"].rearrange("l k d -> (l k d)")):
                n = src.shape[0] // P
                sp.dma_start(scr[r:r + n, 7, 0:P], src.rearrange("(c p) -> c p", p=P)).then_inc(sem("gains_in"), 16)
                r += n
            for t in range(2):
                sp.dma_start(x_nat[:, t, :], A["x_prompt"][0, tileT(t), :]).then_inc(sem("x_in"), 16)
                sp.dma_start(p_nat[:, t, :], A["p_prompt"][0, 0, tileT(t), :]).then_inc(sem("x_in"), 16)
            sp.dma_start(x_nat[0:B, 2, :], A["x_sample"].rearrange("b s d -> b (s d)")).then_inc(sem("x_in"), 16)
            sp.dma_start(p_nat[0:B, 2, :], A["p_sample"][0].rearrange("b s d -> b (s d)")).then_inc(sem("x_in"), 16)
            sp.dma_start(ptab[:, :], A["page_table"].rearrange("(o b) n -> o (b n)", o=1)).then_inc(sem("ptab_in"), 16)
            sp.dma_start(mask[:, 0:M_A], A["mask_a"]).then_inc(sem("mask_a_in"), 16)
            sp.wait_ge(sem("wide_zero"), 1)
            for v, w in enumerate((A["cw_k"], A["cw_v"])):
                for n in range(8):
                    for half in range(2):
                        sp.dma_start(wide[SEG * n:SEG * (n + 1), v, 32 + n - half, :], w[0, SEG * half:SEG * (half + 1), :])\
                          .then_inc(sem("wide_in"), 16)
            sp.wait_ge(sem("ptab_in"), 16)

            def weights(n, w, i, bl, per=4):
                for hf in range(2):
                    q = 2 * (bl % 2) + hf
                    if hf == 0:
                        sp.wait_ge(sem("w_used"), n + 1)
                    else:
                        sp.wait_ge(sem("proj_made"), n * 2 + 2)
                    sp.dma_start(wring[:, q], w[:, hf * HB:(hf + 1) * HB, bass.ds((i * per + bl) * CB, CB)])\
                      .then_inc(sem(f"w_in{q}"), 16)

            def pages(i, n0, bl, pool):
                for n in range(4):
                    pg = 4 * bl + n
                    sp.wait_ge(sem("c_used"), i * 16 + (4 * bl + n + 1 + (16 * n0 if n0 == 0 else CMP_B)))
                    page = sp.value_load(ptab[0:1, bass.ds(i * NPG + (n0 * NPG + pg), 1)], min_val=0, max_val=n_phys - 1)
                    sp.dma_start(cring[:, n, :].rearrange("p (v c) -> p v c", v=2), pool[bass.ds(page, 1)])\
                      .then_inc(sem(f"c_in{n}"), 16)

            with sp.Fori(0, 5) as i:
                for bl in range(4):
                    weights(i * 4 + bl, w_ab, i, bl)
                    pages(i, 0, bl, cmp_pool)

            def cache_a(n):
                kv, b, g = n // (AG * B), n // AG % B, n % AG
                window, dil = PATTERNS[g]
                sp.wait_ge(sem("c_used"), AK + n + 1)
                sp.dma_start(cring[:, n % NP, :], A["cache_a_kv"][b, 0, kv, PAST - window:PAST:dil].rearrange("r h d -> r (h d)"))\
                  .then_inc(sem(f"c_in{n % NP}"), 16)

            def ready_at(n):
                n -= NP
                return DK_AT + 1 + n if n < AG * B else DV_AT + n - AG * B

            for m in range(16):
                weights(AB2 + m, w_ab, 5 + m // 4, m % 4)
                if m == 1:
                    for n in range(NP):
                        cache_a(n)
                if m == 2:
                    sp.wait_ge(sem("nat_taken"), 32)
                    for t in range(2):
                        sp.dma_start(A["new_a_kv_prompt"][0, 0, 0, tileT(t)].rearrange("p h d -> p (h d)"), k_nat[:, t, :])\
                          .then_inc(sem("a_out"), 16)
                        sp.dma_start(A["new_a_kv_prompt"][0, 0, 1, tileT(t)], proj[:, 32:40, tileT(t)]).then_inc(sem("a_out"), 16)
                    sp.dma_start(A["new_a_kv_sample"].rearrange("b l v s h d -> (b l) v (s h d)"), s_nat).then_inc(sem("a_out"), 16)
                if m == 9:
                    sp.wait_ge(sem("qz_set"), 1)
                    sp.dma_start(ws_nat, A["ws_b"][0].rearrange("g t s -> t g s")).then_inc(sem("ws_in"), 16)
                    sp.dma_start(bs, A["bs_b"].rearrange("l g t -> l (g t)")).then_inc(sem("ws_in"), 16)
                for n in range(NP, 2 * AG * B):
                    if ready_at(n) // SLOTS == m - 1:
                        cache_a(n)

            w_o = A["w_out_ab"][0].rearrange("(k p) n -> p k n", p=P)
            with sp.Fori(0, 2) as i:
                for bl in range(4):
                    weights(i * 4 + (OUT0 + bl), w_o, i, bl)
                    pages(i, 5, bl, cmp_pool)
            sp.wait_ge(sem("vn_taken"), 16)
            sp.dma_start(A["state_b_v_prompt"].rearrange("b l c n -> (b l c) n"), vn_nat[:, 1, :]).then_inc(sem("b_out"), 16)
            sp.dma_start(A["state_b_v_sample"].rearrange("b l s n -> b (l s n)"), vn_s).then_inc(sem("b_out"), 16)
            sp.wait_ge(sem("mixed"), 8)
            sp.wait_ge(sem("b_out"), 32)
            sp.dma_start(wple, A["w_ple"][0].rearrange("(k p) n -> p k n", p=P)).then_inc(sem("wple_in"), 16)
            w_g = A["w_ple_gate"][0].rearrange("(k p) n -> p k n", p=P)
            for m in range(8):
                weights(GATE0 + m, w_g, m // 4, m % 4)
                if m < 4:
                    pages(2, 5, m, cmp_pool)
            sp.dma_start(mask[:, :], A["mask_c"]).then_inc(sem("mask_c_in"), 16)
            for t in range(2):
                sp.dma_start(p_nat[:, t, :], A["p_prompt"][1, 0, tileT(t), :]).then_inc(sem("p_in"), 16)
            sp.dma_start(p_nat[0:B, 2, :], A["p_sample"][1].rearrange("b s d -> b (s d)")).then_inc(sem("p_in"), 16)
            w_c = A["w_in_c"][0].rearrange("(k p) n -> p k n", p=P)
            sp.wait_ge(sem("c_used"), NP + CMP_B + 48)
            sp.dma_start(wg, w_c[:, :, 40 * P:40 * P + 48]).then_inc(sem("wg_in"), 16)
            with sp.Fori(0, 5) as i:
                for bl in range(4):
                    weights(i * 4 + (CQ + bl), w_c, i, bl)
            sp.wait_ge(sem("cnat_taken"), 48)
            k2 = {0: ("cmp", 16), 1: ("cmp", 20), 2: ("sel", None), 3: ("sel", 28), 4: ("win", None), 5: ("win", 36)}
            for n, (name, slot) in k2.items():
                for t in range(2):
                    src = proj[:, slot:slot + 4, tileT(t)] if slot is not None else kst[:, n // 4, t, :]
                    dst = A[f"new_c_{name}_kv_prompt"][0, 0, n % 2, tileT(t)]
                    sp.dma_start(dst if slot is not None else dst.rearrange("p h d -> p (h d)"), src).then_inc(sem("c_out"), 16)
                sp.dma_start(A[f"new_c_{name}_kv_sample"][:, 0, n % 2, 0].rearrange("b h d -> b (h d)"), c_nat[:, n, :])\
                  .then_inc(sem("c_out"), 16)
            sp.wait_ge(sem("gate_taken"), 3)
            with nc.allow_non_contiguous_dma(reason="384 gate values change partitions"):
                for j in range(3):
                    for h in range(CH):
                        sp.dma_start(gate_s[32 * h:32 * h + 32, j:j + 1],
                                     gate_8[:, j * HQ + GQ * h:j * HQ + GQ * h + GQ]).then_inc(sem("gate_s_in"), 16)
            sp.wait_ge(sem("c_out"), 16 * 18)
            sel_pool = A["cache_c_sel_kv"].rearrange("n l v r h d -> n r (l v) (h d)")

            def page_of(b_pg):
                return sp.value_load(ptab[0:1, bass.ds(b_pg, 1)], min_val=0, max_val=n_phys - 1)

            def page_set(first, kv, n):
                for q in range(4):
                    page = page_of(first + q)
                    sp.dma_start(hring[:, 4 * (n % 2) + q, :].rearrange("p (o c) -> p o c", o=1),
                                 sel_pool[bass.ds(page, 1), :, kv, :].rearrange("o r c -> r o c")).then_inc(sem(f"set_in{n % 2}"), 16)

            win = A["cache_c_win_kv"].rearrange("b l v (w p) h d -> b w p (l v) (h d)", p=P)

            def win_set(b, kv, n):
                for q in range(WT):
                    sp.dma_start(hring[:, 4 * (n % 2) + q, :].rearrange("p (o c) -> p o c", o=1),
                                 win[bass.ds(b, 1), q, :, kv, :].rearrange("o p c -> p o c")).then_inc(sem(f"set_in{n % 2}"), 16)

            with sp.Fori(0, 4) as i:
                for b in range(B):
                    sp.wait_ge(sem("kt_T"), i * 32 + (4 * b + 4))
                    page_set(i * 4 + b * NPG, 0, b)
            for b in range(B):
                sp.wait_ge(sem("kt_T"), 128 + 4 * b + 4)
                win_set(b, 0, b)
            sp.wait_ge(sem("kt_T"), 8 + 160)
            w_z = w_c[:, :, 40 * P + 48:40 * P + 48 + D]
            sp.wait_ge(sem("kt_used"), K_STEPS)
            with sp.Fori(0, 4) as i:
                for b2 in range(2):
                    weights(i * 2 + (CZ + b2), w_z, i, b2, 2)
                    for k in range(5):
                        n = 5 * b2 + k
                        sp.wait_ge(sem("set_used"), i * 10 + (n + 1))
                        if k < 4:
                            page_set(i * 2 * NPG + (b2 * NPG + 4 * k), 1, n)
                        else:
                            win_set(i * 2 + b2, 1, n)

            w_o1 = A["w_out_c"][0].rearrange("(k p) n -> p k n", p=P)
            with sp.Fori(0, 2) as i:
                for bl in range(4):
                    weights(i * 4 + (OUT1 + bl), w_o1, i, bl)
            sp.wait_ge(sem("cat1"), 2)
            sp.dma_start(wple, A["w_ple"][1].rearrange("(k p) n -> p k n", p=P)).then_inc(sem("wple_in"), 16)
            w_g1 = A["w_ple_gate"][1].rearrange("(k p) n -> p k n", p=P)
            with sp.Fori(0, 2) as i:
                for bl in range(4):
                    weights(i * 4 + (GATE1 + bl), w_g1, i, bl)
            for q in range(4):
                sp.wait_ge(sem("y_taken"), 8 * (q + 1))
                a = slice(q * 512, (q + 1) * 512)
                for t in range(2):
                    sp.dma_start(A["y_prompt"][0, tileT(t), a], y_nat[:, t, a]).then_inc(sem("y_out"), 16)
                sp.dma_start(A["y_sample"][:, 0, a], y_s[:, a]).then_inc(sem("y_out"), 16)
            sp.wait_ge(sem("a_out"), 16 * 5)
            sp.wait_ge(sem("b_out"), 32)
            sp.wait_ge(sem("c_out"), 16 * 18)
            sp.wait_ge(sem("y_out"), 16 * 12)

        @block.gpsimd
        def _(pool):
            nc.gpsimd.memset(wide[:, :, :, :], 0.0).then_inc(sem("wide_zero"), 1)
            nc.gpsimd.memset(ones[:, :], 1.0).then_inc(sem("ones_set"), 1)
            nc.gpsimd.memset(zrow[:, :], 0.0).then_inc(sem("ones_set"), 1)
            nc.gpsimd.memset(eps, EPS).then_inc(sem("ones_set"), 1)

        @block.scalar
        def _(act):
            for f, n in (("w_used", 2), ("proj_made", 4), ("c_used", NP), ("proj_free", 4), ("cmp_free", 1),
                         ("kt_T", 8), ("set_used", 2), ("OT_taken", 2), ("qn_done", 4), ("qn_root", 2),
                         ("cn_done", 2), ("cn_root", 2)):
                act.sem_inc(sem(f), n)
            act.wait_ge(sem("xT_made"), 1)
            nc.scalar.copy(gains, XB[3][:, 0:NG]).then_inc(sem("gains_set"), 1)
            for c in range(KC + 2):
                act.wait_ge(sem("xT_made"), c + 2)
                dst = r0[:, c, :] if c < KC else pT[:, c - KC, :]
                nc.scalar.copy(dst, XB[c % 4][:, 0:T]).then_inc(sem("xT_taken"), 1)
            act.wait_ge(sem("ones_set"), 3)

            def rms(layer, h, sq):
                for c in range(KC):
                    if layer == 0:
                        act.wait_ge(sem("xT_taken"), c + 1)
                    nc.scalar.activation(sq[:, c, :], h[:, c, :], ACT.Square).then_inc(sem(f"rms_sq{layer}"), 1)
                act.wait_ge(sem(f"rms_sum{layer}"), 1)
                nc.scalar.activation(scr[:, 0, :], XB[0][:, 0:T], ACT.Sqrt, bias=eps, scale=1.0 / D)\
                  .then_inc(sem(f"rms_root{layer}"), 1)

            rms(0, r0, r1)

            def ab1_round(r, norm):
                if norm:
                    act.wait_ge(sem("proj_free"), r * 8 + 4)
                for bl in range(4):
                    pair = slice(2 * bl, 2 * bl + 2)
                    if norm:
                        nc.scalar.activation(scr[:, pair, :], proj[:, bass.ds((r - 1) * 8 + 2 * bl, 2), :], ACT.Square)\
                          .then_inc(sem("qn_sq"), 1)
                    for j in range(2 * bl, 2 * bl + 2):
                        act.wait_ge(sem("proj_made"), r * 8 + (4 + j + 1))
                        nc.scalar.copy(proj[:, bass.ds(r * 8 + j, 1), :], PJ[j % 4][:, 0:T]).then_inc(sem("proj_free"), 1)
                    if norm:
                        act.wait_ge(sem("qn_done"), (r - 1) * 4 + (bl + 1))
                        for c in range(2):
                            act.wait_ge(sem("qn_sum"), (r - 1) * 8 + (2 * bl + c + 1))
                            nc.scalar.activation(proj[:, 40 + 2 * bl + c, :], XB[2 + c][:, 0:T], ACT.Sqrt, bias=eps, scale=1.0 / P)\
                              .then_inc(sem("qn_root"), 1)

            ab1_round(0, False)
            with act.Fori(0, 3) as i:
                ab1_round(i + 1, True)
            ab1_round(4, True)

            def natural(t):
                act.wait_ge(sem("nat_made"), t + 1)
                src = XB[t % 4]
                dst = k_nat[:, :, tileT(t - 8)] if t >= 8 else proj[:, 32 + t, 0:S].rearrange("p (t n) -> p t n", t=2)
                nc.scalar.copy(dst, src[:, 0:S].rearrange("p (t n) -> p t n", t=2)).then_inc(sem("nat_taken"), 1)
                nc.scalar.copy(s_nat[:, 1 - t // 8, tileT(t % 8)], src[0:B, S:S + P]).then_inc(sem("nat_taken"), 1)

            def pa_exp(u):
                nk = AG * P * (u % 2 + 1)
                act.wait_ge(sem("pa_max"), u + 1)
                nc.scalar.activation(S_sb[:, u % 2, 0:nk], S_sb[:, u % 2, 0:nk], ACT.Exp, bias=nmx[:, u % 2:u % 2 + 1],
                                     accum_out=den[:, u % 2:u % 2 + 1]).then_inc(sem("pa_exp"), 1)

            def pa_pT(u):
                qt = u % 2
                act.wait_ge(sem("pa_pT"), u + 1)
                nc.scalar.copy(PT[:, u % 2, 0:P * (qt + 1)], XB[3][:, 0:P * (qt + 1)]).then_inc(sem("pa_pT_taken"), 1)

            def pa_out(u):
                act.wait_ge(sem("pa_o"), u + 1)
                nc.scalar.copy(scr[:, u // 2, tileT(u % 2)], XB[3][:, 384:512]).then_inc(sem("pa_o_taken"), 1)

            def dk_copy(n):
                act.wait_ge(sem("dk_T"), n + 1)
                if n >= 2:
                    act.wait_ge(sem("c_used"), AK + NP + n - 1)
                else:
                    act.wait_ge(sem("qz_set"), 1)
                nc.scalar.copy(KT[:, n % 2, 0:512], XB[2][:, :]).then_inc(sem("dk_T_taken"), 1)

            def d_exps():
                for u in range(2):
                    act.wait_ge(sem("d_max"), 1)
                    nc.scalar.activation(Sd[:, u, 0:387], Sd[:, u, 0:387], ACT.Exp, bias=nmx[:, u:u + 1],
                                         accum_out=den[:, u:u + 1]).then_inc(sem("d_exp"), 1)

            def d_probs():
                act.wait_ge(sem("d_pT"), 1)
                nc.scalar.copy(PTd[:, 0:2, :, :], XB[2][:, :].rearrange("p (g u r) -> p g u r", g=2, u=2)).then_inc(sem("d_pT_taken"), 1)
                nc.scalar.copy(PTd[:, 2, :, :], XB[3][:, 0:256].rearrange("p (u r) -> p u r", u=2)).then_inc(sem("d_pT_taken"), 1)

            def vn_rows(g):
                act.wait_ge(sem("vn_T"), g + 1)
                src = XB[g % 2]
                nc.scalar.copy(vn_nat[:, :, tileT(g)], src[:, 0:S].rearrange("p (t n) -> p t n", t=2)).then_inc(sem("vn_taken"), 1)
                nc.scalar.copy(vn_s[:, tileT(g)], src[0:B, S:S + P]).then_inc(sem("vn_taken"), 1)

            for s in range(16 * SLOTS):
                if s % SLOTS in (5, 7):
                    j = 2 * (s // SLOTS) + s % SLOTS // 7
                    if j == 8:
                        act.wait_ge(sem("a_out"), 16 * 5)
                    act.wait_ge(sem("proj_made"), 44 + j + 1)
                    nc.scalar.copy(proj[:, 40 + j if j < 24 else j - 24, :], PJ[j % 4][:, 0:T]).then_inc(sem("proj_free"), 1)
                if s < PA_AT:
                    natural(2 * s)
                    natural(2 * s + 1)
                    if s == PA_AT - 1:
                        pa_exp(0)
                        pa_exp(1)
                elif s < PA_AT + 48:
                    u, part = (s - PA_AT) // 3, (s - PA_AT) % 3
                    if part == 0:
                        pa_pT(u)
                    elif part == 1:
                        pa_out(u)
                    elif u + 2 < 16:
                        pa_exp(u + 2)
                elif DK_AT <= s < DK_AT + AG * B:
                    dk_copy(s - DK_AT)
                elif s == DS_AT + 1:
                    d_exps()
                elif s == DP_AT:
                    d_probs()
                elif DV_AT <= s < DV_AT + AG * B:
                    b, g = (s - DV_AT) // AG, (s - DV_AT) % AG
                    if g == AG - 1:
                        act.wait_ge(sem("c_used"), AV + NP + 3 * b + 3)
                        nc.scalar.copy(Od[:, b % 2, :], XB[b % 2][:, 0:256]).then_inc(sem("dO_taken"), 1)
                elif s == LN_AT + 2:
                    act.wait_ge(sem("ln_centred"), 1)
                    nc.scalar.activation(sq8, xc, ACT.Square).then_inc(sem("ln_sq"), 1)
                elif s == LN_AT + 5:
                    act.wait_ge(sem("ln_sum"), 2)
                    nc.scalar.activation(pnewT, XB[1][:, 0:T], ACT.Sqrt, bias=eps, scale=1.0 / 1024).then_inc(sem("ln_root"), 1)
                elif VN_AT <= s < VN_AT + 4:
                    vn_rows(2 * (s - VN_AT))
                    vn_rows(2 * (s - VN_AT) + 1)
            act.wait_ge(sem("proj_free"), 4 + 72)
            nc.scalar.activation(proj[:, 40:48, :], proj[:, 40:48, :], ACT.Silu).then_inc(sem("silu"), 1)
            nc.scalar.activation(proj[:, 0:8, :], proj[:, 0:8, :], ACT.Silu).then_inc(sem("silu"), 1)

            def ple(layer, free):
                act.wait_ge(sem(free[0]), free[1])
                for c in range(KC):
                    act.wait_ge(sem(f"ple_made{layer}"), c + 1)
                    nc.scalar.copy(proj[:, c, :], XB[c % 4][:, 0:T]).then_inc(sem(f"ple_taken{layer}"), 1)

            def gate(layer, done):
                with act.Fori(0, 2) as i:
                    for j in range(8):
                        act.wait_ge(sem("proj_made"), i * 8 + (4 + done + j + 1))
                        act.wait_ge(sem(f"h_new{layer}"), i * 8 + (j + 1))
                        nc.scalar.activation(scr[:, j % 4, :], PJ[j % 4][:, 0:T], ACT.Sigmoid).then_inc(sem("proj_free"), 1)
            ple(0, ("cat0", 4))
            gate(0, 88)

            for k in range(2):
                act.wait_ge(sem("pT_made"), k + 1)
                nc.scalar.copy(pT[:, k, :], XB[1 + k][:, 0:T]).then_inc(sem("pT_taken"), 1)
            act.wait_ge(sem("h_new0"), 4 + KC)
            rms(1, r1, r0)
            act.wait_ge(sem("xn_ready1"), KC)

            for n in range(4 * B):
                if n >= 2:
                    act.wait_ge(sem("ks_sum"), n - 1)
                nc.scalar.activation(F[:, P * (n % 2):P * (n % 2 + 1)], kcmp[:, n // 4, n % 4, :], ACT.Square,
                                     accum_out=kss[:, n:n + 1]).then_inc(sem("ks_sum"), 1)
            act.wait_ge(sem("ks_sum"), 32)
            nc.scalar.activation(krt, kss, ACT.Sqrt, bias=eps, scale=1.0 / P).then_inc(sem("ks_root"), 1)

            def cq_tile(r, j):
                act.wait_ge(sem("proj_made"), r * 8 + (4 + 104 + j + 1))
                nc.scalar.copy(proj[:, bass.ds(r * 8 + j, 1), :], PJ[j % 4][:, 0:T]).then_inc(sem("proj_free"), 1)

            def cn_squares(odd, first):
                nc.scalar.activation(scr[:, 2 * odd:2 * odd + 2, :], proj[:, bass.ds(first, 2), :], ACT.Square).then_inc(sem("cn_sq"), 1)

            def cn_roots(p, odd):
                act.wait_ge(sem("cn_done"), p + 1)
                for c in range(2):
                    act.wait_ge(sem("cn_sum"), p * 2 + (c + 1))
                    nc.scalar.activation(scr[:, 4 + 2 * odd + c, :], XB[2 + c][:, 0:T], ACT.Sqrt, bias=eps, scale=1.0 / P)\
                      .then_inc(sem("cn_root"), 1)

            def natural_c(n):
                act.wait_ge(sem("cnat_made"), n + 1)
                t = NAT[n]
                src, v = XB[n % 2 + (2 if n >= 16 else 0)], t // 4
                dst = kst[:, v // 4, :, tileT(t % 4)] if v in (2, 4) else proj[:, 16 + t, 0:S].rearrange("p (t n) -> p t n", t=2)
                nc.scalar.copy(dst, src[:, 0:S].rearrange("p (t n) -> p t n", t=2)).then_inc(sem("cnat_taken"), 1)
                nc.scalar.copy(c_nat[:, v, tileT(t % 4)], src[0:B, S:S + P]).then_inc(sem("cnat_taken"), 1)

            for j in range(8):
                cq_tile(0, j)
                if j >= 4:
                    for b in (2 * j - 8, 2 * j - 7):
                        act.wait_ge(sem("kcT_made"), b + 1)
                        nc.scalar.activation(kcmp[:, b].rearrange("p a r -> p (a r)"), XB[b % 2][:, :], ACT.Copy, scale=g_kc[:, 0:1])\
                          .then_inc(sem("kcT_taken"), 1)
            with act.Fori(0, 2) as i:
                act.wait_ge(sem("proj_free"), i * 8 + (4 + 104 + 8))
                for bl in range(4):
                    cn_squares(bl % 2, i * 8 + 2 * bl)
                    cq_tile(i + 1, 2 * bl)
                    cq_tile(i + 1, 2 * bl + 1)
                    cn_roots(i * 4 + bl, bl % 2)
            for r in (3, 4):
                for bl in range(4):
                    if bl >= 2:
                        if bl == 2:
                            act.wait_ge(sem("proj_free"), 4 + 104 + 8 * r + 4)
                        cn_squares(bl % 2, 8 * r + 2 * (bl - 2))
                    for s in range(1, SLOTS, 2):
                        if s >= 5:
                            cq_tile(r, 2 * bl + (s - 5) // 2)
                        if bl < 2:
                            natural_c(8 * (r - 3) + 4 * bl + s // 2)
                    if bl >= 2:
                        cn_roots(8 + 2 * (r - 3) + bl - 2, bl % 2)
            for n in range(16, 20):
                natural_c(n)
            act.wait_ge(sem("cn_done"), 2 + 12)
            act.wait_ge(*done("pc_made"))
            nc.scalar.copy(kcp, XB[0][:, 0:P]).then_inc(sem("act_chain"), 1)
            nc.scalar.copy(vcp, XB[1][0:32, :].rearrange("p (h d) -> p h d", h=CH)).then_inc(sem("vcp_set"), 1)
            act.wait_ge(sem("act_chain"), 1)
            nc.scalar.activation(SC[:, 1600:1728], kcp, ACT.Square, accum_out=kss[:, 0:1]).then_inc(sem("act_chain"), 1)
            act.wait_ge(sem("act_chain"), 2)
            nc.scalar.activation(krt[:, 0:1], kss[:, 0:1], ACT.Sqrt, bias=eps, scale=1.0 / P).then_inc(sem("pc_root"), 1)
            for n in range(20, 24):
                natural_c(n)
            act.wait_ge(*done("gT_made"))
            nc.scalar.activation(gT, PJ[0][0:48, 0:T], ACT.Sigmoid).then_inc(sem("gT_set"), 1)
            act.wait_ge(*done("gate_made"))
            for t in range(2):
                nc.scalar.copy(gate_p[:, t].rearrange("p j h -> p (j h)"), PJ[1][:, 64 * t:64 * t + 48]).then_inc(sem("gate_taken"), 1)
            nc.scalar.copy(gate_8, PJ[1][0:B, 128:176]).then_inc(sem("gate_taken"), 1)
            act.wait_ge(*done("pc_centred"))
            nc.scalar.activation(Pc, Pc, ACT.Exp).then_inc(sem("pc_exp"), 1)
            act.wait_ge(sem("sc_max"), 1)
            nc.scalar.activation(S_cmp[:, 0:NCMP], S_cmp[:, 0:NCMP], ACT.Exp, bias=mx_c[:, 0:1], accum_out=den_c[:, 0:1])\
              .then_inc(sem("sc_exp"), 1)
            act.wait_ge(*done("pc_p"))
            act.wait_ge(sem("c_out"), 16 * 18)

            def pc_exps(u):
                qt, nk = u % 2, P * (u % 2 + 1)
                act.wait_ge(sem("cu_max"), u + 1)
                for br in range(2):
                    a = slice(br * nk, (br + 1) * nk)
                    nc.scalar.activation(S_c[:, qt, a], S_c[:, qt, a], ACT.Exp, bias=nmx[:, 2 * qt + br:2 * qt + br + 1],
                                         accum_out=den[:, 2 * qt + br:2 * qt + br + 1]).then_inc(sem("cu_exp"), 1)

            def pc_pT(u):
                qt, nk = u % 2, P * (u % 2 + 1)
                act.wait_ge(sem("cu_pT"), u + 1)
                nc.scalar.copy(PT_c[:, qt, 0:2 * nk], PJ[2][:, 0:2 * nk]).then_inc(sem("cu_pT_taken"), 1)
                nc.scalar.copy(PcT[:, qt, :], PJ[3][0:16, 0:P]).then_inc(sem("cu_pT_taken"), 1)

            def pc_out(u):
                act.wait_ge(sem("cu_o"), u + 1)
                nc.scalar.copy(proj[:, 40 + u // 2, tileT(u % 2)], PJ[3][:, P:2 * P]).then_inc(sem("cu_o_taken"), 1)

            def k_even(steps):
                for k in steps:
                    if k % 2 == 0:
                        act.wait_ge(sem("kt_T"), 8 + k + 1)
                        if k >= CH:
                            act.wait_ge(sem("kt_used"), k - CH + 1)
                        nc.scalar.copy(KTc[:, k % CH, :], XB[1 + k % 3][:, :]).then_inc(sem("kt_even"), 1)

            pc_exps(0)
            act.wait_ge(*done("psum_made"))
            nc.scalar.copy(P_sum, XB[0][:, 128:256]).then_inc(sem("psum_taken"), 1)
            for u in range(32):
                if u == K_FROM - 1:
                    act.wait_ge(*done("ptexp_made"))
                    nc.scalar.copy(PT_exp.rearrange("p a r -> p (a r)"), XB[3][:, :]).then_inc(sem("ptexp_taken"), 1)
                before, after = k_steps(u)
                pc_pT(u)
                k_even(before)
                if u + 1 < 32:
                    pc_exps(u + 1)
                pc_out(u)
                k_even(after)
            for br, (s_br, n) in enumerate(((S_sel, 2048), (S_win, 512))):
                act.wait_ge(sem("sw_max"), br + 1)
                nc.scalar.activation(s_br, s_br, ACT.Exp, bias=mx_c[:, 1 + br:2 + br], accum_out=den_c[:, 1 + br:2 + br]).then_inc(sem("sw_exp"), 1)
                nc.scalar.activation(p_new[:, br:br + 1], s_new[:, br:br + 1], ACT.Exp, bias=mx_c[:, 1 + br:2 + br]).then_inc(sem("sw_exp"), 1)
            for q in range(5):
                act.wait_ge(sem("sw_pT"), q + 1)
                dst = PT_sel[:, 4 * q:4 * q + 4, :] if q < 4 else PT_win
                nc.scalar.copy(dst.rearrange("p a r -> p (a r)"), XB[q % 4][:, :]).then_inc(sem("sw_pT_taken"), 1)
            with act.Fori(0, 2) as i:
                for j in range(8):
                    act.wait_ge(sem("proj_made"), i * 8 + (4 + 144 + j + 1))
                    nc.scalar.activation(proj[:, bass.ds(i * 8 + j, 1), :], PJ[j % 4][:, 0:T], ACT.Silu).then_inc(sem("proj_free"), 1)
            ple(1, ("cat1", 2))
            gate(1, 176)
            for c in range(KC):
                act.wait_ge(sem("y_made"), c + 1)
                nc.scalar.copy(y_nat[:, :, tileT(c)], XB[c % 4][:, 0:S].rearrange("p (t n) -> p t n", t=2)).then_inc(sem("y_taken"), 1)
                nc.scalar.copy(y_s[:, tileT(c)], XB[c % 4][0:B, S:S + P]).then_inc(sem("y_taken"), 1)

        @block.vector
        def _(dve):
            chain = [0]

            def link(ins):
                chain[0] += 1
                ins.then_inc(sem("dve_chain"), 1)
                dve.wait_ge(sem("dve_chain"), chain[0])

            def normalise(layer, h, xn, g):
                dve.wait_ge(sem(f"rms_root{layer}"), 1)
                link(nc.vector.reciprocal(scr[:, 1, :], scr[:, 0, :]))
                for c in range(KC):
                    nc.vector.scalar_tensor_tensor(xn[:, c, :], h[:, c, :], g[:, c:c + 1], scr[:, 1, :],
                                                   ALU.mult, ALU.mult).then_inc(sem(f"xn_ready{layer}"), 1)

            def compressed(r, b, c0):
                dve.wait_ge(sem("c_used"), r * 16 + (c0 + NP + 16))
                nc.vector.tensor_copy(kcmp[:, bass.ds(b, 1)].rearrange("p o a d -> p (o a) d"),
                                      XB[0][:, :].rearrange("p (a d) -> p a d", a=4)).then_inc(sem("cmp_half"), 1)
                nc.vector.tensor_copy(vcmp[:, bass.ds(b, 1)].rearrange("p o a d -> p (o a) d"),
                                      XB[1][:, :].rearrange("p (a d) -> p a d", a=4)).then_inc(sem("cmp_free"), 1)

            def rope(dst, src, tmp, swp, heads):
                cosb = cos.rearrange("p (o t) -> p o t", o=1).broadcast_to([32, heads, T])
                sinb = sin.rearrange("p (o t) -> p o t", o=1).broadcast_to([32, heads, T])
                link(nc.vector.stream_shuffle(swp, src, [(m + HALF) % 32 for m in range(32)]))
                link(nc.vector.tensor_tensor(swp, swp, sinb, ALU.mult))
                link(nc.vector.tensor_tensor(tmp, src, cosb, ALU.mult))
                link(nc.vector.tensor_tensor(dst, tmp, swp, ALU.add))

            dve.wait_ge(sem("gains_set"), 1)
            normalise(0, r0, r1, g_ab)

            def ab1_round(r, gain):
                for bl in range(4):
                    if bl == 3:
                        compressed(r, r, CMP_A)
                    if gain is not None:
                        dve.wait_ge(sem("qn_root"), (r - 1) * 8 + (2 + 2 * bl + 2))
                        root = proj[:, 40 + 2 * bl:42 + 2 * bl, :]
                        x = proj[:, bass.ds((r - 1) * 8 + 2 * bl, 2), :]
                        link(nc.vector.reciprocal(root, root))
                        link(nc.vector.scalar_tensor_tensor(x, x, gain, root, ALU.mult, ALU.mult))
                        x32 = proj[0:32, bass.ds((r - 1) * 8 + 2 * bl, 2), :]
                        rope(x32, x32, root[0:32], lnt[0:32], 2)
                        dve.sem_inc(sem("qn_done"), 1)

            for r, gain in enumerate((None, g_qa, g_qa, g_qa, g_ka)):
                ab1_round(r, gain)

            def pa_scores(u):
                qt, nk = u % 2, P * (u % 2 + 1)
                dve.wait_ge(sem("pa_s"), u + 1)
                if u >= 2:
                    dve.wait_ge(sem("pa_pT"), u - 1)
                m = mask[:, AG * P * qt:AG * P * qt + AG * nk]
                if qt == 0:
                    link(nc.vector.scalar_tensor_tensor(S_sb[:, 0, 0:384], XB[0][:, 0:384], SCALE, m, ALU.mult, ALU.add))
                else:
                    link(nc.vector.scalar_tensor_tensor(S_sb[:, 1, 0:512], XB[1][:, :], SCALE, m[:, 0:512], ALU.mult, ALU.add))
                    link(nc.vector.scalar_tensor_tensor(S_sb[:, 1, 512:768], XB[2][:, 0:256], SCALE, m[:, 512:768], ALU.mult, ALU.add))
                nc.vector.tensor_reduce(nmx[:, qt:qt + 1], S_sb[:, qt, 0:AG * nk], AX, ALU.max, negate=True).then_inc(sem("pa_max"), 1)

            def pa_probs(u):
                qt, nk = u % 2, P * (u % 2 + 1)
                dve.wait_ge(sem("pa_exp"), u + 1)
                s0, s1, s2 = (S_sb[:, qt, g * nk:(g + 1) * nk] for g in range(AG))
                link(nc.vector.reciprocal(rden[:, qt:qt + 1], den[:, qt:qt + 1]))
                link(nc.vector.tensor_tensor(s0, s0, s1, ALU.add))
                link(nc.vector.tensor_tensor(s0, s0, s2, ALU.add))
                nc.vector.tensor_scalar(s0, s0, rden[:, qt:qt + 1], None, ALU.mult).then_inc(sem("pa_p"), 1)

            dve.wait_ge(sem("mask_a_in"), 16)
            pa_scores(0)
            pa_scores(1)
            for u in range(16):
                pa_probs(u)
                if u + 2 < 16:
                    pa_scores(u + 2)

            dve.wait_ge(sem("pa_o_taken"), 16)
            link(nc.vector.memset(spare_k, 0.0))
            link(nc.vector.memset(spare_v[:, 0:1024], 0.0))
            for g in range(AG):
                for b in range(B):
                    nc.vector.tensor_copy(qz[:, g, b, :, b], proj[:, 8 * g:8 * g + 8, S + b])
            for g in range(AG):
                for u in range(2):
                    ins = nc.vector.tensor_tensor(prod[:, g, u, :].rearrange("p (j b) -> p j b", j=4)[:, :, 0:B],
                                                  proj[:, 8 * g + 4 * u:8 * g + 4 * u + 4, S:T],
                                                  proj[:, 24 + 4 * u:28 + 4 * u, S:T], ALU.mult)
            link(ins)
            dve.sem_inc(sem("qz_set"), 1)
            for n in range(B * AG):
                dve.wait_ge(sem("dk_T"), n + 1)
                if n >= 2:
                    dve.wait_ge(sem("c_used"), AK + NP + n - 1)
                nc.vector.tensor_copy(KT[:, n % 2, 512:1024], XB[3][:, :]).then_inc(sem("dk_T_taken2"), 1)
            dve.wait_ge(sem("d_s"), 1)
            for u in range(2):
                link(nc.vector.tensor_scalar(Sd[:, u, 0:387], XB[u][:, 0:387], SCALE, None, ALU.mult))
            nc.vector.tensor_reduce(nmx[:, 0:2], Sd[:, :, 0:387], AX, ALU.max, negate=True).then_inc(sem("d_max"), 1)
            dve.wait_ge(sem("d_exp"), 2)
            link(nc.vector.reciprocal(rden[:, 0:2], den[:, 0:2]))
            for u in range(2):
                link(nc.vector.tensor_scalar(Sd[:, u, 0:387], Sd[:, u, 0:387], rden[:, u:u + 1], None, ALU.mult))
            link(nc.vector.tensor_reduce(pnew[:, 0:2], Sd[:, :, 384:387], AX, ALU.add))
            for u in range(2):
                link(nc.vector.tensor_scalar(diag[:, u, :], ident, pnew[:, u:u + 1], None, ALU.mult))
            dve.sem_inc(sem("d_p"), 1)
            dve.wait_ge(sem("d_new"), 1)
            link(nc.vector.tensor_tensor(vs_a.rearrange("p (u j b) -> p u j b", u=2, j=4),
                                         XB[1][:, 0:256].rearrange("p (u j b) -> p u j b", u=2, j=4)[:, :, :, 0:B],
                                         proj[:, 32:40, S:T].rearrange("p (u j) b -> p u j b", u=2), ALU.mult))
            dve.sem_inc(sem("d_new_taken"), 1)
            vs4 = vs_a.rearrange("p (u j b) -> p u j b", u=2, j=4)
            scr4 = scr[:, :, :].rearrange("p (u j) t -> p u j t", u=2)
            for b in range(B):
                dve.wait_ge(sem("dO_T"), b + 1)
                src = XB[2 + b % 2][:, 0:256].rearrange("p (u j b) -> p u j b", u=2, j=4)[:, :, :, b]
                nc.vector.tensor_tensor(scr4[:, :, :, S + b], src, vs4[:, :, :, b], ALU.add).then_inc(sem("oTd"), 1)

            dve.wait_ge(sem("ln_sum"), 1)
            link(nc.vector.tensor_scalar(pnewT, XB[0][:, 0:T], 1.0 / 1024, None, ALU.mult))
            link(nc.vector.tensor_tensor(xc, xc, pnewT.rearrange("p (o t) -> p o t", o=1).broadcast_to([P, 8, T]), ALU.subtract))
            dve.sem_inc(sem("ln_centred"), 1)
            dve.wait_ge(sem("ln_root"), 1)
            link(nc.vector.reciprocal(lnr, pnewT))
            for g in range(8):
                ins = nc.vector.scalar_tensor_tensor(xc[:, g, :], xc[:, g, :], g_sgu[:, g:g + 1], lnr, ALU.mult, ALU.mult)
            link(ins)
            dve.sem_inc(sem("vn_ready"), 1)
            for n in range(2):
                dve.wait_ge(sem("ws_T"), n + 1)
                nc.vector.tensor_tensor(wsT[:, 4 * n:4 * n + 4, :], XB[2 + n][:, :].rearrange("p (g s) -> p g s", g=4),
                                        const[:, C_TRIL:C_TRIL + P].rearrange("p (o s) -> p o s", o=1).broadcast_to([P, 4, P]),
                                        ALU.mult).then_inc(sem("wsT_set"), 1)
            dve.wait_ge(sem("w00_made"), 1)
            link(nc.vector.tensor_copy(w00, XB[2][:, 0:8]))
            link(nc.vector.tensor_copy(b00, XB[2][:, 8:16]))
            dve.sem_inc(sem("w00_taken"), 1)
            for g in range(8):
                link(nc.vector.tensor_scalar(rden, xc[:, g, S:T], w00[:, g:g + 1], b00[:, g:g + 1], ALU.mult, ALU.add))
                link(nc.vector.tensor_tensor(proj[:, 48 + g, S:T], proj[:, 48 + g, S:T], rden, ALU.mult))
                dve.wait_ge(sem("mix_made"), g + 1)
                nc.vector.tensor_tensor(proj[:, 48 + g, 0:S], proj[:, 48 + g, 0:S], XB[g % 4][:, 0:S], ALU.mult)\
                  .then_inc(sem("mixed"), 1)
            dve.wait_ge(sem("silu"), 2)
            dve.wait_ge(sem("mixed"), 8)
            for n in range(2):
                a = slice(4 * n, 4 * n + 4)
                nc.vector.tensor_tensor(r1[:, 4 * n:4 * n + 4, :], scr[:, a, :], proj[:, 40 + 4 * n:44 + 4 * n, :], ALU.mult).then_inc(sem("cat0"), 1)
                nc.vector.tensor_tensor(r1[:, 8 + 4 * n:12 + 4 * n, :], proj[:, 48 + 4 * n:52 + 4 * n, :], proj[:, a, :], ALU.mult).then_inc(sem("cat0"), 1)

            def add_mix(h, done, compress):
                with dve.Fori(0, 2) as i:
                    for j in range(8):
                        dve.wait_ge(sem("proj_made"), i * 8 + (4 + done + j + 1))
                        hj = h[:, bass.ds(i * 8 + j, 1), :]
                        nc.vector.tensor_tensor(hj, hj, PJ[j % 4][:, 0:T].rearrange("p (o t) -> p o t", o=1), ALU.add)\
                          .then_inc(sem("proj_free"), 1)
                    if compress:
                        compressed(i, i + 5, CMP_B)

            def gated(layer, h, out, done):
                dve.sem_inc(sem(f"h_new{layer}"), 4)
                dve.wait_ge(sem(f"ple_taken{layer}"), KC)
                with dve.Fori(0, 2) as i:
                    for j in range(8):
                        dve.wait_ge(sem("proj_free"), i * 8 + (4 + done + j + 1))
                        sg = scr[:, j % 4, :].rearrange("p (o t) -> p o t", o=1)
                        tm = scr[:, 4 + j % 4, :].rearrange("p (o t) -> p o t", o=1)
                        nc.vector.tensor_tensor(tm, sg, proj[:, bass.ds(i * 8 + j, 1), :], ALU.mult).then_inc(sem(f"gp{layer}"), 1)
                        dve.wait_ge(sem(f"gp{layer}"), i * 8 + (j + 1))
                        nc.vector.tensor_tensor(out[:, bass.ds(i * 8 + j, 1), :], tm, h[:, bass.ds(i * 8 + j, 1), :], ALU.add)\
                          .then_inc(sem(f"h_new{layer}"), 1)
            add_mix(r0, 72, True)
            gated(0, r0, r1, 88)
            compressed(2, 7, CMP_B)

            normalise(1, r1, r0, g_c)
            dve.wait_ge(sem("ks_root"), 1)
            link(nc.vector.reciprocal(krt, krt))
            k32 = kcmp[:, :, :, :].rearrange("p b a d -> p (b a) d")
            link(nc.vector.tensor_tensor(k32, k32, krt.rearrange("p (n o) -> p n o", o=1).broadcast_to([P, 32, P]), ALU.mult))
            dve.sem_inc(step("kc_ready"), 1)

            for p, first in enumerate(PAIRS):
                dve.wait_ge(sem("cn_root"), 2 + 2 * p + 2)
                root = scr[:, 4 + 2 * (p % 2):6 + 2 * (p % 2), :]
                x = proj[:, first:first + 2, :]
                g = g_qc if p < 8 else g_kc[:, 1:2] if p < 10 else g_kc[:, 2:3]
                link(nc.vector.reciprocal(root, root))
                link(nc.vector.scalar_tensor_tensor(x, x, g, root, ALU.mult, ALU.mult))
                src = dst = proj[0:32, first:first + 2, :]
                if p < 8:
                    link(nc.vector.tensor_copy(proj[:, 40 + first:42 + first, :], x))
                    dst = proj[0:32, 40 + first:42 + first, :]
                rope(dst, src, root[0:32], lnt[0:32], 2)
                dve.sem_inc(sem("cn_done"), 1)

            def over(x, dims):
                return x.broadcast_to(dims)

            dve.wait_ge(sem("pc_root"), 1)
            link(nc.vector.reciprocal(krt[:, 0:1], krt[:, 0:1]))
            nc.vector.tensor_scalar(kcp, kcp, krt[:, 0:1], None, ALU.mult).then_inc(step("kcp_ready"), 1)
            dve.wait_ge(*done("kcpT_made"))
            nc.vector.tensor_scalar(kcpT, XB[1][:, 0:P], g_kc[:, 0:1], None, ALU.mult).then_inc(step("kcpT_set"), 1)
            for n in range(8):
                dve.wait_ge(sem("pcs_made"), n + 1)
                h = n % 4
                nc.vector.tensor_scalar(Pc[:, 4 * n:4 * n + 4, :],
                                        XB[n % 4][:, :].rearrange("p (g m) -> p g m", g=GQ)[:, :, 32 * h:32 * h + 16],
                                        SCALE, None, ALU.mult).then_inc(sem("pcs_taken"), 1)
            dve.wait_ge(sem("pcs_taken"), 8)
            Pq = Pc.rearrange("p (q h) n -> p q h n", q=2)
            vis = const[:, C_VIS:C_VIS + 32].rearrange("p (q o n) -> p q o n", q=2, o=1)
            see = const[:, C_SEE:C_SEE + 32].rearrange("p (q o n) -> p q o n", q=2, o=1)
            pmx = cmx[:, 0:32]
            link(nc.vector.tensor_tensor(Pq, Pq, over(vis, [P, 2, HQ, 16]), ALU.add))
            link(nc.vector.tensor_reduce(pmx, Pc, AX, ALU.max))
            pm3 = pmx.rearrange("p (u o) -> p u o", o=1)
            link(nc.vector.tensor_tensor(Pc, Pc, over(pm3, [P, 32, 16]), ALU.subtract))
            dve.sem_inc(step("pc_centred"), 1)
            dve.wait_ge(sem("proj_made"), 4 + 144)
            link(nc.vector.memset(spare[:, 0:1024], 0.0))
            for b in range(B):
                ins = nc.vector.tensor_copy(qzu[:, b, :, 4 * b:4 * b + 4], proj[:, 0:16, S + b].rearrange("p (h g) -> p h g", h=CH))
            link(ins)
            link(nc.vector.memset(Q[:, 0:1024], 0.0))
            for b in range(B):
                ins = nc.vector.tensor_copy(qzr[:, b, :, 4 * b:4 * b + 4], proj[:, 40:56, S + b].rearrange("p (h g) -> p h g", h=CH))
            for br, slot in enumerate((24, 32)):
                for g in range(GQ):
                    q4 = proj[:, 40:56, S:T].rearrange("p (h g) b -> p g h b", h=CH)[:, g]
                    ins = nc.vector.tensor_tensor(diag_c[:, br, :].rearrange("p (h b g) -> p g h b", h=CH, b=B)[:, g], q4,
                                                  proj[:, slot:slot + 4, S:T], ALU.mult)
            link(ins)
            dve.sem_inc(step("qz_c"), 1)
            dve.wait_ge(sem("pc_exp"), 1)
            link(nc.vector.tensor_tensor(Pq, Pq, over(see, [P, 2, HQ, 16]), ALU.mult))
            link(nc.vector.tensor_reduce(pmx, Pc, AX, ALU.add))
            link(nc.vector.tensor_scalar(pmx, pmx, TINY, None, ALU.max))
            link(nc.vector.reciprocal(pmx, pmx))
            dve.wait_ge(sem("gate_taken"), 3)
            link(nc.vector.tensor_tensor(pmx.rearrange("p (q h) -> p q h", q=2), pmx.rearrange("p (q h) -> p q h", q=2),
                                         gate_p[:, :, 0, :], ALU.mult))
            link(nc.vector.tensor_tensor(Pc, Pc, over(pm3, [P, 32, 16]), ALU.mult))
            dve.sem_inc(step("pc_p"), 1)
            dve.wait_ge(sem("c_out"), 16 * 18)
            dve.wait_ge(sem("mask_c_in"), 16)

            def cu_scores(u):
                qt, nk = u % 2, P * (u % 2 + 1)
                dve.wait_ge(sem("cu_s"), u + 1)
                if u >= 2:
                    dve.wait_ge(sem("cu_pT"), u - 1)
                m = mask[:, P * qt:P * qt + nk].rearrange("p (o n) -> p o n", o=1)
                s2 = S_c[:, qt, 0:2 * nk].rearrange("p (b n) -> p b n", b=2)
                link(nc.vector.scalar_tensor_tensor(s2, PJ[qt][:, 0:2 * nk].rearrange("p (b n) -> p b n", b=2), SCALE,
                                                    over(m, [P, 2, nk]), ALU.mult, ALU.add))
                nc.vector.tensor_reduce(nmx[:, 2 * qt:2 * qt + 2], s2, AX, ALU.max, negate=True).then_inc(sem("cu_max"), 1)

            def cu_probs(u):
                hq, qt, nk = u // 2, u % 2, P * (u % 2 + 1)
                dve.wait_ge(sem("cu_exp"), 2 * u + 2)
                rd = rden[:, 2 * qt:2 * qt + 2]
                link(nc.vector.reciprocal(rd, den[:, 2 * qt:2 * qt + 2]))
                link(nc.vector.tensor_tensor(rd, rd, gate_p[:, qt, 1:3, hq], ALU.mult))
                s2 = S_c[:, qt, 0:2 * nk].rearrange("p (b n) -> p b n", b=2)
                nc.vector.tensor_tensor(s2, s2, over(rd.rearrange("p (b o) -> p b o", o=1), [P, 2, nk]), ALU.mult).then_inc(sem("cu_p"), 1)

            def sc_scores():
                dve.wait_ge(*done("scmp_made"))
                link(nc.vector.tensor_scalar(S_cmp, XB[0][:, 0:P], SCALE, None, ALU.mult))
                link(nc.vector.tensor_scalar(s_new, XB[1][:, 0:2], SCALE, None, ALU.mult))
                nc.vector.tensor_reduce(mx_c[:, 0:1], S_cmp[:, 0:NCMP], AX, ALU.max, negate=True).then_inc(sem("sc_max"), 1)

            def sc_probs():
                dve.wait_ge(sem("sc_exp"), 1)
                link(nc.vector.memset(S_cmp[:, NCMP:P], 0.0))
                link(nc.vector.tensor_scalar(rd_c[:, 0:1], den_c[:, 0:1], TINY, None, ALU.max))
                link(nc.vector.reciprocal(rd_c[:, 0:1], rd_c[:, 0:1]))
                link(nc.vector.tensor_scalar(S_cmp, S_cmp, rd_c[:, 0:1], None, ALU.mult))
                dve.sem_inc(step("scmp_p"), 1)

            def sc_ranks():
                dve.wait_ge(*done("imp_made"))
                link(nc.vector.tensor_copy(imp, XB[1][:, 0:NPICK]))
                imp_i = over(imp.rearrange("p (o i) -> p o i", o=1), [P, NPICK, NPICK])
                imp_j = over(imp.rearrange("p (j o) -> p j o", o=1), [P, NPICK, NPICK])
                link(nc.vector.tensor_tensor(gt, imp_i, imp_j, ALU.is_gt))
                link(nc.vector.tensor_tensor(eq, imp_i, imp_j, ALU.is_equal))
                link(nc.vector.tensor_tensor(eq, eq, mask[:, M_CAUSAL:].rearrange("p (j i) -> p j i", j=NPICK), ALU.mult))
                link(nc.vector.tensor_tensor(gt, gt, eq, ALU.add))
                link(nc.vector.tensor_reduce(rank, gt, AX, ALU.add))
                link(nc.vector.memset(sneg, 0.0))
                link(nc.vector.tensor_scalar(sneg[:, 1:1 + NPICK], rank, float(TOP), NEG, ALU.is_ge, ALU.mult))
                dve.wait_ge(sem("gate_s_in"), 16 * 12)
                link(nc.vector.tensor_scalar(S_cmp, S_cmp, gate_s[:, 0:1], None, ALU.mult))
                for h in range(CH):
                    own = const[:, C_ROW + h:C_ROW + h + 1]
                    ins = nc.vector.tensor_scalar(P_exp[:, :, h, :], S_cmp.rearrange("p (a i) -> p a i", a=4), own, None, ALU.mult)
                link(ins)
                dve.sem_inc(step("pexp_ready"), 1)


            def k_odd(steps):
                for k in steps:
                    if k % 32 == 1 and k > 32:
                        take_scores(k // 32 - 1)
                    if k % 2 == 1:
                        dve.wait_ge(sem("kt_T"), 8 + k + 1)
                        if k >= CH:
                            dve.wait_ge(sem("kt_used"), k - CH + 1)
                        nc.vector.tensor_copy(KTc[:, k % CH, :], XB[1 + k % 3][:, :]).then_inc(sem("kt_odd"), 1)

            def take_scores(c):
                dve.wait_ge(sem("kt_used"), 32 * c + 32)
                src = XB[0][:, :]
                if c < 4:
                    nc.vector.tensor_tensor(S_sel[:, 512 * c:512 * c + 512].rearrange("p (j n) -> p j n", j=8),
                                            src.rearrange("p (j n) -> p j n", j=8),
                                            over(sneg[:, 8 * c:8 * c + 8].rearrange("p (j o) -> p j o", o=1), [P, 8, SB_]),
                                            ALU.add).then_inc(sem("S_taken"), 1)
                else:
                    link(nc.vector.tensor_copy(S_win, src))

            sc_scores()
            cu_scores(0)
            cu_scores(1)
            sc_probs()
            cu_probs(0)
            for u in range(32):
                if u == K_FROM - 2:
                    sc_ranks()
                before, after = k_steps(u)
                k_odd(before)
                if u + 1 < 32:
                    cu_probs(u + 1)
                k_odd(after[:2])
                if u + 2 < 32:
                    cu_scores(u + 2)
                k_odd(after[2:])
            take_scores(4)
            for br, s_br in enumerate((S_sel, S_win)):
                if br == 0:
                    dve.wait_ge(sem("S_taken"), 4)
                link(nc.vector.tensor_scalar(s_br, s_br, SCALE, None, ALU.mult))
                link(nc.vector.tensor_reduce(mx_c[:, 1 + br:2 + br], s_br, AX, ALU.max))
                link(nc.vector.tensor_tensor(mx_c[:, 1 + br:2 + br], mx_c[:, 1 + br:2 + br], s_new[:, br:br + 1], ALU.max))
                link(nc.vector.tensor_scalar(mx_c[:, 1 + br:2 + br], mx_c[:, 1 + br:2 + br], -1.0, None, ALU.mult))
                dve.sem_inc(sem("sw_max"), 1)
            dve.wait_ge(sem("sw_exp"), 4)
            link(nc.vector.tensor_tensor(rd_c[:, 1:3], den_c[:, 1:3], p_new, ALU.add))
            link(nc.vector.reciprocal(rd_c[:, 1:3], rd_c[:, 1:3]))
            link(nc.vector.tensor_tensor(rd_c[:, 1:3], rd_c[:, 1:3], gate_s[:, 1:3], ALU.mult))
            link(nc.vector.tensor_tensor(p_new, p_new, rd_c[:, 1:3], ALU.mult))
            link(nc.vector.tensor_scalar(S_sel, S_sel, rd_c[:, 1:2], None, ALU.mult))
            link(nc.vector.tensor_scalar(S_win, S_win, rd_c[:, 2:3], None, ALU.mult))
            for br in range(2):
                link(nc.vector.tensor_scalar(diag_c[:, br, :], ident, p_new[:, br:br + 1], None, ALU.mult))
            dve.sem_inc(step("sw_p"), 1)
            dve.wait_ge(*done("vn_made"))
            for br, slot in enumerate((28, 36)):
                dst = vnew if br == 0 else diag_c[:, 0, :]
                for g in range(GQ):
                    ins = nc.vector.tensor_tensor(dst.rearrange("p (h b g) -> p g h b", h=CH, b=B)[:, g],
                                                  XB[2][:, tileT(br)].rearrange("p (h b g) -> p g h b", h=CH, b=B)[:, g],
                                                  proj[:, slot:slot + 4, S:T], ALU.mult)
                link(ins)
            link(nc.vector.tensor_tensor(vnew, vnew, diag_c[:, 0, :], ALU.add))
            dve.sem_inc(step("vnew_set"), 1)
            vn4 = vnew.rearrange("p (h b g) -> p b h g", h=CH, b=B)
            with dve.Fori(0, 4) as i:
                for b2 in range(2):
                    dve.wait_ge(sem("set_used"), i * 10 + (2 + 5 * b2 + 5))
                    nc.vector.tensor_copy(O_c[:, b2, :], XB[b2][:, 0:P]).then_inc(sem("O_taken"), 1)
                    dve.wait_ge(sem("OT_made"), i * 2 + (b2 + 1))
                    src = XB[2 + b2][:, 0:P].rearrange("p (h b g) -> p b h g", h=CH, b=B)[:, bass.ds(i * 2 + b2, 1)].rearrange("p o h g -> p (o h) g")
                    new = vn4[:, bass.ds(i * 2 + b2, 1)].rearrange("p o h g -> p (o h) g")
                    dst = proj[:, 40:56, bass.ds(i * 2 + (b2 + S), 1)].rearrange("p (h g) o -> p h (g o)", h=CH)
                    nc.vector.tensor_tensor(dst, src, new, ALU.add).then_inc(sem("OT_taken"), 1)
            dve.wait_ge(sem("OT_taken"), 2 + B)
            dve.wait_ge(sem("proj_free"), 4 + 160)
            for n in range(2):
                a = slice(8 * n, 8 * n + 8)
                nc.vector.tensor_tensor(r0[:, a, :], proj[:, 40 + 8 * n:48 + 8 * n, :], proj[:, a, :], ALU.mult).then_inc(sem("cat1"), 1)
            add_mix(r1, 160, False)
            gated(1, r1, r0, 176)

        @block.tensor
        def _(pe):
            pe.wait_ge(sem("consts_in"), 16)
            pe.wait_ge(sem("gains_in"), 16 * 7)
            nc.tensor.transpose(XB[3][:, 0:NG], scr[0:NG, 7, 0:P], ident[0:NG, 0:NG]).then_inc(sem("xT_made"), 1)
            pe.wait_ge(sem("x_in"), 96)
            for c in range(KC + 2):
                src, k = (x_nat, c) if c < KC else (p_nat, c - KC)
                if c == 3:
                    pe.wait_ge(sem("gains_set"), 1)
                if c >= 4:
                    pe.wait_ge(sem("xT_taken"), c - 3)
                for t in range(3):
                    rows = P if t < 2 else B
                    ins = nc.tensor.transpose(XB[c % 4][:, t * P:t * P + rows], src[0:rows, t, tileT(k)], ident[0:rows, 0:rows])
                ins.then_inc(sem("xT_made"), 1)
            pe.wait_ge(sem("ones_set"), 2)
            pe.wait_ge(sem("xT_taken"), KC + 2)

            def rms(layer, sq):
                for c in range(KC):
                    pe.wait_ge(sem(f"rms_sq{layer}"), c + 1)
                    ins = nc.tensor.matmul(XB[0][:, 0:T], ones[:, :], sq[:, c, :], start=(c == 0), stop=(c == KC - 1))
                ins.then_inc(sem(f"rms_sum{layer}"), 1)

            rms(0, r1)

            def columns(x, bl, tiles, loads, beside=None):
                for hf in range(2):
                    q = 2 * (bl % 2) + hf
                    pe.wait_ge(sem(f"w_in{q}"), loads * 16 + 16)
                    for c in range(2):
                        if hf == 0:
                            pe.wait_ge(sem("proj_free"), tiles + (c + 1))
                        for k in range(HB):
                            ins = nc.tensor.matmul(PJ[(2 * bl + c) % 4][:, 0:T], wring[:, q, k, tileT(c)],
                                                   x[:, hf * HB + k, :], start=(hf == 0 and k == 0),
                                                   stop=(hf == 1 and k == HB - 1))
                            if k == HB - 1 and hf == 1:
                                ins.then_inc(sem("proj_made"), 1)
                            elif k == HB - 1 and c == 1:
                                ins.then_inc(sem("w_used"), 1)
                            if k % 4 == 3 and beside is not None:
                                beside(4 * hf + 2 * c + k // 4)

            def projection(x, first, rounds, beside=None):
                with pe.Fori(0, rounds) as i:
                    for bl in range(4):
                        columns(x, bl, i * 8 + (2 * first + 2 * bl), i * 2 + (first // 2 + bl // 2),
                                beside and (lambda s: beside(i, bl, s)))

            def compress(r, bl, n, free, loads):
                pg = 4 * bl + n
                pe.wait_ge(sem(f"c_in{n}"), r * 64 + (16 * loads + 16 * (bl + 1)))
                if pg == 0:
                    pe.wait_ge(sem("cmp_free"), r + free)
                for v in range(2):
                    for lo, grp in ([(0, pg // 4 - 1)] if n == 0 and pg else []) + [(32 - 8 * (pg % 4), pg // 4)]:
                        for h in range(CH):
                            ins = nc.tensor.matmul(XB[v][32 * h:32 * h + 32, tileT(grp)], wide[:, v, lo:lo + 32, h],
                                                   cring[:, n, (v * CH + h) * P:(v * CH + h + 1) * P],
                                                   start=(pg == 0), stop=(pg == NPG - 1), skip_group_check=True)
                ins.then_inc(sem("c_used"), 1)

            pe.wait_ge(sem("xn_ready0"), KC)
            pe.wait_ge(sem("wide_in"), 16 * 32)

            def ab1_round(r, norm):
                for bl in range(4):
                    def beside(s):
                        if s % 2 == 1:
                            compress(r, bl, s // 2, 1, 0)
                        if s == SLOTS - 1 and norm:
                            pe.wait_ge(sem("qn_sq"), (r - 1) * 4 + (bl + 1))
                            pe.wait_ge(sem("qn_root"), (r - 1) * 8 + (2 + 2 * bl))
                            for c in range(2):
                                nc.tensor.matmul(XB[2 + c][:, 0:T], ones[:, :], scr[:, 2 * bl + c, :], start=True, stop=True)\
                                  .then_inc(sem("qn_sum"), 1)
                    columns(r1, bl, r * 8 + 2 * bl, r * 2 + bl // 2, beside)

            ab1_round(0, False)
            with pe.Fori(0, 3) as i:
                ab1_round(i + 1, True)
            ab1_round(4, True)

            def natural(t):
                if t == 0:
                    pe.wait_ge(sem("cmp_free"), 6)
                    pe.wait_ge(sem("qn_root"), 2 + 32)
                    pe.wait_ge(sem("proj_free"), 4 + 40)
                if t == 8:
                    pe.wait_ge(sem("qn_done"), 4 + 16)
                if t >= 4:
                    pe.wait_ge(sem("nat_taken"), 2 * (t - 3))
                for c in range(3):
                    rows = P if c < 2 else B
                    ins = nc.tensor.transpose(XB[t % 4][0:rows, tileT(c)], proj[:, (32 + t if t < 8 else 16 + t), c * P:c * P + rows], ident)
                ins.then_inc(sem("nat_made"), 1)

            def pa_scores(u):
                h, qt = u // 2, u % 2
                if u >= 2:
                    pe.wait_ge(sem("pa_max"), u - 1)
                for g in range(AG):
                    nk = P * (qt + 1)
                    out = XB[0][:, g * P:(g + 1) * P] if qt == 0 else XB[1 + g // 2][:, (g % 2) * 256:(g % 2) * 256 + 256]
                    ins = nc.tensor.matmul(out, proj[:, 8 * g + h, tileT(qt)], proj[:, 24 + h, 0:nk], start=True, stop=True)
                ins.then_inc(sem("pa_s"), 1)

            def pa_probs(u):
                qt = u % 2
                pe.wait_ge(sem("pa_p"), u + 1)
                if u >= 1:
                    pe.wait_ge(sem("pa_o_taken"), u)
                for k in range(qt + 1):
                    ins = nc.tensor.transpose(XB[3][:, tileT(k)], S_sb[:, qt, tileT(k)], ident)
                ins.then_inc(sem("pa_pT"), 1)

            def pa_values(u):
                h, qt = u // 2, u % 2
                pe.wait_ge(sem("pa_pT_taken"), u + 1)
                for k in range(qt + 1):
                    ins = nc.tensor.matmul(XB[3][:, 384:512], proj[:, 32 + h, tileT(k)], PT[:, qt, tileT(k)],
                                           start=(k == 0), stop=(k == qt))
                ins.then_inc(sem("pa_o"), 1)

            def dk_scores(n):
                b, g = n // AG, n % AG
                if n == 0:
                    pe.wait_ge(sem("qz_set"), 1)
                pe.wait_ge(sem("dk_T_taken"), n + 1)
                pe.wait_ge(sem("dk_T_taken2"), n + 1)
                for h in range(AH):
                    j = h % 4
                    ins = nc.tensor.matmul(XB[h // 4][32 * j:32 * j + B, tileT(g)], qz[:, g, b, h, :],
                                           KT[:, n % 2, tileT(h)], start=False, stop=True, skip_group_check=True)
                ins.then_inc(sem("c_used"), 1)

            def dk_T(n):
                if n == 0:
                    pe.wait_ge(sem("pa_o_taken"), 16)
                    for u in range(2):
                        nc.tensor.matmul(XB[u][:, :], zrow[0:1, 0:P], zrow[0:1, :], start=True, stop=True)
                pe.wait_ge(sem(f"c_in{n % NP}"), 16 * (20 + n // NP + 1))
                for h in range(AH):
                    ins = nc.tensor.transpose(XB[2 + h // 4][:, tileT(h % 4)], cring[:, n % NP, tileT(h)], ident)
                ins.then_inc(sem("dk_T"), 1)

            def d_new_scores():
                for g in range(AG):
                    for u in range(2):
                        ins = nc.tensor.matmul(XB[u][:, 384 + g:385 + g], prod[:, g, u, :], ones[:, 0:1],
                                               start=False, stop=True, skip_group_check=True)
                ins.then_inc(sem("d_s"), 1)

            def d_probs():
                pe.wait_ge(sem("d_p"), 1)
                for g in range(AG):
                    for u in range(2):
                        ins = nc.tensor.transpose(XB[2 + g // 2][:, (g % 2) * 256 + u * P:(g % 2) * 256 + (u + 1) * P],
                                                  Sd[:, u, tileT(g)], ident)
                ins.then_inc(sem("d_pT"), 1)
                for u in range(2):
                    ins = nc.tensor.matmul(XB[1][:, tileT(u)], ones[:, :], diag[:, u, :], start=True, stop=True)
                ins.then_inc(sem("d_new"), 1)

            def dO_T(b):
                pe.wait_ge(sem("dO_taken"), b + 1)
                if b >= 2:
                    pe.wait_ge(sem("oTd"), b - 1)
                for u in range(2):
                    ins = nc.tensor.transpose(XB[2 + b % 2][:, tileT(u)], Od[:, b % 2, tileT(u)], ident)
                ins.then_inc(sem("dO_T"), 1)

            def dv(n):
                b, g = n // AG, n % AG
                if n == 0:
                    pe.wait_ge(sem("d_pT_taken"), 2)
                    pe.wait_ge(sem("d_new_taken"), 1)
                if b >= 2:
                    pe.wait_ge(sem("dO_taken"), b - 1)
                pe.wait_ge(sem(f"c_in{n % NP}"), 16 * (26 + n // NP + 1))
                for h in range(AH):
                    u, j = h // 4, h % 4
                    ins = nc.tensor.matmul(XB[b % 2][32 * j:32 * j + 32, tileT(u)], PTd[:, g, u, 32 * j:32 * j + 32],
                                           cring[:, n % NP, tileT(h)], start=(g == 0 and u == 0), stop=(g == AG - 1),
                                           skip_group_check=True)
                ins.then_inc(sem("c_used"), 1)

            def ln_mean():
                pe.wait_ge(sem("proj_free"), 4 + 64)
                pe.wait_ge(sem("dO_taken"), B)
                for g in range(8):
                    ins = nc.tensor.matmul(XB[0][:, 0:T], ones[:, :], xc[:, g, :], start=(g == 0), stop=(g == 7))
                ins.then_inc(sem("ln_sum"), 1)

            def ws_T():
                pe.wait_ge(sem("ws_in"), 32)
                pe.wait_ge(sem("oTd"), B)
                for g in range(8):
                    ins = nc.tensor.transpose(XB[2 + g // 4][:, tileT(g % 4)], ws_nat[:, g, :], ident)
                    if g % 4 == 3:
                        ins.then_inc(sem("ws_T"), 1)

            def ln_var():
                pe.wait_ge(sem("ln_sq"), 1)
                for g in range(8):
                    ins = nc.tensor.matmul(XB[1][:, 0:T], ones[:, :], sq8[:, g, :], start=(g == 0), stop=(g == 7))
                ins.then_inc(sem("ln_sum"), 1)

            def first_weights():
                pe.wait_ge(sem("wsT_set"), 2)
                nc.tensor.matmul(XB[2][:, 0:8], ones[0:1, :], wsT[0:1, :, 0], start=True, stop=True)
                nc.tensor.matmul(XB[2][:, 8:16], ones[0:1, :], bs.rearrange("p (g t) -> p g t", g=8)[:, :, 0],
                                 start=True, stop=True).then_inc(sem("w00_made"), 1)

            def vn_T(g):
                pe.wait_ge(sem("vn_ready"), 1)
                if g >= 2:
                    pe.wait_ge(sem("vn_taken"), 2 * (g - 1))
                for c in range(3):
                    rows = P if c < 2 else B
                    ins = nc.tensor.transpose(XB[g % 2][0:rows, tileT(c)], xc[:, g, c * P:c * P + rows], ident)
                ins.then_inc(sem("vn_T"), 1)

            def beside_ab2(s):
                if s < PA_AT:
                    natural(2 * s)
                    natural(2 * s + 1)
                    if s == PA_AT - 1:
                        pe.wait_ge(sem("nat_taken"), 32)
                        pa_scores(0)
                        pa_scores(1)
                elif s < PA_AT + 48:
                    u, part = (s - PA_AT) // 3, (s - PA_AT) % 3
                    if part == 0:
                        pa_probs(u)
                    elif part == 1:
                        pa_values(u)
                        if u + 2 < 16:
                            pa_scores(u + 2)
                elif DK_AT <= s <= DK_AT + AG * B:
                    if s > DK_AT:
                        dk_scores(s - DK_AT - 1)
                    if s < DK_AT + AG * B:
                        dk_T(s - DK_AT)
                elif s == DS_AT:
                    d_new_scores()
                elif s == DP_AT:
                    d_probs()
                elif DV_AT <= s < DV_AT + AG * B:
                    dv(s - DV_AT)
                    b, g = (s - DV_AT) // AG, (s - DV_AT) % AG
                    if g == 1 and b >= 1:
                        dO_T(b - 1)
                elif s == LN_AT - 1:
                    dO_T(B - 1)
                elif s == LN_AT:
                    ln_mean()
                elif s == LN_AT + 1:
                    ws_T()
                elif s == LN_AT + 4:
                    ln_var()
                elif s == LN_AT + 5:
                    first_weights()
                elif VN_AT <= s < VN_AT + 4:
                    vn_T(2 * (s - VN_AT))
                    vn_T(2 * (s - VN_AT) + 1)

            for m in range(16):
                columns(r1, m % 4, 40 + 2 * m, 10 + m // 2, lambda s: beside_ab2(m * SLOTS + s))
            pe.wait_ge(sem("vn_taken"), 16)
            pe.wait_ge(sem("w00_taken"), 1)
            for g in range(8):
                if g >= 4:
                    pe.wait_ge(sem("mixed"), g - 3)
                for c in range(2):
                    nc.tensor.matmul(XB[g % 4][:, tileT(c)], vn_nat[:, c, tileT(g)], wsT[:, g, :], start=True, stop=False)
                    ins = nc.tensor.matmul(XB[g % 4][:, tileT(c)], ones[0:1, :], bs[:, tileT(g)], start=False, stop=True)
                ins.then_inc(sem("mix_made"), 1)

            pe.wait_ge(sem("cat0"), 4)

            def beside_out(r, bl, s):
                if s % 2 == 1:
                    compress(r, bl, s // 2, 6, 32)
            projection(r1, OUT0, 2, beside_out)
            pe.wait_ge(sem("cmp_free"), 8)

            def ple(layer):
                pe.wait_ge(sem("wple_in"), 16 * (layer + 1))
                for c in range(KC):
                    if c >= 4:
                        pe.wait_ge(sem(f"ple_taken{layer}"), c - 3)
                    for k in range(2):
                        ins = nc.tensor.matmul(XB[c % 4][:, 0:T], wple[:, k, tileT(c)], pT[:, k, :], start=(k == 0), stop=(k == 1))
                    ins.then_inc(sem(f"ple_made{layer}"), 1)
            ple(0)
            pe.wait_ge(sem("proj_free"), 4 + 88)
            pe.wait_ge(sem("ple_taken0"), KC)
            for m in range(8):
                columns(r0, m % 4, 2 * (GATE0 + m), (GATE0 + m) // 2, (lambda s: beside_out(2, m, s)) if m < 4 else None)
            pe.wait_ge(sem("cmp_free"), 9)

            pe.wait_ge(sem("p_in"), 48)
            pe.wait_ge(sem("ple_taken0"), KC)
            for k in range(2):
                for c in range(3):
                    rows = P if c < 2 else B
                    ins = nc.tensor.transpose(XB[1 + k][:, c * P:c * P + rows], p_nat[0:rows, c, tileT(k)], ident[0:rows, 0:rows])
                ins.then_inc(sem("pT_made"), 1)
            rms(1, r0)
            pe.wait_ge(sem("pT_taken"), 2)
            pe.wait_ge(sem("xn_ready1"), KC)
            pe.wait_ge(sem("proj_free"), 4 + 104)

            def kcT(b):
                pe.wait_ge(*done("kc_ready"))
                if b >= 2:
                    pe.wait_ge(sem("kcT_taken"), b - 1)
                for a in range(4):
                    ins = nc.tensor.transpose(XB[b % 2][:, tileT(a)], kcmp[:, b, a, :], ident)
                ins.then_inc(sem("kcT_made"), 1)

            def cn_sums(p, odd):
                pe.wait_ge(sem("cn_sq"), p + 1)
                pe.wait_ge(sem("cn_root"), p * 2 + 2)
                for c in range(2):
                    nc.tensor.matmul(XB[2 + c][:, 0:T], ones[:, :], scr[:, 2 * odd + c, :], start=True, stop=True)\
                      .then_inc(sem("cn_sum"), 1)

            def natural_c(n):
                t = NAT[n]
                if n == 0:
                    pe.wait_ge(sem("kcT_taken"), B)
                if n == 12:
                    pe.wait_ge(sem("cn_done"), 2 + 10)
                if n == 16:
                    pe.wait_ge(sem("cn_root"), 2 + 24)
                    pe.wait_ge(sem("proj_free"), 4 + 144)
                if n == 20:
                    pe.wait_ge(sem("cn_done"), 2 + 12)
                if n >= 2:
                    pe.wait_ge(sem("cnat_taken"), 2 * (n - 1))
                for c in range(3):
                    rows = P if c < 2 else B
                    ins = nc.tensor.transpose(XB[n % 2 + (2 if n >= 16 else 0)][0:rows, tileT(c)],
                                              proj[:, 16 + t, c * P:c * P + rows], ident)
                ins.then_inc(sem("cnat_made"), 1)

            def cq_block(r, bl, beside):
                columns(r0, bl, r * 8 + (2 * CQ + 2 * bl), r * 2 + (CQ // 2 + bl // 2), beside)

            def beside_q(bl, s):
                if bl >= 2 and s in (5, 7):
                    for b in range(2):
                        kcT(4 * (bl - 2) + s - 5 + b)

            for bl in range(4):
                cq_block(0, bl, lambda s: beside_q(bl, s))
            with pe.Fori(0, 2) as i:
                for bl in range(4):
                    cq_block(i + 1, bl, lambda s: cn_sums(i * 4 + bl, bl % 2) if s == SLOTS - 1 else None)

            def beside_rows(r, bl, s):
                if bl < 2 and s % 2 == 1:
                    natural_c(8 * (r - 3) + 4 * bl + s // 2)
                elif bl >= 2 and s == SLOTS - 1:
                    cn_sums(8 + 2 * (r - 3) + bl - 2, bl % 2)
                elif r == 4 and bl == 2 and s == 3:
                    compress_prompt()

            def compress_prompt():
                pe.wait_ge(sem("cnat_taken"), 32)
                for pg in range(2):
                    lo = 32 - 8 * pg
                    for h in range(CH):
                        nc.tensor.matmul(XB[0][32 * h:32 * h + 32, 0:P], wide[:, 0, lo:lo + 32, h], proj[:, 16 + h, tileT(pg)],
                                         start=(pg == 0), stop=(pg == 1), skip_group_check=True)
                        ins = nc.tensor.matmul(XB[1][0:32, tileT(h)], wide[:, 1, lo:lo + 32, h], proj[:, 20 + h, tileT(pg)],
                                               start=(pg == 0 and h == 0), stop=(pg == 1), skip_group_check=True)
                ins.then_inc(step("pc_made"), 1)

            for r in (3, 4):
                for bl in range(4):
                    cq_block(r, bl, lambda s: beside_rows(r, bl, s))
            for n in range(16, 20):
                natural_c(n)
            pe.wait_ge(sem("wg_in"), 16)
            for k in range(KC):
                ins = nc.tensor.matmul(PJ[0][0:48, 0:T], wg[:, k, :], r0[:, k, :], start=(k == 0), stop=(k == KC - 1))
            ins.then_inc(step("gT_made"), 1)
            for n in range(20, 24):
                natural_c(n)
            pe.wait_ge(sem("gT_set"), 1)
            for c in range(3):
                rows = P if c < 2 else B
                ins = nc.tensor.transpose(PJ[1][0:rows, 64 * c:64 * c + 48], gT[:, c * P:c * P + rows], ident[0:48, 0:48])
            ins.then_inc(step("gate_made"), 1)
            pe.wait_ge(*done("kcp_ready"))
            pe.wait_ge(sem("vcp_set"), 1)
            nc.tensor.transpose(XB[1][:, 0:P], kcp, ident).then_inc(step("kcpT_made"), 1)
            pe.wait_ge(*done("kcpT_set"))
            pe.wait_ge(sem("cnat_taken"), 48)
            pe.wait_ge(sem("gate_taken"), 3)
            for n in range(8):
                if n >= 4:
                    pe.wait_ge(sem("pcs_taken"), n - 3)
                for g in range(GQ):
                    ins = nc.tensor.matmul(XB[n % 4][:, tileT(g)], proj[:, 4 * (n % 4) + g, tileT(n // 4)], kcpT, start=True, stop=True)
                ins.then_inc(sem("pcs_made"), 1)
            pe.wait_ge(sem("pcs_taken"), 8)

            pe.wait_ge(*done("qz_c"))
            for b in range(B):
                for h in range(CH):
                    nc.tensor.matmul(XB[0][32 * h:32 * h + 32, 0:P].rearrange("p (a i) -> p a i", a=4), qzu[:, b, h, :],
                                     kcmp[:, b, :, 32 * h:32 * h + 32], start=(b == 0), stop=(b == B - 1), skip_group_check=True)
            for br in range(2):
                ins = nc.tensor.matmul(XB[1][:, br:br + 1], diag_c[:, br, :], ones[:, 0:1], start=True, stop=True)
            ins.then_inc(step("scmp_made"), 1)

            def cu_scores(u):
                hq, qt = u // 2, u % 2
                nk = P * (qt + 1)
                if u >= 2:
                    pe.wait_ge(sem("cu_max"), u - 1)
                for br, slot in enumerate((24, 32)):
                    ins = nc.tensor.matmul(PJ[qt][:, br * nk:(br + 1) * nk], proj[:, 40 + hq, tileT(qt)],
                                           proj[:, slot + hq // GQ, 0:nk], start=True, stop=True)
                ins.then_inc(sem("cu_s"), 1)

            def cu_probs(u):
                hq, qt = u // 2, u % 2
                pe.wait_ge(sem("cu_p"), u + 1)
                if u >= 1:
                    pe.wait_ge(sem("cu_o_taken"), u)
                nc.tensor.transpose(PJ[3][0:16, 0:P], Pc[:, 16 * qt + hq, :], ident)
                for k in range(2 * (qt + 1)):
                    ins = nc.tensor.transpose(PJ[2][:, tileT(k)], S_c[:, qt, tileT(k)], ident)
                ins.then_inc(sem("cu_pT"), 1)

            def cu_values(u):
                hq, qt = u // 2, u % 2
                h = hq // GQ
                pe.wait_ge(sem("cu_pT_taken"), 2 * u + 2)
                nc.tensor.matmul(PJ[3][:, P:2 * P], vcp[0:16, h, :], PcT[:, qt, :], start=True, stop=False)
                for k in range(2 * (qt + 1)):
                    br, kt = k // (qt + 1), k % (qt + 1)
                    ins = nc.tensor.matmul(PJ[3][:, P:2 * P], proj[:, (28, 36)[br] + h, tileT(kt)], PT_c[:, qt, tileT(k)],
                                           start=False, stop=(k == 2 * qt + 1))
                ins.then_inc(sem("cu_o"), 1)

            def key_scores(k):
                c, b, h = k // 32, k % 32 // CH, k % CH
                if k % 32 == 0 and c >= 1:
                    pe.wait_ge(sem("S_taken"), c)
                pe.wait_ge(sem("kt_odd" if k % 2 else "kt_even"), k // 2 + 1)
                nc.tensor.matmul(XB[0][32 * h:32 * h + 32, :], qzr[:, b, h, :], KTc[:, h, :],
                                 start=(b == 0), stop=(b == B - 1), skip_group_check=True).then_inc(sem("kt_used"), 1)

            def keys(steps):
                for k in steps:
                    n, h = k // CH, k % CH
                    if h == 0:
                        pe.wait_ge(sem(f"set_in{n % 2}"), 64 * (n // 2 + 1))
                    if k >= 3:
                        pe.wait_ge(sem("kt_even" if k % 2 else "kt_odd"), (k - 3) // 2 + 1)
                    for q in range(4):
                        ins = nc.tensor.transpose(XB[1 + k % 3][:, tileT(q)], hring[:, 4 * (n % 2) + q, tileT(h)], ident)
                    ins.then_inc(sem("kt_T"), 1)
                    if k >= 1:
                        key_scores(k - 1)

            pe.wait_ge(*done("pc_p"))
            cu_scores(0)
            cu_scores(1)
            pe.wait_ge(*done("scmp_p"))
            nc.tensor.matmul(XB[0][:, 128:256], S_cmp, const[:, C_GRP:C_GRP + P], start=True, stop=True).then_inc(step("psum_made"), 1)
            for u in range(32):
                if u == K_FROM - 1:
                    pe.wait_ge(*done("pexp_ready"))
                    for a in range(4):
                        ins = nc.tensor.transpose(XB[3][:, tileT(a)], P_exp[:, a].rearrange("p h i -> p (h i)"), ident)
                    ins.then_inc(step("ptexp_made"), 1)
                if u == K_FROM:
                    pe.wait_ge(sem("ptexp_taken"), 1)
                before, after = k_steps(u)
                cu_probs(u)
                keys(before)
                cu_values(u)
                if u + 2 < 32:
                    cu_scores(u + 2)
                keys(after)
                if u == 0:
                    pe.wait_ge(sem("psum_taken"), 1)
                    nc.tensor.matmul(XB[1][:, 0:NPICK], P_sum[0:NCMP, :], const[0:NCMP, C_C2S:C_C2S + NPICK], start=True, stop=True)\
                      .then_inc(step("imp_made"), 1)
            key_scores(K_STEPS - 1)
            pe.wait_ge(sem("cu_o_taken"), 32)
            pe.wait_ge(*done("sw_p"))
            for q in range(5):
                if q == 4:
                    pe.wait_ge(sem("sw_pT_taken"), 1)
                for a in range(4):
                    src = S_sel[:, tileT(4 * q + a)] if q < 4 else S_win[:, tileT(a)]
                    ins = nc.tensor.transpose(XB[q % 4][:, tileT(a)], src, ident)
                ins.then_inc(sem("sw_pT"), 1)
            pe.wait_ge(sem("sw_pT_taken"), 5)
            for br in range(2):
                ins = nc.tensor.matmul(XB[2][:, tileT(br)], ones[:, :], diag_c[:, br, :], start=True, stop=True)
            ins.then_inc(step("vn_made"), 1)
            pe.wait_ge(*done("vnew_set"))
            def first_values(i, b2):
                for a in range(4):
                    nc.tensor.matmul(XB[b2][:, 0:P], PT_exp[:, a, :], vcmp[:, bass.ds(i * 2 + b2, 1), a, :].rearrange("p o d -> p (o d)"),
                                     start=(a == 0), stop=False, skip_group_check=True)

            def values(i, b2, k):
                n = 5 * b2 + k
                pe.wait_ge(sem(f"set_in{n % 2}"), i * 320 + (20 * 64 + 64 * (n // 2 + 1)))
                for q in range(4):
                    lhs = PT_sel[:, 4 * k + q, :] if k < 4 else PT_win[:, q, :]
                    for h in range(CH):
                        ins = nc.tensor.matmul(XB[b2][32 * h:32 * h + 32, 0:P], lhs[:, 32 * h:32 * h + 32],
                                               hring[:, 4 * (n % 2) + q, tileT(h)], start=False,
                                               stop=(k == 4 and q == 3), skip_group_check=True)
                ins.then_inc(sem("set_used"), 1)

            def beside_z(i, b2, s):
                if s == 0:
                    pe.wait_ge(sem("OT_taken"), i * 2 + (b2 + 1))
                    first_values(i, b2)
                if s < 5:
                    values(i, b2, s)
                if s == 6:
                    pe.wait_ge(sem("O_taken"), i * 2 + (b2 + 1))
                    nc.tensor.transpose(XB[2 + b2][:, 0:P], O_c[:, b2, :], ident).then_inc(sem("OT_made"), 1)

            with pe.Fori(0, 4) as i:
                for b2 in range(2):
                    columns(r0, b2, i * 4 + (2 * CZ + 2 * b2), i + CZ // 2, lambda s: beside_z(i, b2, s))
            pe.wait_ge(sem("cat1"), 2)
            projection(r0, OUT1, 2)
            ple(1)
            pe.wait_ge(sem("proj_free"), 4 + 176)
            projection(r1, GATE1, 2)
            for c in range(KC):
                if c >= 4:
                    pe.wait_ge(sem("y_taken"), 2 * (c - 3))
                if c == 0:
                    pe.wait_ge(sem("ple_taken1"), KC)
                pe.wait_ge(sem("h_new1"), 4 + c + 1)
                for a in range(3):
                    rows = P if a < 2 else B
                    ins = nc.tensor.transpose(XB[c % 4][0:rows, tileT(a)], r0[:, c, a * P:a * P + rows], ident)
                ins.then_inc(sem("y_made"), 1)


_OUTS = [("y_prompt", (1, S, D)), ("y_sample", (B, 1, D)),
         ("new_a_kv_prompt", (1, 1, 2, S, AH, P)), ("new_a_kv_sample", (B, 1, 2, 1, AH, P)),
         ("state_b_v_prompt", (1, 1, P, D // 2)), ("state_b_v_sample", (B, 1, 1, D // 2)),
         ("new_c_cmp_kv_prompt", (1, 1, 2, S, CH, P)), ("new_c_cmp_kv_sample", (B, 1, 2, 1, CH, P)),
         ("new_c_sel_kv_prompt", (1, 1, 2, S, CH, P)), ("new_c_sel_kv_sample", (B, 1, 2, 1, CH, P)),
         ("new_c_win_kv_prompt", (1, 1, 2, S, CH, P)), ("new_c_win_kv_sample", (B, 1, 2, 1, CH, P))]


def kernel(**inputs):
    import numpy as _np
    import concourse.bacc as _bacc
    from concourse import mybir as _mybir
    from concourse.bass_utils import run_bass_kernel_spmd as _run

    nc = _bacc.Bacc("TRN2", target_bir_lowering=False, num_devices=1)
    arrays, dram = {}, {}
    const, mask_a, mask_c = shape_constants()
    given = dict(inputs, const=const, mask_a=mask_a, mask_c=mask_c)
    for name, a in given.items():
        a = _np.ascontiguousarray(a)
        arrays[f"in_{name}_dram"] = a
        dram[name] = nc.dram_tensor(f"in_{name}_dram", a.shape, _mybir.dt.from_np(a.dtype), kind="ExternalInput").ap()
    for name, shape in _OUTS:
        dram[name] = nc.dram_tensor(f"out_{name}_dram", shape, _mybir.dt.float32, kind="ExternalOutput").ap()
    hybrid_trunk(nc, dram)
    r = _run(nc, [arrays], core_ids=[0])
    return tuple(r.results[0][f"out_{name}_dram"] for name, _ in _OUTS)
```

```python
from contextlib import ExitStack

import numpy as np

import concourse.bass as bass
from concourse import mybir

ALU = mybir.AluOpType
ACT = mybir.ActivationFunctionType
F32 = mybir.dt.float32
F32R = mybir.dt.float32r
I32 = mybir.dt.int32
AX = mybir.AxisListType.X

P = 128
D = 2048
KC = D // P
S = 256
B = 8
T = S + B
PAST = 2048
NPG = PAST // P
AH = 8
PATTERNS = ((128, 1), (512, 4), (2048, 16))
AG = len(PATTERNS)
CH = 4
GQ = 4
HQ = CH * GQ
CKV = CH * P
CMP, SEG = 32, 16
NCMP = PAST // SEG - 1
NCP = S // SEG - 1
SB_ = 64
NSEL = PAST // SB_
NPICK = NSEL - 2
TOP = 16 - 3
WIN = 512
WT = WIN // P
PLE = 256
EPS = 1e-6
SCALE = float(P) ** -0.5
NEG = -1e30
TINY = 1e-30
HALF = 16
CB = 256
QB = KC // 4
NW = 4
EB = QB // 2
NE = 4
BLOCKS = 96
SLOTS = 8
NP = 4

C_ID = 0
C_GRP = C_ID + P
C_TRIL = C_GRP + P
C_COS = C_TRIL + P
C_SIN = C_COS + T
C_VIS = C_SIN + T
C_SEE = C_VIS + 32
C_C2S = C_SEE + 32
C_ROW = C_C2S + NPICK
C_END = C_ROW + CH
M_A = AG * 3 * P
M_CAUSAL = 3 * P
M_C = M_CAUSAL + NPICK * NPICK


def shape_constants():
    c = np.zeros((P, C_END), np.float32)
    i = np.arange(P)
    c[:, C_ID:C_ID + P] = np.eye(P)
    c[:, C_GRP:C_GRP + P] = (i[:, None] // GQ) == (i[None, :] // GQ)
    c[:, C_TRIL:C_TRIL + P] = i[:, None] <= i[None, :]
    pos = np.concatenate([np.arange(S), np.full(B, PAST)]).astype(np.float32)
    inv = np.exp((-np.log(np.float32(500000.0)) * np.arange(HALF, dtype=np.float32) / np.float32(HALF)).astype(np.float32)).astype(np.float32)
    ang = (pos[None, :] * inv[:, None]).astype(np.float32)
    cos, sin = np.cos(ang.astype(np.float64)), np.sin(ang.astype(np.float64))
    c[0:HALF, C_COS:C_COS + T] = cos
    c[HALF:2 * HALF, C_COS:C_COS + T] = cos
    c[0:HALF, C_SIN:C_SIN + T] = -sin
    c[HALF:2 * HALF, C_SIN:C_SIN + T] = sin
    for qt in range(2):
        see = (np.arange(16)[None, :] * SEG + CMP - 1 <= (qt * P + i)[:, None]) & (np.arange(16)[None, :] < NCP)
        c[:, C_VIS + 16 * qt:C_VIS + 16 * qt + 16] = np.where(see, 0.0, NEG)
        c[:, C_SEE + 16 * qt:C_SEE + 16 * qt + 16] = see
    n = np.arange(NCMP)[:, None]
    j = np.arange(1, NPICK + 1)[None, :]
    shared = np.minimum(n * SEG + CMP, (j + 1) * SB_) - np.maximum(n * SEG, j * SB_)
    c[:NCMP, C_C2S:C_ROW] = np.maximum(shared, 0) / CMP
    c[:, C_ROW:C_END] = (i[:, None] // 32) == np.arange(CH)[None, :]
    a = np.full((P, M_A), NEG, np.float32)
    m = np.zeros((P, M_C), np.float32)
    for qt in range(2):
        nk = P * (qt + 1)
        q, k = (qt * P + i)[:, None], np.arange(nk)[None, :]
        off = AG * P * qt
        for g, (window, dil) in enumerate(PATTERNS):
            ok = (k <= q) & (q - k <= window) & ((q - k) % dil == 0)
            a[:, off + g * nk:off + (g + 1) * nk] = np.where(ok, 0.0, NEG)
        m[:, P * qt:P * qt + nk] = np.where(k <= q, 0.0, NEG)
    e = np.arange(NPICK)
    m[:, M_CAUSAL:] = (e[None, None, :] < e[None, :, None]).reshape(1, -1)
    return c, a, m


def hybrid_trunk(nc, A):
    with ExitStack() as ctx:
        def sb(name, shape, dt=F32):
            return ctx.enter_context(nc.sbuf_tensor(name, shape, dt))

        def bank(name):
            return ctx.enter_context(nc.psum_tensor(name, [P, 512], F32))

        made = {}

        def sem(name):
            if name not in made:
                made[name] = ctx.enter_context(nc.semaphore(name))
            return made[name]

        PE_STEPS = ("pc_made", "gT_made", "gate_made", "kcpT_made", "scmp_made", "psum_made", "imp_made", "ptexp_made", "vn_made")
        DVE_STEPS = ("kc_ready", "kcp_ready", "kcpT_set", "pc_centred", "qz_c", "pc_p", "scmp_p", "pexp_ready", "sw_p", "vnew_set")

        def step(name):
            return sem("pe_steps" if name in PE_STEPS else "dve_steps")

        def done(name):
            steps = PE_STEPS if name in PE_STEPS else DVE_STEPS
            return step(name), steps.index(name) + 1

        const = sb("const", [P, C_END])
        mask = sb("mask", [P, M_C])
        ones = sb("ones", [P, P])
        zrow = sb("zrow", [1, 512])
        xh, xl = sb("xh", [P, KC, T], F32R), sb("xl", [P, KC, T], F32R)
        wring = sb("wring", [P, NW, QB, CB])
        w_up, w_low = sb("w_up", [P, NE, EB, CB], F32R), sb("w_low", [P, NE, EB, CB], F32R)
        proj = sb("proj", [P, 64, T])
        kcmp = sb("kcmp", [P, B, 4, P])
        vcmp = sb("vcmp", [P, B, 4, P])
        cring = sb("cring", [P, NP, 2 * CKV])
        scr = sb("scr", [P, 8, T])
        pT = sb("pT", [P, 2, T])
        small = sb("small", [P, 384])
        wide = sb("wide", [P, 2, 64, CH])
        ptab = sb("ptab", [1, B * NPG], I32)
        PJ = [bank(f"PJ{i}") for i in range(4)]
        XB = [bank(f"XB{i}") for i in range(4)]
        ident = const[:, C_ID:C_ID + P]
        cos, sin = const[0:32, C_COS:C_COS + T], const[0:32, C_SIN:C_SIN + T]

        at = [0]

        def cols(n):
            a = at[0]
            at[0] += n
            assert at[0] <= 384
            return small[:, a:a + n]
        NG = 2 * KC + 8 + 6
        gains = cols(NG)
        g_ab, g_c, g_sgu = gains[:, 0:KC], gains[:, KC:2 * KC], gains[:, 2 * KC:2 * KC + 8]
        g_qa, g_ka, g_qc = (gains[:, 2 * KC + 8 + n:2 * KC + 9 + n] for n in range(3))
        g_kc = gains[:, 2 * KC + 11:NG]
        eps = cols(1)
        nmx, den = cols(8), cols(8)
        rden, pnew = cols(8), cols(8)
        w00, b00 = cols(8), cols(8)
        lnt = sb("lnt", [P, 2, T])
        pnewT, lnr = lnt[:, 0, :], lnt[:, 1, :]
        vs_a = cols(AH * B)

        Z = proj[:, 40:64, :].rearrange("p a t -> p (a t)")
        x_nat = Z[:, 0:3 * D].rearrange("p (a n) -> p a n", a=3)
        p_nat = proj[:, 36:39, :].rearrange("p a t -> p (a t)")[:, 0:3 * PLE].rearrange("p (a n) -> p a n", a=3)
        p_nat1 = proj[:, 48:51, :].rearrange("p a t -> p (a t)")[:, 0:3 * PLE].rearrange("p (a n) -> p a n", a=3)

        w_ab = A["w_in_ab"][0].rearrange("(k p) n -> p k n", p=P)
        cmp_pool = A["cache_c_cmp_kv"].rearrange("n l v r h d -> n r (l v) (h d)")
        n_phys = A["cache_c_cmp_kv"].shape[0]

        AB1, AB2, OUT0, GATE0 = 0, 20, 36, 44
        CQ, CZ, OUT1, GATE1 = 52, 72, 80, 88
        CMP_A, AK, AV, CMP_B = 0, 80, 104, 128

        k_nat = proj[:, 48:56, :].rearrange("p a t -> p (a t)")[:, 0:2048].rearrange("p (t n) -> p t n", t=2)
        s_nat = proj[0:B, 56:64, :].rearrange("p a t -> p (a t)")[:, 0:2048].rearrange("p (v n) -> p v n", v=2)
        spare_k = kcmp[:, 5:8].rearrange("p b a r -> p (b a r)")
        spare_v = vcmp[:, 5:8].rearrange("p b a r -> p (b a r)")
        S_sb = spare_k.rearrange("p (u n) -> p u n", u=2)
        PT = spare_v[:, 0:512].rearrange("p (u n) -> p u n", u=2)
        qz = spare_k.rearrange("p (g b h m) -> p g b h m", g=AG, b=B, h=AH)
        prod = spare_v[:, 0:768].rearrange("p (g u r) -> p g u r", g=AG, u=2)
        diag = spare_v[:, 768:1024].rearrange("p (u r) -> p u r", u=2)
        W = proj[:, 8:32, :].rearrange("p a t -> p (a t)")
        KT = W[:, 0:2048].rearrange("p (u n) -> p u n", u=2)
        Sd = W[:, 2048:2832].rearrange("p (u n) -> p u n", u=2)
        PTd = W[:, 2832:3600].rearrange("p (g u r) -> p g u r", g=AG, u=2)
        Od = W[:, 3600:4112].rearrange("p (u n) -> p u n", u=2)

        PA_AT = 8
        DK_AT = PA_AT + 3 * 16 + 1
        DS_AT = DK_AT + AG * B + 1
        DP_AT = DS_AT + 4
        DV_AT = DP_AT + 2
        LN_AT = DV_AT + AG * B + 1
        VN_AT = LN_AT + 9

        xc = proj[:, 56:64, :]
        sq8 = proj[:, 8:16, :]
        vn_nat = sq8.rearrange("p a t -> p (a t)")[:, 0:2048].rearrange("p (t n) -> p t n", t=2)
        vn_s = proj[0:B, 16:20, :].rearrange("p a t -> p (a t)")[:, 0:1024]
        ws_nat = proj[:, 24:28, :].rearrange("p a t -> p (a t)")[:, 0:1024].rearrange("p (g s) -> p g s", g=8)
        wsT = proj[:, 20:24, :].rearrange("p a t -> p (a t)")[:, 0:1024].rearrange("p (g s) -> p g s", g=8)
        bs = proj[0:1, 28:32, :].rearrange("p a t -> p (a t)")[:, 0:1024]
        wple = proj[:, 32:48, :].rearrange("p a t -> p (a t)")[:, 0:4096].rearrange("p (k n) -> p k n", k=2)

        F = proj[:, 56:64, :].rearrange("p a t -> p (a t)")
        SC = scr[:, :, :].rearrange("p a t -> p (a t)")
        Q = proj[:, 0:16, :].rearrange("p a t -> p (a t)")
        KV = proj[:, 16:24, :].rearrange("p a t -> p (a t)")
        kst = F[:, 0:2048].rearrange("p (a t n) -> p a t n", a=2, t=2)
        c_nat = cring[0:B, 0:3, :].rearrange("p a (v n) -> p (a v) n", v=2)
        PAIRS = [2 * n for n in range(8)] + [24, 26, 32, 34]
        NAT = [v * CH + h for v in (0, 1, 3, 2, 5, 4) for h in range(CH)]
        wg = cring[:, 3, 0:16 * 48].rearrange("p (k n) -> p k n", k=16)
        gT = lnt[0:48, 0, :]
        gate_p = lnt[:, 1, 0:96].rearrange("p (t j h) -> p t j h", t=2, j=3)
        gate_8 = lnt[0:B, 1, 96:144]
        gate_s = lnt[:, 1, 144:147]
        kcp = SC[:, 0:128]
        kcpT = SC[:, 128:256]
        vcp = SC[0:32, 256:768].rearrange("p (h d) -> p h d", h=CH)
        Pc = SC[:, 768:1280].rearrange("p (u n) -> p u n", n=16)
        PcT = SC[0:16, 1280:1536].rearrange("p (u n) -> p u n", u=2)
        S_c = F[:, 0:1024].rearrange("p (u n) -> p u n", u=2)
        PT_c = F[:, 1024:2048].rearrange("p (u n) -> p u n", u=2)
        spare = wring[:, 2].rearrange("p k n -> p (k n)")
        qzu = spare[:, 0:1024].rearrange("p (b h m) -> p b h m", b=B, h=CH)
        qzr = Q[:, 0:1024].rearrange("p (b h m) -> p b h m", b=B, h=CH)
        S_sel = KV[:, 0:2048]
        KTc = wring[:, 2:4].rearrange("p q k n -> p (q k n)").rearrange("p (h n) -> p h n", h=CH)
        PT_sel = SC[:, 0:2048].rearrange("p (g r) -> p g r", g=NPG)
        S_win = Q[:, 1024:1536]
        S_cmp = Q[:, 1536:1664]
        P_sum = Q[:, 1664:1792]
        imp = Q[:, 1792:1792 + NPICK]
        rank = Q[:, 1824:1824 + NPICK]
        sneg = Q[:, 1856:1888]
        gt = Q[:, 1888:2788].rearrange("p (j i) -> p j i", j=NPICK)
        eq = Q[:, 2788:3688].rearrange("p (j i) -> p j i", j=NPICK)
        P_exp = Q[:, 1888:2400].rearrange("p (a h i) -> p a h i", a=4, h=CH)
        PT_exp = mask[:, M_CAUSAL:M_CAUSAL + 512].rearrange("p (a r) -> p a r", a=4)
        diag_c = Q[:, 3688:3944].rearrange("p (u r) -> p u r", u=2)
        O_c = KV[:, 0:256].rearrange("p (u d) -> p u d", u=2)
        PT_win = KV[:, 256:768].rearrange("p (a r) -> p a r", a=4)
        vnew = KV[:, 768:896]

        K_STEPS, K_FROM = 5 * 32, 3

        def k_steps(u):
            lo, hi = ((u + n - K_FROM) * K_STEPS // (32 - K_FROM) for n in range(2))
            return (range(lo, lo + 3), range(lo + 3, hi)) if u >= K_FROM else ((), ())

        s_new = cols(2)
        p_new = cols(2)
        mx_c, den_c, rd_c = cols(3), cols(3), cols(3)
        cmx = cols(32)
        kss, krt = cols(32), cols(32)
        y_nat = proj[:, 48:64, :].rearrange("p a t -> p (a t)")[:, 0:4096].rearrange("p (t n) -> p t n", t=2)
        y_s = proj[0:B, 32:40, :].rearrange("p a t -> p (a t)")[:, 0:2048]
        hring = cring[:, :, :].rearrange("p a (s n) -> p (a s) n", s=2)

        hs = proj[:, 16:32, :]
        resid = A["resid"].rearrange("p (k t) -> p k t", k=KC)
        tmp_n = proj[:, 0:16, :]
        cat = proj[:, 40:56, :]
        X0, CAT0, H0, X1, CAT1, H1 = range(6)

        def tileT(c):
            return slice(c * P, (c + 1) * P)

        def ahead(s):
            return (s + 3) // 8, (s + 3) % 8

        def root_a(p):
            return proj[:, 40 + 2 * (p % 4):42 + 2 * (p % 4), :]

        def root_c(p):
            return scr[:, 4 + 2 * (p % 2):6 + 2 * (p % 2), :]

        def raw(e):
            return wring[:, e // 2, e % 2 * EB:(e % 2 + 1) * EB, :]

        block = ctx.enter_context(nc.Block())

        @block.sync
        def _(sp):
            sp.dma_start(const[:, :], A["const"]).then_inc(sem("consts_in"), 16)
            r = 0
            for src in (A["ln_ab"][0], A["ln_c"][0], A["ln_sgu"][0], A["qn_a"][0], A["kn_a"][0], A["qn_c"][0],
                        A["kn_c"].rearrange("l k d -> (l k d)")):
                n = src.shape[0] // P
                sp.dma_start(scr[r:r + n, 7, 0:P], src.rearrange("(c p) -> c p", p=P)).then_inc(sem("gains_in"), 16)
                r += n
            for t in range(2):
                sp.dma_start(x_nat[:, t, :], A["x_prompt"][0, tileT(t), :]).then_inc(sem("x_in"), 16)
                sp.dma_start(p_nat[:, t, :], A["p_prompt"][0, 0, tileT(t), :]).then_inc(sem("x_in"), 16)
            sp.dma_start(x_nat[0:B, 2, :], A["x_sample"].rearrange("b s d -> b (s d)")).then_inc(sem("x_in"), 16)
            sp.dma_start(p_nat[0:B, 2, :], A["p_sample"][0].rearrange("b s d -> b (s d)")).then_inc(sem("x_in"), 16)
            sp.dma_start(ptab[:, :], A["page_table"].rearrange("(o b) n -> o (b n)", o=1)).then_inc(sem("ptab_in"), 16)
            sp.dma_start(mask[:, 0:M_A], A["mask_a"]).then_inc(sem("mask_a_in"), 16)
            sp.wait_ge(sem("wide_zero"), 1)
            for v, w in enumerate((A["cw_k"], A["cw_v"])):
                for n in range(8):
                    for half in range(2):
                        sp.dma_start(wide[SEG * n:SEG * (n + 1), v, 32 + n - half, :], w[0, SEG * half:SEG * (half + 1), :])\
                          .then_inc(sem("wide_in"), 16)
            sp.wait_ge(sem("xT_taken"), KC + 2)
            sp.dma_start(resid, hs).then_inc(sem("spilled"), 16)
            sp.wait_ge(sem("ptab_in"), 16)

            def quarter(n, w, i, bl, q, per=4):
                sp.wait_ge(sem("w_lo"), n * 8 + (2 * q + 2))
                sp.dma_start(wring[:, q], w[:, q * QB:(q + 1) * QB, bass.ds((i * per + bl) * CB, CB)])\
                  .then_inc(sem(f"w_in{q}"), 16)

            def page(i, n0, bl, n):
                pg = 4 * bl + n
                sp.wait_ge(sem("c_used"), i * 16 + (4 * bl + n + 1 + (16 * n0 if n0 == 0 else CMP_B)))
                at = sp.value_load(ptab[0:1, bass.ds(i * NPG + (n0 * NPG + pg), 1)], min_val=0, max_val=n_phys - 1)
                sp.dma_start(cring[:, n, :].rearrange("p (v c) -> p v c", v=2), cmp_pool[bass.ds(at, 1)])\
                  .then_inc(sem(f"c_in{n}"), 16)

            with sp.Fori(0, 5) as i:
                for bl in range(4):
                    for q in range(4):
                        quarter(i * 4 + bl, w_ab, i, bl, q)
                        page(i, 0, bl, q)

            def cache_a(n):
                kv, b, g = n // (AG * B), n // AG % B, n % AG
                window, dil = PATTERNS[g]
                sp.wait_ge(sem("c_used"), AK + n + 1)
                sp.dma_start(cring[:, n % NP, :], A["cache_a_kv"][b, 0, kv, PAST - window:PAST:dil].rearrange("r h d -> r (h d)"))\
                  .then_inc(sem(f"c_in{n % NP}"), 16)

            def ready_at(n):
                n -= NP
                return DK_AT + 1 + n if n < AG * B else DV_AT + n - AG * B

            w_o = A["w_out_ab"][0].rearrange("(k p) n -> p k n", p=P)
            w_g = A["w_ple_gate"][0].rearrange("(k p) n -> p k n", p=P)
            for m in range(16):
                for q in range(4):
                    quarter(AB2 + m, w_ab, 5 + m // 4, m % 4, q)
                    for n in range(NP, 2 * AG * B):
                        if ready_at(n) // 2 == 4 * (m - 1) + q:
                            cache_a(n)
                if m == 0:
                    for n in range(NP):
                        cache_a(n)
                if m == 1:
                    sp.wait_ge(sem("nat_taken"), 32)
                    for t in range(2):
                        sp.dma_start(A["new_a_kv_prompt"][0, 0, 0, tileT(t)].rearrange("p h d -> p (h d)"), k_nat[:, t, :])\
                          .then_inc(sem("a_out"), 16)
                        sp.dma_start(A["new_a_kv_prompt"][0, 0, 1, tileT(t)], proj[:, 32:40, tileT(t)]).then_inc(sem("a_out"), 16)
                    sp.dma_start(A["new_a_kv_sample"].rearrange("b l v s h d -> (b l) v (s h d)"), s_nat).then_inc(sem("a_out"), 16)
                if m == 8:
                    sp.wait_ge(sem("qz_set"), 1)
                    sp.dma_start(ws_nat, A["ws_b"][0].rearrange("g t s -> t g s")).then_inc(sem("ws_in"), 16)
                    sp.dma_start(bs, A["bs_b"].rearrange("l g t -> l (g t)")).then_inc(sem("ws_in"), 16)
            for q in range(4):
                quarter(OUT0, w_o, 0, 0, q)
                page(0, 5, 0, q)
            sp.wait_ge(sem("vn_taken"), 16)
            sp.dma_start(A["state_b_v_prompt"].rearrange("b l c n -> (b l c) n"), vn_nat[:, 1, :]).then_inc(sem("b_out"), 16)
            sp.dma_start(A["state_b_v_sample"].rearrange("b l s n -> b (l s n)"), vn_s).then_inc(sem("b_out"), 16)
            sp.wait_ge(sem("mixed"), 8)
            sp.wait_ge(sem("b_out"), 32)
            sp.wait_ge(sem("spilled"), 16)
            sp.dma_start(hs, resid).then_inc(sem("resid_in"), 16)
            for m in range(1, 8):
                for q in range(4):
                    quarter(OUT0 + m, w_o, 0, m, q)
                    page(m // 4, 5, m % 4, q)
            for m in range(8):
                for q in range(4):
                    quarter(GATE0 + m, w_g, 0, m, q)
                    if m < 4:
                        page(2, 5, m, q)
                    if m == 0 and q == 1:
                        sp.wait_ge(sem("x_lo"), 4 * (CAT0 + 1))
                        sp.dma_start(wple, A["w_ple"][0].rearrange("(k p) n -> p k n", p=P)).then_inc(sem("wple_in"), 16)
            w_c = A["w_in_c"][0].rearrange("(k p) n -> p k n", p=P)
            for q in range(2):
                quarter(CQ, w_c, 0, 0, q)
            sp.dma_start(mask[:, :], A["mask_c"]).then_inc(sem("mask_c_in"), 16)
            for t in range(2):
                sp.dma_start(p_nat1[:, t, :], A["p_prompt"][1, 0, tileT(t), :]).then_inc(sem("p_in"), 16)
            sp.dma_start(p_nat1[0:B, 2, :], A["p_sample"][1].rearrange("b s d -> b (s d)")).then_inc(sem("p_in"), 16)
            sp.wait_ge(sem("c_used"), NP + CMP_B + 48)
            sp.dma_start(wg, w_c[:, :, 40 * P:40 * P + 48]).then_inc(sem("wg_in"), 16)
            for q in range(2, 4):
                quarter(CQ, w_c, 0, 0, q)
            sp.wait_ge(sem("h_new0"), 4 + KC)
            sp.dma_start(resid, hs).then_inc(sem("spilled"), 16)
            for bl in range(1, 4):
                for q in range(4):
                    quarter(CQ + bl, w_c, 0, bl, q)
            with sp.Fori(0, 4) as i:
                for bl in range(4):
                    for q in range(4):
                        quarter(i * 4 + (CQ + 4 + bl), w_c, i + 1, bl, q)
            w_z = w_c[:, :, 40 * P + 48:40 * P + 48 + D]
            for q in range(2):
                quarter(CZ, w_z, 0, 0, q)
            sp.wait_ge(sem("cnat_taken"), 48)
            k2 = {0: ("cmp", 16), 1: ("cmp", 20), 2: ("sel", None), 3: ("sel", 28), 4: ("win", None), 5: ("win", 36)}
            for n, (name, slot) in k2.items():
                for t in range(2):
                    src = proj[:, slot:slot + 4, tileT(t)] if slot is not None else kst[:, n // 4, t, :]
                    dst = A[f"new_c_{name}_kv_prompt"][0, 0, n % 2, tileT(t)]
                    sp.dma_start(dst if slot is not None else dst.rearrange("p h d -> p (h d)"), src).then_inc(sem("c_out"), 16)
                sp.dma_start(A[f"new_c_{name}_kv_sample"][:, 0, n % 2, 0].rearrange("b h d -> b (h d)"), c_nat[:, n, :])\
                  .then_inc(sem("c_out"), 16)
            sp.wait_ge(sem("gate_taken"), 3)
            with nc.allow_non_contiguous_dma(reason="384 gate values change partitions"):
                for j in range(3):
                    for h in range(CH):
                        sp.dma_start(gate_s[32 * h:32 * h + 32, j:j + 1],
                                     gate_8[:, j * HQ + GQ * h:j * HQ + GQ * h + GQ]).then_inc(sem("gate_s_in"), 16)
            sp.wait_ge(sem("c_out"), 16 * 18)
            sel_pool = A["cache_c_sel_kv"].rearrange("n l v r h d -> n r (l v) (h d)")

            def page_of(b_pg):
                return sp.value_load(ptab[0:1, bass.ds(b_pg, 1)], min_val=0, max_val=n_phys - 1)

            def page_set(first, kv, n):
                for q in range(4):
                    at = page_of(first + q)
                    sp.dma_start(hring[:, 4 * (n % 2) + q, :].rearrange("p (o c) -> p o c", o=1),
                                 sel_pool[bass.ds(at, 1), :, kv, :].rearrange("o r c -> r o c")).then_inc(sem(f"set_in{n % 2}"), 16)

            win = A["cache_c_win_kv"].rearrange("b l v (w p) h d -> b w p (l v) (h d)", p=P)

            def win_set(b, kv, n):
                for q in range(WT):
                    sp.dma_start(hring[:, 4 * (n % 2) + q, :].rearrange("p (o c) -> p o c", o=1),
                                 win[bass.ds(b, 1), q, :, kv, :].rearrange("o p c -> p o c")).then_inc(sem(f"set_in{n % 2}"), 16)

            with sp.Fori(0, 4) as i:
                for b in range(B):
                    sp.wait_ge(sem("kt_T"), i * 32 + (4 * b + 4))
                    page_set(i * 4 + b * NPG, 0, b)
            for b in range(B):
                sp.wait_ge(sem("kt_T"), 128 + 4 * b + 4)
                win_set(b, 0, b)
            sp.wait_ge(sem("kt_T"), 8 + 160)
            w_o1 = A["w_out_c"][0].rearrange("(k p) n -> p k n", p=P)
            sp.wait_ge(sem("kt_used"), K_STEPS)

            def value_set(i, b2, k):
                n = 5 * b2 + k
                sp.wait_ge(sem("set_used"), i * 10 + (n + 1))
                if k < 4:
                    page_set(i * 2 * NPG + (b2 * NPG + 4 * k), 1, n)
                else:
                    win_set(i * 2 + b2, 1, n)

            def value_loads(i, b2, w, nxt):
                value_set(i, b2, 0)
                quarter(i * 2 + (CZ + b2), w_z, i, b2, 2, 2)
                value_set(i, b2, 1)
                quarter(i * 2 + (CZ + b2), w_z, i, b2, 3, 2)
                for k in range(2, 5):
                    value_set(i, b2, k)
                    if k > 2:
                        quarter(i * 2 + (CZ + b2 + 1), w, *nxt, k - 3, 2)

            with sp.Fori(0, 3) as i:
                for b2 in range(2):
                    value_loads(i, b2, w_z, (i, b2 + 1))
            value_loads(3, 0, w_z, (3, 1))
            value_loads(3, 1, w_o1, (0, 0))
            for q in range(2, 4):
                quarter(OUT1, w_o1, 0, 0, q)
            sp.wait_ge(sem("OT_taken"), 2 + B)
            sp.wait_ge(sem("spilled"), 32)
            sp.dma_start(hs, resid).then_inc(sem("resid_in"), 16)
            for m in range(1, 8):
                for q in range(4):
                    quarter(OUT1 + m, w_o1, 0, m, q)
            w_g1 = A["w_ple_gate"][1].rearrange("(k p) n -> p k n", p=P)
            for m in range(8):
                for q in range(4):
                    quarter(GATE1 + m, w_g1, 0, m, q)
                    if m == 0 and q == 1:
                        sp.wait_ge(sem("x_lo"), 4 * (CAT1 + 1))
                        sp.dma_start(wple, A["w_ple"][1].rearrange("(k p) n -> p k n", p=P)).then_inc(sem("wple_in"), 16)
            for q in range(4):
                sp.wait_ge(sem("y_taken"), 8 * (q + 1))
                a = slice(q * 512, (q + 1) * 512)
                for t in range(2):
                    sp.dma_start(A["y_prompt"][0, tileT(t), a], y_nat[:, t, a]).then_inc(sem("y_out"), 16)
                sp.dma_start(A["y_sample"][:, 0, a], y_s[:, a]).then_inc(sem("y_out"), 16)
            sp.wait_ge(sem("a_out"), 16 * 5)
            sp.wait_ge(sem("b_out"), 32)
            sp.wait_ge(sem("c_out"), 16 * 18)
            sp.wait_ge(sem("y_out"), 16 * 12)

        @block.gpsimd
        def _(pool):
            nc.gpsimd.memset(wide[:, :, :, :], 0.0).then_inc(sem("wide_zero"), 1)
            nc.gpsimd.memset(ones[:, :], 1.0).then_inc(sem("ones_set"), 1)
            nc.gpsimd.memset(zrow[:, :], 0.0).then_inc(sem("ones_set"), 1)
            nc.gpsimd.memset(eps, EPS).then_inc(sem("ones_set"), 1)

        @block.scalar
        def _(act):
            for f, n in (("w_used", 7), ("w_lo", 8), ("proj_made", 4), ("c_used", NP), ("proj_free", 4), ("cmp_free", 1),
                         ("kt_T", 8), ("set_used", 2), ("OT_taken", 2), ("qn_done", 4), ("qn_root", 2),
                         ("cn_done", 2), ("cn_root", 2)):
                act.sem_inc(sem(f), n)
            act.wait_ge(sem("xT_made"), 1)
            nc.scalar.copy(gains, XB[3][:, 0:NG]).then_inc(sem("gains_set"), 1)
            for c in range(KC + 2):
                act.wait_ge(sem("xT_made"), c + 2)
                dst = hs[:, c, :] if c < KC else pT[:, c - KC, :]
                nc.scalar.copy(dst, XB[c % 4][:, 0:T]).then_inc(sem("xT_taken"), 1)
            act.wait_ge(sem("ones_set"), 3)

            def split(n, e):
                act.wait_ge(sem(f"w_in{e // 2}"), n * 16 + 16)
                if e < 3:
                    act.wait_ge(sem("w_used"), n * 7 + (e + 5))
                elif e == 3:
                    act.wait_ge(sem("proj_made"), n * 2 + 4)
                else:
                    act.wait_ge(sem("w_used"), n * 7 + (e + 4))
                nc.scalar.copy(w_up[:, e % NE], raw(e)).then_inc(sem("w_hi"), 1)

            def upper(n, s):
                on, e = ahead(s)
                split(n + on, e)

            def uppers(n, slots=range(8)):
                for s in slots:
                    upper(n, s)

            def upper_x(k, src):
                for g in range(4):
                    a = slice(4 * g, 4 * g + 4)
                    act.wait_ge(sem("x_tmp"), 4 * k + g + 1)
                    nc.scalar.copy(xh[:, a, :], src[:, a, :]).then_inc(sem("x_hi"), 1)

            def square(c):
                nc.scalar.activation(tmp_n[:, c, :], hs[:, c, :], ACT.Square).then_inc(sem("rms_sq1"), 1)

            def rms_root(layer, src):
                act.wait_ge(sem(f"rms_sum{layer}"), 1)
                nc.scalar.activation(scr[:, 0, :], src[:, 0:T], ACT.Sqrt, bias=eps, scale=1.0 / D)\
                  .then_inc(sem(f"rms_root{layer}"), 1)

            rms_root(0, XB[0])
            upper_x(X0, tmp_n)
            for e in range(3):
                split(0, e)
            act.wait_ge(sem("spilled"), 16)

            def ab1_round(r, norm):
                if norm:
                    act.wait_ge(sem("proj_free"), r * 8 + 4)
                for bl in range(4):
                    uppers(r * 4 + bl, range(4))
                    if norm:
                        act.wait_ge(sem("qn_done"), (r - 1) * 4 + (bl + 1))
                        nc.scalar.activation(scr[:, 2 * bl:2 * bl + 2, :], proj[:, bass.ds((r - 1) * 8 + 2 * bl, 2), :], ACT.Square)\
                          .then_inc(sem("qn_sq"), 1)
                    uppers(r * 4 + bl, range(4, 8))
                    for j in range(2 * bl, 2 * bl + 2):
                        act.wait_ge(sem("proj_made"), r * 8 + (4 + j + 1))
                        nc.scalar.copy(proj[:, bass.ds(r * 8 + j, 1), :], PJ[j % 4][:, 0:T]).then_inc(sem("proj_free"), 1)
                    if norm:
                        for c in range(2):
                            act.wait_ge(sem("qn_sum"), (r - 1) * 8 + (2 * bl + c + 1))
                            nc.scalar.activation(root_a(bl)[:, c, :], XB[2 + c][:, 0:T], ACT.Sqrt, bias=eps, scale=1.0 / P)\
                              .then_inc(sem("qn_root"), 1)

            ab1_round(0, False)
            with act.Fori(0, 3) as i:
                ab1_round(i + 1, True)
            ab1_round(4, True)

            def natural(t):
                act.wait_ge(sem("nat_made"), t + 1)
                src = XB[t % 4]
                dst = k_nat[:, :, tileT(t - 8)] if t >= 8 else proj[:, 32 + t, 0:S].rearrange("p (t n) -> p t n", t=2)
                nc.scalar.copy(dst, src[:, 0:S].rearrange("p (t n) -> p t n", t=2)).then_inc(sem("nat_taken"), 1)
                nc.scalar.copy(s_nat[:, 1 - t // 8, tileT(t % 8)], src[0:B, S:S + P]).then_inc(sem("nat_taken"), 1)

            def pa_exp(u):
                nk = AG * P * (u % 2 + 1)
                act.wait_ge(sem("pa_max"), u + 1)
                nc.scalar.activation(S_sb[:, u % 2, 0:nk], S_sb[:, u % 2, 0:nk], ACT.Exp, bias=nmx[:, u % 2:u % 2 + 1],
                                     accum_out=den[:, u % 2:u % 2 + 1]).then_inc(sem("pa_exp"), 1)

            def pa_pT(u):
                qt = u % 2
                act.wait_ge(sem("pa_pT"), u + 1)
                nc.scalar.copy(PT[:, u % 2, 0:P * (qt + 1)], XB[3][:, 0:P * (qt + 1)]).then_inc(sem("pa_pT_taken"), 1)

            def pa_out(u):
                act.wait_ge(sem("pa_o"), u + 1)
                nc.scalar.copy(scr[:, u // 2, tileT(u % 2)], XB[3][:, 384:512]).then_inc(sem("pa_o_taken"), 1)

            def dk_copy(n):
                act.wait_ge(sem("dk_T"), n + 1)
                if n >= 2:
                    act.wait_ge(sem("c_used"), AK + NP + n - 1)
                else:
                    act.wait_ge(sem("qz_set"), 1)
                nc.scalar.copy(KT[:, n % 2, 0:512], XB[2][:, :]).then_inc(sem("dk_T_taken"), 1)

            def d_exps():
                for u in range(2):
                    act.wait_ge(sem("d_max"), 1)
                    nc.scalar.activation(Sd[:, u, 0:387], Sd[:, u, 0:387], ACT.Exp, bias=nmx[:, u:u + 1],
                                         accum_out=den[:, u:u + 1]).then_inc(sem("d_exp"), 1)

            def d_probs():
                act.wait_ge(sem("d_pT"), 1)
                nc.scalar.copy(PTd[:, 0:2, :, :], XB[2][:, :].rearrange("p (g u r) -> p g u r", g=2, u=2)).then_inc(sem("d_pT_taken"), 1)
                nc.scalar.copy(PTd[:, 2, :, :], XB[3][:, 0:256].rearrange("p (u r) -> p u r", u=2)).then_inc(sem("d_pT_taken"), 1)

            def vn_rows(g):
                act.wait_ge(sem("vn_T"), g + 1)
                src = XB[g % 2]
                nc.scalar.copy(vn_nat[:, :, tileT(g)], src[:, 0:S].rearrange("p (t n) -> p t n", t=2)).then_inc(sem("vn_taken"), 1)
                nc.scalar.copy(vn_s[:, tileT(g)], src[0:B, S:S + P]).then_inc(sem("vn_taken"), 1)

            for s in range(16 * SLOTS):
                upper(AB2 + s // SLOTS, s % SLOTS)
                for j in range(2 * (s // SLOTS), 2 * (s // SLOTS) + 2) if s % SLOTS == SLOTS - 1 else ():
                    if j == 8:
                        act.wait_ge(sem("a_out"), 16 * 5)
                    act.wait_ge(sem("proj_made"), 44 + j + 1)
                    if j < 24:
                        nc.scalar.copy(proj[:, 40 + j, :], PJ[j % 4][:, 0:T]).then_inc(sem("proj_free"), 1)
                    else:
                        nc.scalar.activation(proj[:, j - 24, :], PJ[j % 4][:, 0:T], ACT.Silu).then_inc(sem("proj_free"), 1)
                if s < PA_AT:
                    natural(2 * s)
                    natural(2 * s + 1)
                    if s == PA_AT - 1:
                        pa_exp(0)
                        pa_exp(1)
                elif s < PA_AT + 48:
                    u, part = (s - PA_AT) // 3, (s - PA_AT) % 3
                    if part == 0:
                        pa_pT(u)
                    elif part == 1:
                        pa_out(u)
                    elif u + 2 < 16:
                        pa_exp(u + 2)
                elif DK_AT <= s < DK_AT + AG * B:
                    dk_copy(s - DK_AT)
                elif s == DS_AT + 1:
                    d_exps()
                elif s == DP_AT:
                    d_probs()
                elif s == DP_AT + 1:
                    act.wait_ge(sem("proj_free"), 4 + 48)
                    nc.scalar.activation(proj[:, 40:48, :], proj[:, 40:48, :], ACT.Silu).then_inc(sem("silu"), 1)
                elif DV_AT <= s < DV_AT + AG * B:
                    b, g = (s - DV_AT) // AG, (s - DV_AT) % AG
                    if g == AG - 1:
                        act.wait_ge(sem("c_used"), AV + NP + 3 * b + 3)
                        nc.scalar.copy(Od[:, b % 2, :], XB[b % 2][:, 0:256]).then_inc(sem("dO_taken"), 1)
                elif s == LN_AT + 2:
                    act.wait_ge(sem("ln_centred"), 1)
                    nc.scalar.activation(sq8, xc, ACT.Square).then_inc(sem("ln_sq"), 1)
                elif s == LN_AT + 5:
                    act.wait_ge(sem("ln_sum"), 2)
                    nc.scalar.activation(pnewT, XB[1][:, 0:T], ACT.Sqrt, bias=eps, scale=1.0 / 1024).then_inc(sem("ln_root"), 1)
                elif VN_AT <= s < VN_AT + 4:
                    vn_rows(2 * (s - VN_AT))
                    vn_rows(2 * (s - VN_AT) + 1)

            def ple(layer):
                for c in range(KC):
                    act.wait_ge(sem(f"ple_made{layer}"), c + 1)
                    nc.scalar.copy(proj[:, c, :], XB[c % 4][:, 0:T]).then_inc(sem(f"ple_taken{layer}"), 1)

            def out_proj(first):
                with act.Fori(0, 2) as i:
                    for bl in range(4):
                        uppers(i * 4 + (first + bl))

            def gate(layer, first):
                for m in range(8):
                    uppers(first + m, range(8 if first + m < BLOCKS - 1 else 5))
                    for j in range(2 * m, 2 * m + 2):
                        act.wait_ge(sem("proj_made"), 4 + 2 * first + j + 1)
                        act.wait_ge(sem(f"h_new{layer}"), j + 1)
                        nc.scalar.activation(scr[:, j % 4, :], PJ[j % 4][:, 0:T], ACT.Sigmoid).then_inc(sem("proj_free"), 1)
                    if layer == 0 and m >= 1:
                        for j in range(2 * m - 2, 2 * m):
                            act.wait_ge(sem("h_new0"), 4 + j + 1)
                            square(j)
            upper_x(CAT0, cat)
            out_proj(OUT0)
            upper_x(H0, hs)
            ple(0)
            gate(0, GATE0)

            for k in range(2):
                act.wait_ge(sem("pT_made"), k + 1)
                nc.scalar.copy(pT[:, k, :], XB[1 + k][:, 0:T]).then_inc(sem("pT_taken"), 1)
            act.wait_ge(sem("h_new0"), 4 + KC)
            square(KC - 2)
            square(KC - 1)
            rms_root(1, XB[3])
            upper_x(X1, tmp_n)
            act.wait_ge(sem("spilled"), 32)

            def ks_square(n):
                if n >= 2:
                    act.wait_ge(sem("ks_sum"), n - 1)
                nc.scalar.activation(F[:, P * (n % 2):P * (n % 2 + 1)], kcmp[:, n // 4, n % 4, :], ACT.Square,
                                     accum_out=kss[:, n:n + 1]).then_inc(sem("ks_sum"), 1)

            def cq_tile(r, j):
                act.wait_ge(sem("proj_made"), r * 8 + (4 + 104 + j + 1))
                nc.scalar.copy(proj[:, bass.ds(r * 8 + j, 1), :], PJ[j % 4][:, 0:T]).then_inc(sem("proj_free"), 1)

            def cn_squares(p, odd, first):
                act.wait_ge(sem("cn_done"), p + 1)
                nc.scalar.activation(scr[:, 2 * odd:2 * odd + 2, :], proj[:, bass.ds(first, 2), :], ACT.Square).then_inc(sem("cn_sq"), 1)

            def cn_roots(p, odd):
                for c in range(2):
                    act.wait_ge(sem("cn_sum"), p * 2 + (c + 1))
                    nc.scalar.activation(root_c(odd)[:, c, :], XB[2 + c][:, 0:T], ACT.Sqrt, bias=eps, scale=1.0 / P)\
                      .then_inc(sem("cn_root"), 1)

            def natural_c(n):
                act.wait_ge(sem("cnat_made"), n + 1)
                t = NAT[n]
                src, v = XB[n % 2 + (2 if n >= 16 else 0)], t // 4
                dst = kst[:, v // 4, :, tileT(t % 4)] if v in (2, 4) else proj[:, 16 + t, 0:S].rearrange("p (t n) -> p t n", t=2)
                nc.scalar.copy(dst, src[:, 0:S].rearrange("p (t n) -> p t n", t=2)).then_inc(sem("cnat_taken"), 1)
                nc.scalar.copy(c_nat[:, v, tileT(t % 4)], src[0:B, S:S + P]).then_inc(sem("cnat_taken"), 1)

            for bl in range(4):
                for s in range(SLOTS):
                    upper(CQ + bl, s)
                    if s == SLOTS - 1:
                        cq_tile(0, 2 * bl)
                        cq_tile(0, 2 * bl + 1)
                    if bl < 2:
                        ks_square(16 * bl + 2 * s)
                        ks_square(16 * bl + 2 * s + 1)
                    elif bl == 2 and s == 0:
                        act.wait_ge(sem("ks_sum"), 32)
                        nc.scalar.activation(krt, kss, ACT.Sqrt, bias=eps, scale=1.0 / P).then_inc(sem("ks_root"), 1)
                    elif bl == 3 and s >= 4:
                        for b in range(2 * s - 8, 2 * s - 6):
                            act.wait_ge(sem("kcT_made"), b + 1)
                            nc.scalar.activation(kcmp[:, b].rearrange("p a r -> p (a r)"), XB[b % 2][:, :], ACT.Copy, scale=g_kc[:, 0:1])\
                              .then_inc(sem("kcT_taken"), 1)
            with act.Fori(0, 2) as i:
                act.wait_ge(sem("proj_free"), i * 8 + (4 + 104 + 8))
                for bl in range(4):
                    uppers(i * 4 + (CQ + 4 + bl), range(4))
                    cn_squares(i * 4 + bl, bl % 2, i * 8 + 2 * bl)
                    uppers(i * 4 + (CQ + 4 + bl), range(4, 8))
                    cq_tile(i + 1, 2 * bl)
                    cq_tile(i + 1, 2 * bl + 1)
                    cn_roots(i * 4 + bl, bl % 2)
            for r in (3, 4):
                for bl in range(4):
                    if bl >= 2:
                        if bl == 2:
                            act.wait_ge(sem("proj_free"), 4 + 104 + 8 * r + 4)
                        cn_squares(8 + 2 * (r - 3) + bl - 2, bl % 2, 8 * r + 2 * (bl - 2))
                    for s in range(SLOTS):
                        upper(CQ + 4 * r + bl, s)
                        if s == SLOTS - 1:
                            cq_tile(r, 2 * bl)
                            cq_tile(r, 2 * bl + 1)
                        if bl < 2 and s % 2 == 1:
                            natural_c(8 * (r - 3) + 4 * bl + s // 2)
                    if bl >= 2:
                        cn_roots(8 + 2 * (r - 3) + bl - 2, bl % 2)
            for n in range(16, 20):
                natural_c(n)
            act.wait_ge(sem("cn_done"), 2 + 12)
            act.wait_ge(*done("pc_made"))
            nc.scalar.copy(kcp, XB[0][:, 0:P]).then_inc(sem("act_chain"), 1)
            nc.scalar.copy(vcp, XB[1][0:32, :].rearrange("p (h d) -> p h d", h=CH)).then_inc(sem("vcp_set"), 1)
            act.wait_ge(sem("act_chain"), 1)
            nc.scalar.activation(SC[:, 1600:1728], kcp, ACT.Square, accum_out=kss[:, 0:1]).then_inc(sem("act_chain"), 1)
            act.wait_ge(sem("act_chain"), 2)
            nc.scalar.activation(krt[:, 0:1], kss[:, 0:1], ACT.Sqrt, bias=eps, scale=1.0 / P).then_inc(sem("pc_root"), 1)
            for n in range(20, 24):
                natural_c(n)
            act.wait_ge(*done("gT_made"))
            nc.scalar.activation(gT, PJ[0][0:48, 0:T], ACT.Sigmoid).then_inc(sem("gT_set"), 1)
            act.wait_ge(*done("gate_made"))
            for t in range(2):
                nc.scalar.copy(gate_p[:, t].rearrange("p j h -> p (j h)"), PJ[1][:, 64 * t:64 * t + 48]).then_inc(sem("gate_taken"), 1)
            nc.scalar.copy(gate_8, PJ[1][0:B, 128:176]).then_inc(sem("gate_taken"), 1)
            act.wait_ge(*done("pc_centred"))
            nc.scalar.activation(Pc, Pc, ACT.Exp).then_inc(sem("pc_exp"), 1)
            act.wait_ge(sem("sc_max"), 1)
            nc.scalar.activation(S_cmp[:, 0:NCMP], S_cmp[:, 0:NCMP], ACT.Exp, bias=mx_c[:, 0:1], accum_out=den_c[:, 0:1])\
              .then_inc(sem("sc_exp"), 1)
            act.wait_ge(*done("pc_p"))
            act.wait_ge(sem("c_out"), 16 * 18)

            def pc_exps(u):
                qt, nk = u % 2, P * (u % 2 + 1)
                act.wait_ge(sem("cu_max"), u + 1)
                for br in range(2):
                    a = slice(br * nk, (br + 1) * nk)
                    nc.scalar.activation(S_c[:, qt, a], S_c[:, qt, a], ACT.Exp, bias=nmx[:, 2 * qt + br:2 * qt + br + 1],
                                         accum_out=den[:, 2 * qt + br:2 * qt + br + 1]).then_inc(sem("cu_exp"), 1)

            def pc_pT(u):
                qt, nk = u % 2, P * (u % 2 + 1)
                act.wait_ge(sem("cu_pT"), u + 1)
                nc.scalar.copy(PT_c[:, qt, 0:2 * nk], PJ[2][:, 0:2 * nk]).then_inc(sem("cu_pT_taken"), 1)
                nc.scalar.copy(PcT[:, qt, :], PJ[3][0:16, 0:P]).then_inc(sem("cu_pT_taken"), 1)

            def pc_out(u):
                act.wait_ge(sem("cu_o"), u + 1)
                nc.scalar.copy(proj[:, 40 + u // 2, tileT(u % 2)], PJ[3][:, P:2 * P]).then_inc(sem("cu_o_taken"), 1)

            def k_even(steps):
                for k in steps:
                    if k % 2 == 0:
                        act.wait_ge(sem("kt_T"), 8 + k + 1)
                        if k >= CH:
                            act.wait_ge(sem("kt_used"), k - CH + 1)
                        nc.scalar.copy(KTc[:, k % CH, :], XB[1 + k % 3][:, :]).then_inc(sem("kt_even"), 1)

            pc_exps(0)
            act.wait_ge(*done("psum_made"))
            nc.scalar.copy(P_sum, XB[0][:, 128:256]).then_inc(sem("psum_taken"), 1)
            for u in range(32):
                if u == K_FROM - 1:
                    act.wait_ge(*done("ptexp_made"))
                    nc.scalar.copy(PT_exp.rearrange("p a r -> p (a r)"), XB[3][:, :]).then_inc(sem("ptexp_taken"), 1)
                before, after = k_steps(u)
                pc_pT(u)
                k_even(before)
                if u + 1 < 32:
                    pc_exps(u + 1)
                pc_out(u)
                k_even(after)
            for br, (s_br, n) in enumerate(((S_sel, 2048), (S_win, 512))):
                act.wait_ge(sem("sw_max"), br + 1)
                nc.scalar.activation(s_br, s_br, ACT.Exp, bias=mx_c[:, 1 + br:2 + br], scale=SCALE, accum_out=den_c[:, 1 + br:2 + br]).then_inc(sem("sw_exp"), 1)
                nc.scalar.activation(p_new[:, br:br + 1], s_new[:, br:br + 1], ACT.Exp, bias=mx_c[:, 1 + br:2 + br]).then_inc(sem("sw_exp"), 1)
            for q in range(5):
                act.wait_ge(sem("sw_pT"), q + 1)
                dst = PT_sel[:, 4 * q:4 * q + 4, :] if q < 4 else PT_win
                nc.scalar.copy(dst.rearrange("p a r -> p (a r)"), XB[q % 4][:, :]).then_inc(sem("sw_pT_taken"), 1)
            with act.Fori(0, 4) as i:
                for b2 in range(2):
                    uppers(i * 2 + (CZ + b2))
                    for j in range(2 * b2, 2 * b2 + 2):
                        act.wait_ge(sem("proj_made"), i * 4 + (4 + 144 + j + 1))
                        nc.scalar.activation(proj[:, bass.ds(i * 4 + j, 1), :], PJ[j][:, 0:T], ACT.Silu).then_inc(sem("proj_free"), 1)
            upper_x(CAT1, cat)
            out_proj(OUT1)
            upper_x(H1, hs)
            ple(1)
            gate(1, GATE1)
            for c in range(KC):
                act.wait_ge(sem("y_made"), c + 1)
                nc.scalar.copy(y_nat[:, :, tileT(c)], XB[c % 4][:, 0:S].rearrange("p (t n) -> p t n", t=2)).then_inc(sem("y_taken"), 1)
                nc.scalar.copy(y_s[:, tileT(c)], XB[c % 4][0:B, S:S + P]).then_inc(sem("y_taken"), 1)

        @block.vector
        def _(dve):
            chain = [0]

            def link(ins):
                chain[0] += 1
                ins.then_inc(sem("dve_chain"), 1)
                dve.wait_ge(sem("dve_chain"), chain[0])

            def split(n, e):
                dve.wait_ge(sem("w_hi"), n * 8 + (e + 1))
                nc.vector.tensor_tensor(w_low[:, e % NE], raw(e), w_up[:, e % NE].bitcast(F32), ALU.subtract).then_inc(sem("w_lo"), 1)

            def lower(n, s):
                on, e = ahead(s)
                split(n + on, e)

            def lowers(n, slots=range(8)):
                for s in slots:
                    lower(n, s)

            def head_norm(step, first, gain, rotated, root, sums, name):
                x = proj[:, first:first + 2, :]
                src, dst = proj[0:32, first:first + 2, :], proj[0:32, rotated:rotated + 2, :]
                swp = lnt[0:32]
                cosb, sinb = (a.rearrange("p (o t) -> p o t", o=1).broadcast_to([32, 2, T]) for a in (cos, sin))
                if step < 2:
                    dve.wait_ge(sem(name + "_root"), 2 + sums + step + 1)
                    link(nc.vector.reciprocal(root[:, step, :], root[:, step, :]))
                elif step == 2:
                    link(nc.vector.scalar_tensor_tensor(x, x, gain, root, ALU.mult, ALU.mult))
                    if rotated != first:
                        link(nc.vector.tensor_copy(proj[:, rotated:rotated + 2, :], x))
                elif step == 3:
                    link(nc.vector.stream_shuffle(swp, src, [(m + HALF) % 32 for m in range(32)]))
                    link(nc.vector.tensor_tensor(swp, swp, sinb, ALU.mult))
                else:
                    link(nc.vector.tensor_tensor(root[0:32], src, cosb, ALU.mult))
                    link(nc.vector.tensor_tensor(dst, root[0:32], swp, ALU.add))
                    dve.sem_inc(sem(name + "_done"), 1)

            def a_norm(p, step):
                head_norm(step, 2 * p, g_qa if p < 12 else g_ka, 2 * p, root_a(p), 2 * p, "qn")

            def c_norm(p, step):
                gain = g_qc if p < 8 else g_kc[:, 1:2] if p < 10 else g_kc[:, 2:3]
                head_norm(step, PAIRS[p], gain, PAIRS[p] + (40 if p < 8 else 0), root_c(p), 2 * p, "cn")

            def lower_x(k, src, g):
                a = slice(4 * g, 4 * g + 4)
                dve.wait_ge(sem("x_hi"), 4 * k + g + 1)
                nc.vector.tensor_tensor(xl[:, a, :], src[:, a, :], xh[:, a, :].bitcast(F32), ALU.subtract).then_inc(sem("x_lo"), 1)

            def normalise(layer, k, g):
                dve.wait_ge(sem(f"rms_root{layer}"), 1)
                link(nc.vector.reciprocal(scr[:, 1, :], scr[:, 0, :]))
                for c in range(KC):
                    ins = nc.vector.scalar_tensor_tensor(tmp_n[:, c, :], hs[:, c, :], g[:, c:c + 1], scr[:, 1, :],
                                                         ALU.mult, ALU.mult)
                    if c % 4 == 3:
                        ins.then_inc(sem("x_tmp"), 1)
                        if c > 4:
                            lower_x(k, tmp_n, c // 4 - 1)
                lower_x(k, tmp_n, 3)

            def compressed(r, b, c0):
                dve.wait_ge(sem("c_used"), r * 16 + (c0 + NP + 16))
                nc.vector.tensor_copy(kcmp[:, bass.ds(b, 1)].rearrange("p o a d -> p (o a) d"),
                                      XB[0][:, :].rearrange("p (a d) -> p a d", a=4)).then_inc(sem("cmp_half"), 1)
                nc.vector.tensor_copy(vcmp[:, bass.ds(b, 1)].rearrange("p o a d -> p (o a) d"),
                                      XB[1][:, :].rearrange("p (a d) -> p a d", a=4)).then_inc(sem("cmp_free"), 1)

            for c in range(KC):
                dve.wait_ge(sem("xT_taken"), c + 1)
                nc.vector.tensor_tensor(tmp_n[:, c, :], hs[:, c, :], hs[:, c, :], ALU.mult).then_inc(sem("rms_sq0"), 1)
            dve.wait_ge(sem("gains_set"), 1)
            normalise(0, X0, g_ab)
            for e in range(3):
                split(0, e)

            for n in range(20):
                for s in range(SLOTS):
                    lower(n, s)
                    if s < 5 and n >= 5:
                        a_norm(n - 5, s)
                if n % 4 == 3:
                    compressed(n // 4, n // 4, CMP_A)

            def pa_scores(u):
                qt, nk = u % 2, P * (u % 2 + 1)
                dve.wait_ge(sem("pa_s"), u + 1)
                if u >= 2:
                    dve.wait_ge(sem("pa_pT"), u - 1)
                m = mask[:, AG * P * qt:AG * P * qt + AG * nk]
                if qt == 0:
                    link(nc.vector.scalar_tensor_tensor(S_sb[:, 0, 0:384], XB[0][:, 0:384], SCALE, m, ALU.mult, ALU.add))
                else:
                    link(nc.vector.scalar_tensor_tensor(S_sb[:, 1, 0:512], XB[1][:, :], SCALE, m[:, 0:512], ALU.mult, ALU.add))
                    link(nc.vector.scalar_tensor_tensor(S_sb[:, 1, 512:768], XB[2][:, 0:256], SCALE, m[:, 512:768], ALU.mult, ALU.add))
                nc.vector.tensor_reduce(nmx[:, qt:qt + 1], S_sb[:, qt, 0:AG * nk], AX, ALU.max, negate=True).then_inc(sem("pa_max"), 1)

            def pa_probs(u):
                qt, nk = u % 2, P * (u % 2 + 1)
                dve.wait_ge(sem("pa_exp"), u + 1)
                s0, s1, s2 = (S_sb[:, qt, g * nk:(g + 1) * nk] for g in range(AG))
                link(nc.vector.reciprocal(rden[:, qt:qt + 1], den[:, qt:qt + 1]))
                link(nc.vector.tensor_tensor(s0, s0, s1, ALU.add))
                link(nc.vector.tensor_tensor(s0, s0, s2, ALU.add))
                nc.vector.tensor_scalar(s0, s0, rden[:, qt:qt + 1], None, ALU.mult).then_inc(sem("pa_p"), 1)

            def d_queries():
                dve.wait_ge(sem("pa_o_taken"), 16)
                link(nc.vector.memset(spare_k, 0.0))
                link(nc.vector.memset(spare_v[:, 0:1024], 0.0))
                for g in range(AG):
                    for b in range(B):
                        nc.vector.tensor_copy(qz[:, g, b, :, b], proj[:, 8 * g:8 * g + 8, S + b])
                for g in range(AG):
                    for u in range(2):
                        ins = nc.vector.tensor_tensor(prod[:, g, u, :].rearrange("p (j b) -> p j b", j=4)[:, :, 0:B],
                                                      proj[:, 8 * g + 4 * u:8 * g + 4 * u + 4, S:T],
                                                      proj[:, 24 + 4 * u:28 + 4 * u, S:T], ALU.mult)
                link(ins)
                dve.sem_inc(sem("qz_set"), 1)

            def dk_copy(n):
                dve.wait_ge(sem("dk_T"), n + 1)
                if n >= 2:
                    dve.wait_ge(sem("c_used"), AK + NP + n - 1)
                nc.vector.tensor_copy(KT[:, n % 2, 512:1024], XB[3][:, :]).then_inc(sem("dk_T_taken2"), 1)

            def d_scores():
                dve.wait_ge(sem("d_s"), 1)
                for u in range(2):
                    link(nc.vector.tensor_scalar(Sd[:, u, 0:387], XB[u][:, 0:387], SCALE, None, ALU.mult))
                nc.vector.tensor_reduce(nmx[:, 0:2], Sd[:, :, 0:387], AX, ALU.max, negate=True).then_inc(sem("d_max"), 1)

            def d_probs():
                dve.wait_ge(sem("d_exp"), 2)
                link(nc.vector.reciprocal(rden[:, 0:2], den[:, 0:2]))
                for u in range(2):
                    link(nc.vector.tensor_scalar(Sd[:, u, 0:387], Sd[:, u, 0:387], rden[:, u:u + 1], None, ALU.mult))
                link(nc.vector.tensor_reduce(pnew[:, 0:2], Sd[:, :, 384:387], AX, ALU.add))
                for u in range(2):
                    link(nc.vector.tensor_scalar(diag[:, u, :], ident, pnew[:, u:u + 1], None, ALU.mult))
                dve.sem_inc(sem("d_p"), 1)

            def d_new_values():
                dve.wait_ge(sem("d_new"), 1)
                link(nc.vector.tensor_tensor(vs_a.rearrange("p (u j b) -> p u j b", u=2, j=4),
                                             XB[1][:, 0:256].rearrange("p (u j b) -> p u j b", u=2, j=4)[:, :, :, 0:B],
                                             proj[:, 32:40, S:T].rearrange("p (u j) b -> p u j b", u=2), ALU.mult))
                dve.sem_inc(sem("d_new_taken"), 1)

            def d_out(b):
                vs4 = vs_a.rearrange("p (u j b) -> p u j b", u=2, j=4)
                scr4 = scr[:, :, :].rearrange("p (u j) t -> p u j t", u=2)
                dve.wait_ge(sem("dO_T"), b + 1)
                src = XB[2 + b % 2][:, 0:256].rearrange("p (u j b) -> p u j b", u=2, j=4)[:, :, :, b]
                nc.vector.tensor_tensor(scr4[:, :, :, S + b], src, vs4[:, :, :, b], ALU.add).then_inc(sem("oTd"), 1)

            def ln_centre():
                dve.wait_ge(sem("ln_sum"), 1)
                link(nc.vector.tensor_scalar(pnewT, XB[0][:, 0:T], 1.0 / 1024, None, ALU.mult))
                link(nc.vector.tensor_tensor(xc, xc, pnewT.rearrange("p (o t) -> p o t", o=1).broadcast_to([P, 8, T]), ALU.subtract))
                dve.sem_inc(sem("ln_centred"), 1)

            def ln_scale():
                dve.wait_ge(sem("ln_root"), 1)
                link(nc.vector.reciprocal(lnr, pnewT))
                for g in range(8):
                    ins = nc.vector.scalar_tensor_tensor(xc[:, g, :], xc[:, g, :], g_sgu[:, g:g + 1], lnr, ALU.mult, ALU.mult)
                link(ins)
                dve.sem_inc(sem("vn_ready"), 1)

            def ws_lower():
                for n in range(2):
                    dve.wait_ge(sem("ws_T"), n + 1)
                    nc.vector.tensor_tensor(wsT[:, 4 * n:4 * n + 4, :], XB[2 + n][:, :].rearrange("p (g s) -> p g s", g=4),
                                            const[:, C_TRIL:C_TRIL + P].rearrange("p (o s) -> p o s", o=1).broadcast_to([P, 4, P]),
                                            ALU.mult).then_inc(sem("wsT_set"), 1)

            def first_weights():
                dve.wait_ge(sem("w00_made"), 1)
                link(nc.vector.tensor_copy(w00, XB[2][:, 0:8]))
                link(nc.vector.tensor_copy(b00, XB[2][:, 8:16]))
                dve.sem_inc(sem("w00_taken"), 1)

            for s in range(16 * SLOTS):
                lower(AB2 + s // SLOTS, s % SLOTS)
                if s < 5:
                    a_norm(15, s)
                if s == PA_AT - 1:
                    dve.wait_ge(sem("mask_a_in"), 16)
                    pa_scores(0)
                    pa_scores(1)
                    pa_probs(0)
                elif PA_AT <= s < PA_AT + 48:
                    u, part = (s - PA_AT) // 3, (s - PA_AT) % 3
                    if part == 1 and u + 2 < 16:
                        pa_scores(u + 2)
                    if part == 2 and u + 1 < 16:
                        pa_probs(u + 1)
                    if part == 2 and u == 15:
                        d_queries()
                elif DK_AT <= s < DK_AT + AG * B:
                    dk_copy(s - DK_AT)
                elif s == DS_AT:
                    d_scores()
                elif s == DS_AT + 2:
                    d_probs()
                elif s == DP_AT:
                    d_new_values()
                elif DV_AT <= s < DV_AT + AG * B:
                    b, g = (s - DV_AT) // AG, (s - DV_AT) % AG
                    if g == 1 and b >= 1:
                        d_out(b - 1)
                elif s == LN_AT - 1:
                    d_out(B - 1)
                elif s == LN_AT + 1:
                    ln_centre()
                    ws_lower()
                elif s == LN_AT + 6:
                    ln_scale()
                elif s == LN_AT + 7:
                    first_weights()
                elif s == LN_AT + 8:
                    for g in range(8):
                        link(nc.vector.tensor_scalar(rden, xc[:, g, S:T], w00[:, g:g + 1], b00[:, g:g + 1], ALU.mult, ALU.add))
                        link(nc.vector.tensor_tensor(proj[:, 48 + g, S:T], proj[:, 48 + g, S:T], rden, ALU.mult))
                elif s >= VN_AT + 4:
                    for g in range(4 * (s - VN_AT - 4), 4 * (s - VN_AT - 3)):
                        dve.wait_ge(sem("mix_made"), g + 1)
                        nc.vector.tensor_tensor(proj[:, 48 + g, 0:S], proj[:, 48 + g, 0:S], XB[g % 4][:, 0:S], ALU.mult)\
                          .then_inc(sem("mixed"), 1)
            dve.wait_ge(sem("silu"), 1)
            dve.wait_ge(sem("proj_free"), 4 + 72)
            dve.wait_ge(sem("mixed"), 8)
            for n in range(4):
                a = slice(4 * n, 4 * n + 4)
                other = scr[:, 4 * n:4 * n + 4, :] if n < 2 else proj[:, 4 * n - 8:4 * n - 4, :]
                nc.vector.tensor_tensor(cat[:, a, :], cat[:, a, :], other, ALU.mult).then_inc(sem("x_tmp"), 1)
                if n >= 1:
                    lower_x(CAT0, cat, n - 1)
            lower_x(CAT0, cat, 3)

            def add_mix(k, first):
                dve.wait_ge(sem("resid_in"), 16 * (1 + (k == H1)))
                with dve.Fori(0, 2) as i:
                    for bl in range(4):
                        lowers(i * 4 + (first + bl))
                        for j in range(2 * bl, 2 * bl + 2):
                            dve.wait_ge(sem("proj_made"), i * 8 + (4 + 2 * first + j + 1))
                            hj = proj[:, bass.ds(i * 8 + (16 + j), 1), :]
                            nc.vector.tensor_tensor(hj, hj, PJ[j % 4][:, 0:T].rearrange("p (o t) -> p o t", o=1), ALU.add)\
                              .then_inc(sem("proj_free"), 1)
                    if k == H0:
                        compressed(i, i + 5, CMP_B)
                dve.wait_ge(sem("proj_free"), 4 + 2 * first + 16)
                dve.sem_inc(sem("x_tmp"), 4)
                for g in range(4):
                    lower_x(k, hs, g)

            def gated(layer, first):
                dve.sem_inc(sem(f"h_new{layer}"), 4)
                dve.wait_ge(sem(f"ple_taken{layer}"), KC)
                for m in range(8):
                    if layer == 0 and m == 5:
                        compressed(2, 7, CMP_B)
                    lowers(first + m, range(8 if first + m < BLOCKS - 1 else 5))
                    for j in range(2 * m, 2 * m + 2):
                        dve.wait_ge(sem("proj_free"), 4 + 2 * first + j + 1)
                        link(nc.vector.tensor_tensor(scr[:, 4 + j % 4, :], scr[:, j % 4, :], proj[:, j, :], ALU.mult))
                        nc.vector.tensor_tensor(hs[:, j, :], scr[:, 4 + j % 4, :], hs[:, j, :], ALU.add).then_inc(sem(f"h_new{layer}"), 1)
            add_mix(H0, OUT0)
            gated(0, GATE0)
            normalise(1, X1, g_c)
            def kc_norm(s):
                if s == 0:
                    dve.wait_ge(sem("ks_root"), 1)
                    link(nc.vector.reciprocal(krt, krt))
                ins = nc.vector.tensor_tensor(kcmp[:, s], kcmp[:, s], krt[:, 4 * s:4 * s + 4].rearrange("p (n o) -> p n o", o=1)
                                              .broadcast_to([P, 4, P]), ALU.mult)
                if s == B - 1:
                    link(ins)
                    dve.sem_inc(step("kc_ready"), 1)

            summed = {5 + p: p for p in range(8)} | {15: 8, 16: 9, 19: 10, 20: 11}
            for m in range(20):
                for s in range(SLOTS):
                    lower(CQ + m, s)
                    if s < 5 and m in summed:
                        c_norm(summed[m], s)
                    if m == 2:
                        kc_norm(s)
            for step_ in range(5):
                c_norm(11, step_)

            def over(x, dims):
                return x.broadcast_to(dims)

            dve.wait_ge(sem("pc_root"), 1)
            link(nc.vector.reciprocal(krt[:, 0:1], krt[:, 0:1]))
            nc.vector.tensor_scalar(kcp, kcp, krt[:, 0:1], None, ALU.mult).then_inc(step("kcp_ready"), 1)
            dve.wait_ge(*done("kcpT_made"))
            nc.vector.tensor_scalar(kcpT, XB[1][:, 0:P], g_kc[:, 0:1], None, ALU.mult).then_inc(step("kcpT_set"), 1)
            for n in range(8):
                dve.wait_ge(sem("pcs_made"), n + 1)
                h = n % 4
                nc.vector.tensor_scalar(Pc[:, 4 * n:4 * n + 4, :],
                                        XB[n % 4][:, :].rearrange("p (g m) -> p g m", g=GQ)[:, :, 32 * h:32 * h + 16],
                                        SCALE, None, ALU.mult).then_inc(sem("pcs_taken"), 1)
            dve.wait_ge(sem("pcs_taken"), 8)
            Pq = Pc.rearrange("p (q h) n -> p q h n", q=2)
            vis = const[:, C_VIS:C_VIS + 32].rearrange("p (q o n) -> p q o n", q=2, o=1)
            see = const[:, C_SEE:C_SEE + 32].rearrange("p (q o n) -> p q o n", q=2, o=1)
            pmx = cmx[:, 0:32]
            link(nc.vector.tensor_tensor(Pq, Pq, over(vis, [P, 2, HQ, 16]), ALU.add))
            link(nc.vector.tensor_reduce(pmx, Pc, AX, ALU.max))
            pm3 = pmx.rearrange("p (u o) -> p u o", o=1)
            link(nc.vector.tensor_tensor(Pc, Pc, over(pm3, [P, 32, 16]), ALU.subtract))
            dve.sem_inc(step("pc_centred"), 1)
            dve.wait_ge(sem("proj_made"), 4 + 144)
            link(nc.vector.memset(spare[:, 0:1024], 0.0))
            for b in range(B):
                ins = nc.vector.tensor_copy(qzu[:, b, :, 4 * b:4 * b + 4], proj[:, 0:16, S + b].rearrange("p (h g) -> p h g", h=CH))
            link(ins)
            link(nc.vector.memset(Q[:, 0:1024], 0.0))
            for b in range(B):
                ins = nc.vector.tensor_copy(qzr[:, b, :, 4 * b:4 * b + 4], proj[:, 40:56, S + b].rearrange("p (h g) -> p h g", h=CH))
            for br, slot in enumerate((24, 32)):
                for g in range(GQ):
                    q4 = proj[:, 40:56, S:T].rearrange("p (h g) b -> p g h b", h=CH)[:, g]
                    ins = nc.vector.tensor_tensor(diag_c[:, br, :].rearrange("p (h b g) -> p g h b", h=CH, b=B)[:, g], q4,
                                                  proj[:, slot:slot + 4, S:T], ALU.mult)
            link(ins)
            dve.sem_inc(step("qz_c"), 1)
            dve.wait_ge(sem("pc_exp"), 1)
            link(nc.vector.tensor_tensor(Pq, Pq, over(see, [P, 2, HQ, 16]), ALU.mult))
            link(nc.vector.tensor_reduce(pmx, Pc, AX, ALU.add))
            link(nc.vector.tensor_scalar(pmx, pmx, TINY, None, ALU.max))
            link(nc.vector.reciprocal(pmx, pmx))
            dve.wait_ge(sem("gate_taken"), 3)
            link(nc.vector.tensor_tensor(pmx.rearrange("p (q h) -> p q h", q=2), pmx.rearrange("p (q h) -> p q h", q=2),
                                         gate_p[:, :, 0, :], ALU.mult))
            link(nc.vector.tensor_tensor(Pc, Pc, over(pm3, [P, 32, 16]), ALU.mult))
            dve.sem_inc(step("pc_p"), 1)
            dve.wait_ge(sem("c_out"), 16 * 18)
            dve.wait_ge(sem("mask_c_in"), 16)

            def cu_scores(u):
                qt, nk = u % 2, P * (u % 2 + 1)
                dve.wait_ge(sem("cu_s"), u + 1)
                if u >= 2:
                    dve.wait_ge(sem("cu_pT"), u - 1)
                m = mask[:, P * qt:P * qt + nk].rearrange("p (o n) -> p o n", o=1)
                s2 = S_c[:, qt, 0:2 * nk].rearrange("p (b n) -> p b n", b=2)
                link(nc.vector.scalar_tensor_tensor(s2, PJ[qt][:, 0:2 * nk].rearrange("p (b n) -> p b n", b=2), SCALE,
                                                    over(m, [P, 2, nk]), ALU.mult, ALU.add))
                nc.vector.tensor_reduce(nmx[:, 2 * qt:2 * qt + 2], s2, AX, ALU.max, negate=True).then_inc(sem("cu_max"), 1)

            def cu_probs(u):
                hq, qt, nk = u // 2, u % 2, P * (u % 2 + 1)
                dve.wait_ge(sem("cu_exp"), 2 * u + 2)
                rd = rden[:, 2 * qt:2 * qt + 2]
                link(nc.vector.reciprocal(rd, den[:, 2 * qt:2 * qt + 2]))
                link(nc.vector.tensor_tensor(rd, rd, gate_p[:, qt, 1:3, hq], ALU.mult))
                s2 = S_c[:, qt, 0:2 * nk].rearrange("p (b n) -> p b n", b=2)
                nc.vector.tensor_tensor(s2, s2, over(rd.rearrange("p (b o) -> p b o", o=1), [P, 2, nk]), ALU.mult).then_inc(sem("cu_p"), 1)

            def sc_scores():
                dve.wait_ge(*done("scmp_made"))
                link(nc.vector.tensor_scalar(S_cmp, XB[0][:, 0:P], SCALE, None, ALU.mult))
                link(nc.vector.tensor_scalar(s_new, XB[1][:, 0:2], SCALE, None, ALU.mult))
                nc.vector.tensor_reduce(mx_c[:, 0:1], S_cmp[:, 0:NCMP], AX, ALU.max, negate=True).then_inc(sem("sc_max"), 1)

            def sc_probs():
                dve.wait_ge(sem("sc_exp"), 1)
                link(nc.vector.memset(S_cmp[:, NCMP:P], 0.0))
                link(nc.vector.tensor_scalar(rd_c[:, 0:1], den_c[:, 0:1], TINY, None, ALU.max))
                link(nc.vector.reciprocal(rd_c[:, 0:1], rd_c[:, 0:1]))
                link(nc.vector.tensor_scalar(S_cmp, S_cmp, rd_c[:, 0:1], None, ALU.mult))
                dve.sem_inc(step("scmp_p"), 1)

            def sc_ranks():
                dve.wait_ge(*done("imp_made"))
                link(nc.vector.tensor_copy(imp, XB[1][:, 0:NPICK]))
                imp_i = over(imp.rearrange("p (o i) -> p o i", o=1), [P, NPICK, NPICK])
                imp_j = over(imp.rearrange("p (j o) -> p j o", o=1), [P, NPICK, NPICK])
                link(nc.vector.tensor_tensor(gt, imp_i, imp_j, ALU.is_gt))
                link(nc.vector.tensor_tensor(eq, imp_i, imp_j, ALU.is_equal))
                link(nc.vector.tensor_tensor(eq, eq, mask[:, M_CAUSAL:].rearrange("p (j i) -> p j i", j=NPICK), ALU.mult))
                link(nc.vector.tensor_tensor(gt, gt, eq, ALU.add))
                link(nc.vector.tensor_reduce(rank, gt, AX, ALU.add))
                link(nc.vector.memset(sneg, 0.0))
                link(nc.vector.tensor_scalar(sneg[:, 1:1 + NPICK], rank, float(TOP), NEG, ALU.is_ge, ALU.mult))
                dve.wait_ge(sem("gate_s_in"), 16 * 12)
                link(nc.vector.tensor_scalar(S_cmp, S_cmp, gate_s[:, 0:1], None, ALU.mult))
                for h in range(CH):
                    own = const[:, C_ROW + h:C_ROW + h + 1]
                    ins = nc.vector.tensor_scalar(P_exp[:, :, h, :], S_cmp.rearrange("p (a i) -> p a i", a=4), own, None, ALU.mult)
                link(ins)
                dve.sem_inc(step("pexp_ready"), 1)


            def k_odd(steps):
                for k in steps:
                    if k % 32 == 1 and k > 32:
                        take_scores(k // 32 - 1)
                    if k % 2 == 1:
                        dve.wait_ge(sem("kt_T"), 8 + k + 1)
                        if k >= CH:
                            dve.wait_ge(sem("kt_used"), k - CH + 1)
                        nc.vector.tensor_copy(KTc[:, k % CH, :], XB[1 + k % 3][:, :]).then_inc(sem("kt_odd"), 1)

            def take_scores(c):
                dve.wait_ge(sem("kt_used"), 32 * c + 32)
                src = XB[0][:, :]
                if c < 4:
                    nc.vector.tensor_tensor(S_sel[:, 512 * c:512 * c + 512].rearrange("p (j n) -> p j n", j=8),
                                            src.rearrange("p (j n) -> p j n", j=8),
                                            over(sneg[:, 8 * c:8 * c + 8].rearrange("p (j o) -> p j o", o=1), [P, 8, SB_]),
                                            ALU.add).then_inc(sem("S_taken"), 1)
                    dve.wait_ge(sem("S_taken"), c + 1)
                    nc.vector.tensor_reduce(cmx[:, c:c + 1], S_sel[:, 512 * c:512 * c + 512], AX, ALU.max)
                else:
                    link(nc.vector.tensor_copy(S_win, src))
                    link(nc.vector.tensor_reduce(cmx[:, c:c + 1], S_win, AX, ALU.max))

            sc_scores()
            cu_scores(0)
            cu_scores(1)
            sc_probs()
            cu_probs(0)
            for u in range(32):
                if u == K_FROM - 2:
                    sc_ranks()
                before, after = k_steps(u)
                k_odd(before)
                if u + 1 < 32:
                    cu_probs(u + 1)
                k_odd(after[:2])
                if u + 2 < 32:
                    cu_scores(u + 2)
                k_odd(after[2:])
            take_scores(4)
            for br, chunks in enumerate((cmx[:, 0:4], cmx[:, 4:5])):
                link(nc.vector.tensor_reduce(mx_c[:, 1 + br:2 + br], chunks, AX, ALU.max))
                link(nc.vector.tensor_scalar(mx_c[:, 1 + br:2 + br], mx_c[:, 1 + br:2 + br], SCALE, None, ALU.mult))
                link(nc.vector.tensor_tensor(mx_c[:, 1 + br:2 + br], mx_c[:, 1 + br:2 + br], s_new[:, br:br + 1], ALU.max))
                link(nc.vector.tensor_scalar(mx_c[:, 1 + br:2 + br], mx_c[:, 1 + br:2 + br], -1.0, None, ALU.mult))
                dve.sem_inc(sem("sw_max"), 1)
            dve.wait_ge(sem("sw_exp"), 4)
            link(nc.vector.tensor_tensor(rd_c[:, 1:3], den_c[:, 1:3], p_new, ALU.add))
            link(nc.vector.reciprocal(rd_c[:, 1:3], rd_c[:, 1:3]))
            link(nc.vector.tensor_tensor(rd_c[:, 1:3], rd_c[:, 1:3], gate_s[:, 1:3], ALU.mult))
            link(nc.vector.tensor_tensor(p_new, p_new, rd_c[:, 1:3], ALU.mult))
            link(nc.vector.tensor_scalar(S_sel, S_sel, rd_c[:, 1:2], None, ALU.mult))
            link(nc.vector.tensor_scalar(S_win, S_win, rd_c[:, 2:3], None, ALU.mult))
            for br in range(2):
                link(nc.vector.tensor_scalar(diag_c[:, br, :], ident, p_new[:, br:br + 1], None, ALU.mult))
            dve.sem_inc(step("sw_p"), 1)
            dve.wait_ge(*done("vn_made"))
            for br, slot in enumerate((28, 36)):
                dst = vnew if br == 0 else diag_c[:, 0, :]
                for g in range(GQ):
                    ins = nc.vector.tensor_tensor(dst.rearrange("p (h b g) -> p g h b", h=CH, b=B)[:, g],
                                                  XB[2][:, tileT(br)].rearrange("p (h b g) -> p g h b", h=CH, b=B)[:, g],
                                                  proj[:, slot:slot + 4, S:T], ALU.mult)
                link(ins)
            link(nc.vector.tensor_tensor(vnew, vnew, diag_c[:, 0, :], ALU.add))
            dve.sem_inc(step("vnew_set"), 1)
            vn4 = vnew.rearrange("p (h b g) -> p b h g", h=CH, b=B)
            with dve.Fori(0, 4) as i:
                for b2 in range(2):
                    lowers(i * 2 + (CZ + b2))
                    dve.wait_ge(sem("set_used"), i * 10 + (2 + 5 * b2 + 5))
                    nc.vector.tensor_copy(O_c[:, b2, :], XB[b2][:, 0:P]).then_inc(sem("O_taken"), 1)
                    dve.wait_ge(sem("OT_made"), i * 2 + (b2 + 1))
                    src = XB[2 + b2][:, 0:P].rearrange("p (h b g) -> p b h g", h=CH, b=B)[:, bass.ds(i * 2 + b2, 1)].rearrange("p o h g -> p (o h) g")
                    new = vn4[:, bass.ds(i * 2 + b2, 1)].rearrange("p o h g -> p (o h) g")
                    dst = proj[:, 40:56, bass.ds(i * 2 + (b2 + S), 1)].rearrange("p (h g) o -> p h (g o)", h=CH)
                    nc.vector.tensor_tensor(dst, src, new, ALU.add).then_inc(sem("OT_taken"), 1)
            dve.wait_ge(sem("OT_taken"), 2 + B)
            dve.wait_ge(sem("proj_free"), 4 + 160)
            for n in range(4):
                a = slice(4 * n, 4 * n + 4)
                nc.vector.tensor_tensor(cat[:, a, :], cat[:, a, :], proj[:, a, :], ALU.mult).then_inc(sem("x_tmp"), 1)
                if n >= 1:
                    lower_x(CAT1, cat, n - 1)
            lower_x(CAT1, cat, 3)
            add_mix(H1, OUT1)
            gated(1, GATE1)

        @block.tensor
        def _(pe):
            pe.wait_ge(sem("consts_in"), 16)
            pe.wait_ge(sem("gains_in"), 16 * 7)
            nc.tensor.transpose(XB[3][:, 0:NG], scr[0:NG, 7, 0:P], ident[0:NG, 0:NG]).then_inc(sem("xT_made"), 1)
            pe.wait_ge(sem("x_in"), 96)
            for c in range(KC + 2):
                src, k = (x_nat, c) if c < KC else (p_nat, c - KC)
                if c == 3:
                    pe.wait_ge(sem("gains_set"), 1)
                if c >= 4:
                    pe.wait_ge(sem("xT_taken"), c - 3)
                for t in range(3):
                    rows = P if t < 2 else B
                    ins = nc.tensor.transpose(XB[c % 4][:, t * P:t * P + rows], src[0:rows, t, tileT(k)], ident[0:rows, 0:rows])
                ins.then_inc(sem("xT_made"), 1)
            pe.wait_ge(sem("ones_set"), 2)
            pe.wait_ge(sem("xT_taken"), KC + 2)

            def rms(layer, dst, chunks):
                for c in chunks:
                    pe.wait_ge(sem(f"rms_sq{layer}"), c + 1)
                    ins = nc.tensor.matmul(dst[:, 0:T], ones[:, :], tmp_n[:, c, :], start=(c == 0), stop=(c == KC - 1))
                if chunks[-1] == KC - 1:
                    ins.then_inc(sem(f"rms_sum{layer}"), 1)

            rms(0, XB[0], range(KC))

            def columns(bl, n, beside=None, operand=None):
                for e in range(SLOTS):
                    if operand is not None and e % 2 == 0:
                        pe.wait_ge(sem("x_lo"), 4 * operand + e // 2 + 1)
                    pe.wait_ge(sem("w_lo"), n * 8 + (8 + e + 1))
                    for c in range(2):
                        if e == 0:
                            pe.wait_ge(sem("proj_free"), n * 2 + (c + 1))
                        for k in range(EB):
                            kx = e * EB + k
                            for w, x in ((w_up, xh), (w_up, xl), (w_low, xh)):
                                ins = nc.tensor.matmul(PJ[(2 * bl + c) % 4][:, 0:T], w[:, e % NE, k, tileT(c)], x[:, kx, :],
                                                       start=(kx == 0 and w is w_up and x is xh),
                                                       stop=(kx == KC - 1 and w is w_low))
                        if e == SLOTS - 1:
                            ins.then_inc(sem("proj_made"), 1)
                        elif c == 1:
                            ins.then_inc(sem("w_used"), 1)
                    if beside is not None:
                        beside(e)

            def projection(k, first, beside=None):
                for m in range(8):
                    columns(m % 4, first + m, beside and (lambda s: beside(m, s)), k if m == 0 else None)

            def compress(r, bl, n, free, loads):
                pg = 4 * bl + n
                pe.wait_ge(sem(f"c_in{n}"), r * 64 + (16 * loads + 16 * (bl + 1)))
                if pg == 0:
                    pe.wait_ge(sem("cmp_free"), r + free)
                for v in range(2):
                    for lo, grp in ([(0, pg // 4 - 1)] if n == 0 and pg else []) + [(32 - 8 * (pg % 4), pg // 4)]:
                        for h in range(CH):
                            ins = nc.tensor.matmul(XB[v][32 * h:32 * h + 32, tileT(grp)], wide[:, v, lo:lo + 32, h],
                                                   cring[:, n, (v * CH + h) * P:(v * CH + h + 1) * P],
                                                   start=(pg == 0), stop=(pg == NPG - 1), skip_group_check=True)
                ins.then_inc(sem("c_used"), 1)

            pe.wait_ge(sem("wide_in"), 16 * 32)

            def ab1_round(r, norm):
                for bl in range(4):
                    def beside(s):
                        if s % 2 == 1:
                            compress(r, bl, s // 2, 1, 0)
                        if s == SLOTS - 1 and norm:
                            pe.wait_ge(sem("qn_sq"), (r - 1) * 4 + (bl + 1))
                            pe.wait_ge(sem("qn_root"), (r - 1) * 8 + (2 + 2 * bl))
                            for c in range(2):
                                nc.tensor.matmul(XB[2 + c][:, 0:T], ones[:, :], scr[:, 2 * bl + c, :], start=True, stop=True)\
                                  .then_inc(sem("qn_sum"), 1)
                    columns(bl, r * 4 + bl, beside, X0 if not norm and bl == 0 else None)

            ab1_round(0, False)
            with pe.Fori(0, 3) as i:
                ab1_round(i + 1, True)
            ab1_round(4, True)

            def natural(t):
                if t == 0:
                    pe.wait_ge(sem("cmp_free"), 6)
                    pe.wait_ge(sem("qn_root"), 2 + 32)
                    pe.wait_ge(sem("proj_free"), 4 + 40)
                if t == 8:
                    pe.wait_ge(sem("qn_done"), 4 + 16)
                if t >= 4:
                    pe.wait_ge(sem("nat_taken"), 2 * (t - 3))
                for c in range(3):
                    rows = P if c < 2 else B
                    ins = nc.tensor.transpose(XB[t % 4][0:rows, tileT(c)], proj[:, (32 + t if t < 8 else 16 + t), c * P:c * P + rows], ident)
                ins.then_inc(sem("nat_made"), 1)

            def pa_scores(u):
                h, qt = u // 2, u % 2
                if u >= 2:
                    pe.wait_ge(sem("pa_max"), u - 1)
                for g in range(AG):
                    nk = P * (qt + 1)
                    out = XB[0][:, g * P:(g + 1) * P] if qt == 0 else XB[1 + g // 2][:, (g % 2) * 256:(g % 2) * 256 + 256]
                    ins = nc.tensor.matmul(out, proj[:, 8 * g + h, tileT(qt)], proj[:, 24 + h, 0:nk], start=True, stop=True)
                ins.then_inc(sem("pa_s"), 1)

            def pa_probs(u):
                qt = u % 2
                pe.wait_ge(sem("pa_p"), u + 1)
                if u >= 1:
                    pe.wait_ge(sem("pa_o_taken"), u)
                for k in range(qt + 1):
                    ins = nc.tensor.transpose(XB[3][:, tileT(k)], S_sb[:, qt, tileT(k)], ident)
                ins.then_inc(sem("pa_pT"), 1)

            def pa_values(u):
                h, qt = u // 2, u % 2
                pe.wait_ge(sem("pa_pT_taken"), u + 1)
                for k in range(qt + 1):
                    ins = nc.tensor.matmul(XB[3][:, 384:512], proj[:, 32 + h, tileT(k)], PT[:, qt, tileT(k)],
                                           start=(k == 0), stop=(k == qt))
                ins.then_inc(sem("pa_o"), 1)

            def dk_scores(n):
                b, g = n // AG, n % AG
                if n == 0:
                    pe.wait_ge(sem("qz_set"), 1)
                pe.wait_ge(sem("dk_T_taken"), n + 1)
                pe.wait_ge(sem("dk_T_taken2"), n + 1)
                for h in range(AH):
                    j = h % 4
                    ins = nc.tensor.matmul(XB[h // 4][32 * j:32 * j + B, tileT(g)], qz[:, g, b, h, :],
                                           KT[:, n % 2, tileT(h)], start=False, stop=True, skip_group_check=True)
                ins.then_inc(sem("c_used"), 1)

            def dk_T(n):
                if n == 0:
                    pe.wait_ge(sem("pa_o_taken"), 16)
                    for u in range(2):
                        nc.tensor.matmul(XB[u][:, :], zrow[0:1, 0:P], zrow[0:1, :], start=True, stop=True)
                pe.wait_ge(sem(f"c_in{n % NP}"), 16 * (20 + n // NP + 1))
                for h in range(AH):
                    ins = nc.tensor.transpose(XB[2 + h // 4][:, tileT(h % 4)], cring[:, n % NP, tileT(h)], ident)
                ins.then_inc(sem("dk_T"), 1)

            def d_new_scores():
                for g in range(AG):
                    for u in range(2):
                        ins = nc.tensor.matmul(XB[u][:, 384 + g:385 + g], prod[:, g, u, :], ones[:, 0:1],
                                               start=False, stop=True, skip_group_check=True)
                ins.then_inc(sem("d_s"), 1)

            def d_probs():
                pe.wait_ge(sem("d_p"), 1)
                for g in range(AG):
                    for u in range(2):
                        ins = nc.tensor.transpose(XB[2 + g // 2][:, (g % 2) * 256 + u * P:(g % 2) * 256 + (u + 1) * P],
                                                  Sd[:, u, tileT(g)], ident)
                ins.then_inc(sem("d_pT"), 1)
                for u in range(2):
                    ins = nc.tensor.matmul(XB[1][:, tileT(u)], ones[:, :], diag[:, u, :], start=True, stop=True)
                ins.then_inc(sem("d_new"), 1)

            def dO_T(b):
                pe.wait_ge(sem("dO_taken"), b + 1)
                if b >= 2:
                    pe.wait_ge(sem("oTd"), b - 1)
                for u in range(2):
                    ins = nc.tensor.transpose(XB[2 + b % 2][:, tileT(u)], Od[:, b % 2, tileT(u)], ident)
                ins.then_inc(sem("dO_T"), 1)

            def dv(n):
                b, g = n // AG, n % AG
                if n == 0:
                    pe.wait_ge(sem("d_pT_taken"), 2)
                    pe.wait_ge(sem("d_new_taken"), 1)
                if b >= 2:
                    pe.wait_ge(sem("dO_taken"), b - 1)
                pe.wait_ge(sem(f"c_in{n % NP}"), 16 * (26 + n // NP + 1))
                for h in range(AH):
                    u, j = h // 4, h % 4
                    ins = nc.tensor.matmul(XB[b % 2][32 * j:32 * j + 32, tileT(u)], PTd[:, g, u, 32 * j:32 * j + 32],
                                           cring[:, n % NP, tileT(h)], start=(g == 0 and u == 0), stop=(g == AG - 1),
                                           skip_group_check=True)
                ins.then_inc(sem("c_used"), 1)

            def ln_mean():
                pe.wait_ge(sem("proj_free"), 4 + 64)
                pe.wait_ge(sem("dO_taken"), B)
                for g in range(8):
                    ins = nc.tensor.matmul(XB[0][:, 0:T], ones[:, :], xc[:, g, :], start=(g == 0), stop=(g == 7))
                ins.then_inc(sem("ln_sum"), 1)

            def ws_T():
                pe.wait_ge(sem("ws_in"), 32)
                pe.wait_ge(sem("oTd"), B)
                for g in range(8):
                    ins = nc.tensor.transpose(XB[2 + g // 4][:, tileT(g % 4)], ws_nat[:, g, :], ident)
                    if g % 4 == 3:
                        ins.then_inc(sem("ws_T"), 1)

            def ln_var():
                pe.wait_ge(sem("ln_sq"), 1)
                for g in range(8):
                    ins = nc.tensor.matmul(XB[1][:, 0:T], ones[:, :], sq8[:, g, :], start=(g == 0), stop=(g == 7))
                ins.then_inc(sem("ln_sum"), 1)

            def first_weights():
                pe.wait_ge(sem("wsT_set"), 2)
                nc.tensor.matmul(XB[2][:, 0:8], ones[0:1, :], wsT[0:1, :, 0], start=True, stop=True)
                nc.tensor.matmul(XB[2][:, 8:16], ones[0:1, :], bs.rearrange("p (g t) -> p g t", g=8)[:, :, 0],
                                 start=True, stop=True).then_inc(sem("w00_made"), 1)

            def vn_T(g):
                pe.wait_ge(sem("vn_ready"), 1)
                if g >= 2:
                    pe.wait_ge(sem("vn_taken"), 2 * (g - 1))
                for c in range(3):
                    rows = P if c < 2 else B
                    ins = nc.tensor.transpose(XB[g % 2][0:rows, tileT(c)], xc[:, g, c * P:c * P + rows], ident)
                ins.then_inc(sem("vn_T"), 1)

            def mix(g):
                if g == 0:
                    pe.wait_ge(sem("vn_taken"), 16)
                    pe.wait_ge(sem("w00_taken"), 1)
                if g >= 4:
                    pe.wait_ge(sem("mixed"), g - 3)
                for c in range(2):
                    nc.tensor.matmul(XB[g % 4][:, tileT(c)], vn_nat[:, c, tileT(g)], wsT[:, g, :], start=True, stop=False)
                    ins = nc.tensor.matmul(XB[g % 4][:, tileT(c)], ones[0:1, :], bs[:, tileT(g)], start=False, stop=True)
                ins.then_inc(sem("mix_made"), 1)

            def beside_ab2(s):
                if s < PA_AT:
                    natural(2 * s)
                    natural(2 * s + 1)
                    if s == PA_AT - 1:
                        pe.wait_ge(sem("nat_taken"), 32)
                        pa_scores(0)
                        pa_scores(1)
                elif s < PA_AT + 48:
                    u, part = (s - PA_AT) // 3, (s - PA_AT) % 3
                    if part == 0:
                        pa_probs(u)
                    elif part == 1:
                        pa_values(u)
                        if u + 2 < 16:
                            pa_scores(u + 2)
                elif DK_AT <= s <= DK_AT + AG * B:
                    if s > DK_AT:
                        dk_scores(s - DK_AT - 1)
                    if s < DK_AT + AG * B:
                        dk_T(s - DK_AT)
                elif s == DS_AT:
                    d_new_scores()
                elif s == DP_AT:
                    d_probs()
                elif DV_AT <= s < DV_AT + AG * B:
                    dv(s - DV_AT)
                    b, g = (s - DV_AT) // AG, (s - DV_AT) % AG
                    if g == 1 and b >= 1:
                        dO_T(b - 1)
                elif s == LN_AT - 1:
                    dO_T(B - 1)
                elif s == LN_AT:
                    ln_mean()
                elif s == LN_AT + 1:
                    ws_T()
                elif s == LN_AT + 4:
                    ln_var()
                elif s == LN_AT + 5:
                    first_weights()
                elif VN_AT <= s < VN_AT + 4:
                    vn_T(2 * (s - VN_AT))
                    vn_T(2 * (s - VN_AT) + 1)
                elif s >= VN_AT + 4:
                    for g in range(4 * (s - VN_AT - 4), 4 * (s - VN_AT - 3)):
                        mix(g)

            for m in range(16):
                columns(m % 4, AB2 + m, lambda s: beside_ab2(m * SLOTS + s))
            def beside_out(m, s):
                if s % 2 == 1:
                    compress(m // 4, m % 4, s // 2, 6, 32)
            projection(CAT0, OUT0, beside_out)
            pe.wait_ge(sem("cmp_free"), 8)

            def ple(layer):
                pe.wait_ge(sem("wple_in"), 16 * (layer + 1))
                for c in range(KC):
                    if c >= 4:
                        pe.wait_ge(sem(f"ple_taken{layer}"), c - 3)
                    for k in range(2):
                        ins = nc.tensor.matmul(XB[c % 4][:, 0:T], wple[:, k, tileT(c)], pT[:, k, :], start=(k == 0), stop=(k == 1))
                    ins.then_inc(sem(f"ple_made{layer}"), 1)
            ple(0)
            pe.wait_ge(sem("ple_taken0"), KC)

            def beside_gate(m, s):
                if m < 4:
                    beside_out(8 + m, s)
                if m >= 2 and s >= 6:
                    c = 2 * (m - 2) + s - 6
                    rms(1, XB[3], range(c, c + 1))
            projection(H0, GATE0, beside_gate)
            pe.wait_ge(sem("cmp_free"), 9)

            pe.wait_ge(sem("p_in"), 48)
            pe.wait_ge(sem("ple_taken0"), KC)
            for k in range(2):
                for c in range(3):
                    rows = P if c < 2 else B
                    ins = nc.tensor.transpose(XB[1 + k][:, c * P:c * P + rows], p_nat1[0:rows, c, tileT(k)], ident[0:rows, 0:rows])
                ins.then_inc(sem("pT_made"), 1)
            rms(1, XB[3], range(KC - 4, KC))
            pe.wait_ge(sem("pT_taken"), 2)

            def kcT(b):
                pe.wait_ge(*done("kc_ready"))
                if b >= 2:
                    pe.wait_ge(sem("kcT_taken"), b - 1)
                for a in range(4):
                    ins = nc.tensor.transpose(XB[b % 2][:, tileT(a)], kcmp[:, b, a, :], ident)
                ins.then_inc(sem("kcT_made"), 1)

            def cn_sums(p, odd):
                pe.wait_ge(sem("cn_sq"), p + 1)
                pe.wait_ge(sem("cn_root"), p * 2 + 2)
                for c in range(2):
                    nc.tensor.matmul(XB[2 + c][:, 0:T], ones[:, :], scr[:, 2 * odd + c, :], start=True, stop=True)\
                      .then_inc(sem("cn_sum"), 1)

            def natural_c(n):
                t = NAT[n]
                if n == 0:
                    pe.wait_ge(sem("kcT_taken"), B)
                if n == 12:
                    pe.wait_ge(sem("cn_done"), 2 + 10)
                if n == 16:
                    pe.wait_ge(sem("cn_root"), 2 + 24)
                    pe.wait_ge(sem("proj_free"), 4 + 144)
                if n == 20:
                    pe.wait_ge(sem("cn_done"), 2 + 12)
                if n >= 2:
                    pe.wait_ge(sem("cnat_taken"), 2 * (n - 1))
                for c in range(3):
                    rows = P if c < 2 else B
                    ins = nc.tensor.transpose(XB[n % 2 + (2 if n >= 16 else 0)][0:rows, tileT(c)],
                                              proj[:, 16 + t, c * P:c * P + rows], ident)
                ins.then_inc(sem("cnat_made"), 1)

            def cq_block(r, bl, beside, operand=None):
                columns(bl, r * 4 + (CQ + bl), beside, operand)

            def beside_q(bl, s):
                if bl == 3 and s >= 4:
                    for b in range(2 * s - 8, 2 * s - 6):
                        kcT(b)

            for bl in range(4):
                cq_block(0, bl, lambda s: beside_q(bl, s), X1 if bl == 0 else None)
            with pe.Fori(0, 2) as i:
                for bl in range(4):
                    cq_block(i + 1, bl, lambda s: cn_sums(i * 4 + bl, bl % 2) if s == SLOTS - 1 else None)

            def beside_rows(r, bl, s):
                if bl < 2 and s % 2 == 1:
                    natural_c(8 * (r - 3) + 4 * bl + s // 2)
                elif bl >= 2 and s == SLOTS - 1:
                    cn_sums(8 + 2 * (r - 3) + bl - 2, bl % 2)
                elif r == 4 and bl == 2 and s == 3:
                    compress_prompt()

            def compress_prompt():
                pe.wait_ge(sem("cnat_taken"), 32)
                for pg in range(2):
                    lo = 32 - 8 * pg
                    for h in range(CH):
                        nc.tensor.matmul(XB[0][32 * h:32 * h + 32, 0:P], wide[:, 0, lo:lo + 32, h], proj[:, 16 + h, tileT(pg)],
                                         start=(pg == 0), stop=(pg == 1), skip_group_check=True)
                        ins = nc.tensor.matmul(XB[1][0:32, tileT(h)], wide[:, 1, lo:lo + 32, h], proj[:, 20 + h, tileT(pg)],
                                               start=(pg == 0 and h == 0), stop=(pg == 1), skip_group_check=True)
                ins.then_inc(step("pc_made"), 1)

            for r in (3, 4):
                for bl in range(4):
                    cq_block(r, bl, lambda s: beside_rows(r, bl, s))
            for n in range(16, 20):
                natural_c(n)
            pe.wait_ge(sem("wg_in"), 16)
            for k in range(KC):
                for x in (xh, xl):
                    ins = nc.tensor.matmul(PJ[0][0:48, 0:T], wg[:, k, :], x[:, k, :].bitcast(F32), start=(k == 0 and x is xh),
                                           stop=(k == KC - 1 and x is xl))
            ins.then_inc(step("gT_made"), 1)
            for n in range(20, 24):
                natural_c(n)
            pe.wait_ge(sem("gT_set"), 1)
            for c in range(3):
                rows = P if c < 2 else B
                ins = nc.tensor.transpose(PJ[1][0:rows, 64 * c:64 * c + 48], gT[:, c * P:c * P + rows], ident[0:48, 0:48])
            ins.then_inc(step("gate_made"), 1)
            pe.wait_ge(*done("kcp_ready"))
            pe.wait_ge(sem("vcp_set"), 1)
            nc.tensor.transpose(XB[1][:, 0:P], kcp, ident).then_inc(step("kcpT_made"), 1)
            pe.wait_ge(*done("kcpT_set"))
            pe.wait_ge(sem("cnat_taken"), 48)
            pe.wait_ge(sem("gate_taken"), 3)
            for n in range(8):
                if n >= 4:
                    pe.wait_ge(sem("pcs_taken"), n - 3)
                for g in range(GQ):
                    ins = nc.tensor.matmul(XB[n % 4][:, tileT(g)], proj[:, 4 * (n % 4) + g, tileT(n // 4)], kcpT, start=True, stop=True)
                ins.then_inc(sem("pcs_made"), 1)
            pe.wait_ge(sem("pcs_taken"), 8)

            pe.wait_ge(*done("qz_c"))
            for b in range(B):
                for h in range(CH):
                    nc.tensor.matmul(XB[0][32 * h:32 * h + 32, 0:P].rearrange("p (a i) -> p a i", a=4), qzu[:, b, h, :],
                                     kcmp[:, b, :, 32 * h:32 * h + 32], start=(b == 0), stop=(b == B - 1), skip_group_check=True)
            for br in range(2):
                ins = nc.tensor.matmul(XB[1][:, br:br + 1], diag_c[:, br, :], ones[:, 0:1], start=True, stop=True)
            ins.then_inc(step("scmp_made"), 1)

            def cu_scores(u):
                hq, qt = u // 2, u % 2
                nk = P * (qt + 1)
                if u >= 2:
                    pe.wait_ge(sem("cu_max"), u - 1)
                for br, slot in enumerate((24, 32)):
                    ins = nc.tensor.matmul(PJ[qt][:, br * nk:(br + 1) * nk], proj[:, 40 + hq, tileT(qt)],
                                           proj[:, slot + hq // GQ, 0:nk], start=True, stop=True)
                ins.then_inc(sem("cu_s"), 1)

            def cu_probs(u):
                hq, qt = u // 2, u % 2
                pe.wait_ge(sem("cu_p"), u + 1)
                if u >= 1:
                    pe.wait_ge(sem("cu_o_taken"), u)
                nc.tensor.transpose(PJ[3][0:16, 0:P], Pc[:, 16 * qt + hq, :], ident)
                for k in range(2 * (qt + 1)):
                    ins = nc.tensor.transpose(PJ[2][:, tileT(k)], S_c[:, qt, tileT(k)], ident)
                ins.then_inc(sem("cu_pT"), 1)

            def cu_values(u):
                hq, qt = u // 2, u % 2
                h = hq // GQ
                pe.wait_ge(sem("cu_pT_taken"), 2 * u + 2)
                nc.tensor.matmul(PJ[3][:, P:2 * P], vcp[0:16, h, :], PcT[:, qt, :], start=True, stop=False)
                for k in range(2 * (qt + 1)):
                    br, kt = k // (qt + 1), k % (qt + 1)
                    ins = nc.tensor.matmul(PJ[3][:, P:2 * P], proj[:, (28, 36)[br] + h, tileT(kt)], PT_c[:, qt, tileT(k)],
                                           start=False, stop=(k == 2 * qt + 1))
                ins.then_inc(sem("cu_o"), 1)

            def key_scores(k):
                c, b, h = k // 32, k % 32 // CH, k % CH
                if k % 32 == 0 and c >= 1:
                    pe.wait_ge(sem("S_taken"), c)
                pe.wait_ge(sem("kt_odd" if k % 2 else "kt_even"), k // 2 + 1)
                nc.tensor.matmul(XB[0][32 * h:32 * h + 32, :], qzr[:, b, h, :], KTc[:, h, :],
                                 start=(b == 0), stop=(b == B - 1), skip_group_check=True).then_inc(sem("kt_used"), 1)

            def keys(steps):
                for k in steps:
                    n, h = k // CH, k % CH
                    if h == 0:
                        pe.wait_ge(sem(f"set_in{n % 2}"), 64 * (n // 2 + 1))
                    if k >= 3:
                        pe.wait_ge(sem("kt_even" if k % 2 else "kt_odd"), (k - 3) // 2 + 1)
                    for q in range(4):
                        ins = nc.tensor.transpose(XB[1 + k % 3][:, tileT(q)], hring[:, 4 * (n % 2) + q, tileT(h)], ident)
                    ins.then_inc(sem("kt_T"), 1)
                    if k >= 1:
                        key_scores(k - 1)

            pe.wait_ge(*done("pc_p"))
            cu_scores(0)
            cu_scores(1)
            pe.wait_ge(*done("scmp_p"))
            nc.tensor.matmul(XB[0][:, 128:256], S_cmp, const[:, C_GRP:C_GRP + P], start=True, stop=True).then_inc(step("psum_made"), 1)
            for u in range(32):
                if u == K_FROM - 1:
                    pe.wait_ge(*done("pexp_ready"))
                    for a in range(4):
                        ins = nc.tensor.transpose(XB[3][:, tileT(a)], P_exp[:, a].rearrange("p h i -> p (h i)"), ident)
                    ins.then_inc(step("ptexp_made"), 1)
                if u == K_FROM:
                    pe.wait_ge(sem("ptexp_taken"), 1)
                before, after = k_steps(u)
                cu_probs(u)
                keys(before)
                cu_values(u)
                if u + 2 < 32:
                    cu_scores(u + 2)
                keys(after)
                if u == 0:
                    pe.wait_ge(sem("psum_taken"), 1)
                    nc.tensor.matmul(XB[1][:, 0:NPICK], P_sum[0:NCMP, :], const[0:NCMP, C_C2S:C_C2S + NPICK], start=True, stop=True)\
                      .then_inc(step("imp_made"), 1)
            key_scores(K_STEPS - 1)
            pe.wait_ge(sem("cu_o_taken"), 32)
            pe.wait_ge(*done("sw_p"))
            for q in range(5):
                if q == 4:
                    pe.wait_ge(sem("sw_pT_taken"), 1)
                for a in range(4):
                    src = S_sel[:, tileT(4 * q + a)] if q < 4 else S_win[:, tileT(a)]
                    ins = nc.tensor.transpose(XB[q % 4][:, tileT(a)], src, ident)
                ins.then_inc(sem("sw_pT"), 1)
            pe.wait_ge(sem("sw_pT_taken"), 5)
            for br in range(2):
                ins = nc.tensor.matmul(XB[2][:, tileT(br)], ones[:, :], diag_c[:, br, :], start=True, stop=True)
            ins.then_inc(step("vn_made"), 1)
            pe.wait_ge(*done("vnew_set"))
            def first_values(i, b2):
                for a in range(4):
                    nc.tensor.matmul(XB[b2][:, 0:P], PT_exp[:, a, :], vcmp[:, bass.ds(i * 2 + b2, 1), a, :].rearrange("p o d -> p (o d)"),
                                     start=(a == 0), stop=False, skip_group_check=True)

            def values(i, b2, k):
                n = 5 * b2 + k
                pe.wait_ge(sem(f"set_in{n % 2}"), i * 320 + (20 * 64 + 64 * (n // 2 + 1)))
                for q in range(4):
                    lhs = PT_sel[:, 4 * k + q, :] if k < 4 else PT_win[:, q, :]
                    for h in range(CH):
                        ins = nc.tensor.matmul(XB[b2][32 * h:32 * h + 32, 0:P], lhs[:, 32 * h:32 * h + 32],
                                               hring[:, 4 * (n % 2) + q, tileT(h)], start=False,
                                               stop=(k == 4 and q == 3), skip_group_check=True)
                ins.then_inc(sem("set_used"), 1)

            def beside_z(i, b2, s):
                if s == 0:
                    pe.wait_ge(sem("OT_taken"), i * 2 + (b2 + 1))
                    first_values(i, b2)
                if s in (0, 2, 3, 5, 6):
                    values(i, b2, (0, 2, 3, 5, 6).index(s))
                if s == 7:
                    pe.wait_ge(sem("O_taken"), i * 2 + (b2 + 1))
                    nc.tensor.transpose(XB[2 + b2][:, 0:P], O_c[:, b2, :], ident).then_inc(sem("OT_made"), 1)

            with pe.Fori(0, 4) as i:
                for b2 in range(2):
                    columns(b2, i * 2 + (CZ + b2), lambda s: beside_z(i, b2, s))
            projection(CAT1, OUT1)
            ple(1)
            projection(H1, GATE1)
            for c in range(KC):
                if c >= 4:
                    pe.wait_ge(sem("y_taken"), 2 * (c - 3))
                if c == 0:
                    pe.wait_ge(sem("ple_taken1"), KC)
                pe.wait_ge(sem("h_new1"), 4 + c + 1)
                for a in range(3):
                    rows = P if a < 2 else B
                    ins = nc.tensor.transpose(XB[c % 4][0:rows, tileT(a)], hs[:, c, a * P:a * P + rows], ident)
                ins.then_inc(sem("y_made"), 1)


_OUTS = [("y_prompt", (1, S, D)), ("y_sample", (B, 1, D)),
         ("new_a_kv_prompt", (1, 1, 2, S, AH, P)), ("new_a_kv_sample", (B, 1, 2, 1, AH, P)),
         ("state_b_v_prompt", (1, 1, P, D // 2)), ("state_b_v_sample", (B, 1, 1, D // 2)),
         ("new_c_cmp_kv_prompt", (1, 1, 2, S, CH, P)), ("new_c_cmp_kv_sample", (B, 1, 2, 1, CH, P)),
         ("new_c_sel_kv_prompt", (1, 1, 2, S, CH, P)), ("new_c_sel_kv_sample", (B, 1, 2, 1, CH, P)),
         ("new_c_win_kv_prompt", (1, 1, 2, S, CH, P)), ("new_c_win_kv_sample", (B, 1, 2, 1, CH, P))]


def kernel(**inputs):
    import numpy as _np
    import concourse.bacc as _bacc
    from concourse import mybir as _mybir
    from concourse.bass_utils import run_bass_kernel_spmd as _run

    nc = _bacc.Bacc("TRN2", target_bir_lowering=False, num_devices=1)
    arrays, dram = {}, {}
    const, mask_a, mask_c = shape_constants()
    given = dict(inputs, const=const, mask_a=mask_a, mask_c=mask_c)
    for name, a in given.items():
        a = _np.ascontiguousarray(a)
        arrays[f"in_{name}_dram"] = a
        dram[name] = nc.dram_tensor(f"in_{name}_dram", a.shape, _mybir.dt.from_np(a.dtype), kind="ExternalInput").ap()
    for name, shape in _OUTS:
        dram[name] = nc.dram_tensor(f"out_{name}_dram", shape, _mybir.dt.float32, kind="ExternalOutput").ap()
    dram["resid"] = nc.dram_tensor("resid_dram", (P, KC * T), _mybir.dt.float32, kind="Internal").ap()
    hybrid_trunk(nc, dram)
    r = _run(nc, [arrays], core_ids=[0])
    return tuple(r.results[0][f"out_{name}_dram"] for name, _ in _OUTS)
```
